# Optimizing a Trainium2 kernel written in Bass

```python
import jax, jax.numpy as jnp
from jax import lax
import numpy as np

D_MODEL = 1024
BATCH = 1
SEQ = 256
DEPTH = 2

GLA_HEADS = 4
GLA_DK = 128
GLA_DV = 128
GLA_LOWRANK = 16
GLA_GATE_NORM = 16.0
GLA_CHUNK = 64
MOBA_HEADS = 8
MOBA_HD = 64
MOBA_BLOCK = 256
MOBA_TOPK = 3
MOBA_QCHUNK = 64
ROPE_THETA = 10000.0
MLSTM_HEADS = 4
MLSTM_DQK = 64
MLSTM_DV = 128
MLSTM_CHUNK = 64
MLSTM_CONV = 4
D_FF = 4 * D_MODEL
N_BRANCH = 3
EPS = 1e-6

GLA_K = GLA_HEADS * GLA_DK
GLA_V = GLA_HEADS * GLA_DV
MOBA_W = MOBA_HEADS * MOBA_HD
MLSTM_QK = MLSTM_HEADS * MLSTM_DQK
MLSTM_V = MLSTM_HEADS * MLSTM_DV
IN_SPLITS = (GLA_K, GLA_K, GLA_V, GLA_V, GLA_LOWRANK,
             MOBA_W, MOBA_W, MOBA_W,
             MLSTM_QK, MLSTM_QK, MLSTM_V, MLSTM_V, MLSTM_HEADS, MLSTM_HEADS,
             N_BRANCH * D_MODEL)
D_IN = sum(IN_SPLITS)


def rms_norm(x, g):
    xf = x.astype(jnp.float32)
    y = xf * lax.rsqrt(jnp.mean(xf * xf, axis=-1, keepdims=True) + EPS)
    return (y * g.astype(jnp.float32)).astype(x.dtype)

def split_heads(x, h):
    b, t, _ = x.shape
    return x.reshape(b, t, h, -1).transpose(0, 2, 1, 3)

def merge_heads(x):
    b, h, t, d = x.shape
    return x.transpose(0, 2, 1, 3).reshape(b, t, h * d)

def rope_tables(seq, dim):
    inv = 1.0 / (ROPE_THETA ** (jnp.arange(0, dim, 2, dtype=jnp.float32) / dim))
    ang = jnp.arange(seq, dtype=jnp.float32)[:, None] * inv[None, :]
    return jnp.cos(ang), jnp.sin(ang)

def apply_rope(x, cos, sin):
    x1, x2 = jnp.split(x, 2, axis=-1)
    return jnp.concatenate([x1 * cos - x2 * sin, x2 * cos + x1 * sin], axis=-1)

def causal_dwconv(x, w):
    wd, c = w.shape
    return lax.conv_general_dilated(x, w[:, None, :], window_strides=(1,), padding=((wd - 1, 0),),
                                    dimension_numbers=('NWC', 'WIO', 'NWC'), feature_group_count=c)

def gla_mixer(q, k, v, log_a):
    b, h, t, dk = q.shape
    dv = v.shape[-1]
    L = GLA_CHUNK
    n = t // L
    qc = (q * dk ** -0.5).reshape(b, h, n, L, dk)
    kc = k.reshape(b, h, n, L, dk)
    vc = v.reshape(b, h, n, L, dv)
    bcum = jnp.cumsum(log_a.reshape(b, h, n, L, dk), axis=3)
    b_last = bcum[:, :, :, -1:, :]
    q_dec = qc * jnp.exp(bcum)
    k_inv = kc * jnp.exp(-bcum)
    k_end = kc * jnp.exp(b_last - bcum)
    causal = jnp.tril(jnp.ones((L, L), dtype=bool))
    attn = jnp.where(causal, jnp.einsum('bhnid,bhnjd->bhnij', q_dec, k_inv), 0.0)
    o_intra = jnp.einsum('bhnij,bhnjv->bhniv', attn, vc)
    chunk_kv = jnp.einsum('bhnld,bhnlv->bhndv', k_end, vc)
    decay = jnp.exp(b_last[:, :, :, 0, :])

    def step(S, inp):
        dec, kv = inp
        return dec[..., None] * S + kv, S

    S0 = jnp.zeros((b, h, dk, dv), q.dtype)
    _, S_prev = lax.scan(step, S0, (jnp.moveaxis(decay, 2, 0), jnp.moveaxis(chunk_kv, 2, 0)))
    S_prev = jnp.moveaxis(S_prev, 0, 2)
    o_inter = jnp.einsum('bhnld,bhndv->bhnlv', q_dec, S_prev)
    return (o_intra + o_inter).reshape(b, h, t, dv)

def moba_mixer(q, k, v):
    b, h, t, d = q.shape
    t_pad = -(-t // MOBA_BLOCK) * MOBA_BLOCK
    pad = ((0, 0), (0, 0), (0, t_pad - t), (0, 0))
    q, k, v = jnp.pad(q, pad), jnp.pad(k, pad), jnp.pad(v, pad)
    nb = t_pad // MOBA_BLOCK
    k_sel = min(MOBA_TOPK, nb)
    scale = d ** -0.5
    k_blocks = k.reshape(b, h, nb, MOBA_BLOCK, d)
    v_blocks = v.reshape(b, h, nb, MOBA_BLOCK, d)
    k_mean = jnp.mean(k_blocks, axis=3)
    pos = jnp.arange(t_pad)
    past = jnp.arange(nb)[None, :] < (pos // MOBA_BLOCK)[:, None]
    gate = jnp.einsum('bhtd,bhnd->bhtn', q, k_mean)
    gate = jnp.where(past, gate, -jnp.inf)
    top_val, top_idx = lax.top_k(gate, k_sel)
    valid = jnp.isfinite(top_val)
    bi = jnp.arange(b)[:, None, None, None]
    hi = jnp.arange(h)[None, :, None, None]
    qn = MOBA_QCHUNK

    def chunk_fn(c):
        start = c * qn
        qc = lax.dynamic_slice_in_dim(q, start, qn, axis=2)
        idx = lax.dynamic_slice_in_dim(top_idx, start, qn, axis=2)
        ok = lax.dynamic_slice_in_dim(valid, start, qn, axis=2)
        kg = k_blocks[bi, hi, idx]
        vg = v_blocks[bi, hi, idx]
        s_sel = jnp.einsum('bhqd,bhqskd->bhqsk', qc, kg) * scale
        s_sel = jnp.where(ok[..., None], s_sel, -jnp.inf).reshape(b, h, qn, k_sel * MOBA_BLOCK)
        own_start = (start // MOBA_BLOCK) * MOBA_BLOCK
        ko = lax.dynamic_slice_in_dim(k, own_start, MOBA_BLOCK, axis=2)
        vo = lax.dynamic_slice_in_dim(v, own_start, MOBA_BLOCK, axis=2)
        s_own = jnp.einsum('bhqd,bhkd->bhqk', qc, ko) * scale
        qpos = start + jnp.arange(qn)
        kpos = own_start + jnp.arange(MOBA_BLOCK)
        s_own = jnp.where(kpos[None, :] <= qpos[:, None], s_own, -jnp.inf)
        p = jax.nn.softmax(jnp.concatenate([s_sel, s_own], axis=-1).astype(jnp.float32), axis=-1)
        p_sel = p[..., :k_sel * MOBA_BLOCK].reshape(b, h, qn, k_sel, MOBA_BLOCK)
        p_own = p[..., k_sel * MOBA_BLOCK:]
        return (jnp.einsum('bhqsk,bhqskd->bhqd', p_sel, vg)
                + jnp.einsum('bhqk,bhkd->bhqd', p_own, vo))

    outs = lax.map(chunk_fn, jnp.arange(t_pad // qn))
    out = outs.transpose(1, 2, 0, 3, 4).reshape(b, h, t_pad, d)
    return out[:, :, :t]

def mlstm_mixer(q, k, v, log_i, log_f):
    b, h, t, dk = q.shape
    dv = v.shape[-1]
    L = MLSTM_CHUNK
    n = t // L
    qc = q.reshape(b, h, n, L, dk)
    kc = (k * dk ** -0.5).reshape(b, h, n, L, dk)
    vc = v.reshape(b, h, n, L, dv)
    li = log_i.reshape(b, h, n, L)
    bcum = jnp.cumsum(log_f.reshape(b, h, n, L), axis=-1)
    b_last = bcum[..., -1]
    causal = jnp.tril(jnp.ones((L, L), dtype=bool))
    logD = jnp.where(causal, bcum[..., :, None] - bcum[..., None, :] + li[..., None, :], -jnp.inf)
    log_end = b_last[..., None] - bcum + li
    m_local = jnp.max(log_end, axis=-1)
    w_loc = jnp.exp(log_end - m_local[..., None])
    chunk_kv = jnp.einsum('bhnl,bhnld,bhnlv->bhndv', w_loc, kc, vc)
    chunk_k = jnp.einsum('bhnl,bhnld->bhnd', w_loc, kc)

    def step(carry, inp):
        S, nv, m = carry
        bl, ml, ckv, ck = inp
        m_new = jnp.maximum(bl + m, ml)
        a = jnp.exp(bl + m - m_new)
        c = jnp.exp(ml - m_new)
        S_new = a[..., None, None] * S + c[..., None, None] * ckv
        n_new = a[..., None] * nv + c[..., None] * ck
        return (S_new, n_new, m_new), (S, nv, m)

    init = (jnp.zeros((b, h, dk, dv), q.dtype), jnp.zeros((b, h, dk), q.dtype), jnp.zeros((b, h), q.dtype))
    xs = (jnp.moveaxis(b_last, 2, 0), jnp.moveaxis(m_local, 2, 0),
          jnp.moveaxis(chunk_kv, 2, 0), jnp.moveaxis(chunk_k, 2, 0))
    _, (S_prev, n_prev, m_prev) = lax.scan(step, init, xs)
    S_prev = jnp.moveaxis(S_prev, 0, 2)
    n_prev = jnp.moveaxis(n_prev, 0, 2)
    m_prev = jnp.moveaxis(m_prev, 0, 2)
    m_inter = bcum + m_prev[..., None]
    m_row = jnp.maximum(m_inter, jnp.max(logD, axis=-1))
    s = jnp.einsum('bhnid,bhnjd->bhnij', qc, kc) * jnp.exp(logD - m_row[..., None])
    inter_w = jnp.exp(m_inter - m_row)
    num = (jnp.einsum('bhnij,bhnjv->bhniv', s, vc)
           + inter_w[..., None] * jnp.einsum('bhnid,bhndv->bhniv', qc, S_prev))
    den = jnp.sum(s, axis=-1) + inter_w * jnp.einsum('bhnid,bhnd->bhni', qc, n_prev)
    hid = num / jnp.maximum(jnp.abs(den), jnp.exp(-m_row))[..., None]
    return hid.reshape(b, h, t, dv)

def hybrid_layer(x, cos, sin, norm1_g, w_in, gla_a_up, gla_a_b, gla_norm_g, moba_qn_g, moba_kn_g,
                 mlstm_conv_w, mlstm_i_b, mlstm_f_b, mlstm_norm_g, gate_b, w_br_gla, w_br_moba,
                 w_br_mlstm, w_out, norm2_g, w_ff1, w_ff2):
    dt = x.dtype
    f32 = jnp.float32
    bsz, t, _ = x.shape
    hn = rms_norm(x, norm1_g)
    proj = hn @ w_in
    offsets = np.cumsum(IN_SPLITS)[:-1].tolist()
    (g_q, g_k, g_v, g_g, g_a, m_q, m_k, m_v,
     l_q, l_k, l_v, l_o, l_i, l_f, br_gate) = jnp.split(proj, offsets, axis=-1)

    log_a = jax.nn.log_sigmoid((g_a @ gla_a_up + gla_a_b).astype(f32)) / GLA_GATE_NORM
    o_gla = gla_mixer(split_heads(g_q.astype(f32), GLA_HEADS), split_heads(g_k.astype(f32), GLA_HEADS),
                      split_heads(g_v.astype(f32), GLA_HEADS), split_heads(log_a, GLA_HEADS))
    o_gla = rms_norm(o_gla, gla_norm_g)
    y_gla = (merge_heads(o_gla) * jax.nn.silu(g_g.astype(f32))).astype(dt)

    mq = apply_rope(rms_norm(split_heads(m_q.astype(f32), MOBA_HEADS), moba_qn_g), cos, sin)
    mk = apply_rope(rms_norm(split_heads(m_k.astype(f32), MOBA_HEADS), moba_kn_g), cos, sin)
    mv = split_heads(m_v.astype(f32), MOBA_HEADS)
    y_moba = merge_heads(moba_mixer(mq, mk, mv)).astype(dt)

    qk = causal_dwconv(jnp.concatenate([l_q, l_k], axis=-1).astype(f32), mlstm_conv_w.astype(f32))
    lq, lk = jnp.split(qk, 2, axis=-1)
    log_i = (l_i + mlstm_i_b).astype(f32).transpose(0, 2, 1)
    log_f = jax.nn.log_sigmoid((l_f + mlstm_f_b).astype(f32)).transpose(0, 2, 1)
    h_ml = mlstm_mixer(split_heads(lq, MLSTM_HEADS), split_heads(lk, MLSTM_HEADS),
                       split_heads(l_v.astype(f32), MLSTM_HEADS), log_i, log_f)
    h_ml = rms_norm(h_ml, mlstm_norm_g)
    y_mlstm = (merge_heads(h_ml) * jax.nn.sigmoid(l_o.astype(f32))).astype(dt)

    gates = jax.nn.sigmoid(br_gate + gate_b).reshape(bsz, t, N_BRANCH, D_MODEL)
    mixed = (gates[:, :, 0] * (y_gla @ w_br_gla)
             + gates[:, :, 1] * (y_moba @ w_br_moba)
             + gates[:, :, 2] * (y_mlstm @ w_br_mlstm))
    x = x + mixed @ w_out

    h2 = rms_norm(x, norm2_g)
    x = x + jnp.square(jax.nn.relu(h2 @ w_ff1)) @ w_ff2
    return x

def first_inputs(seed: int = 0) -> dict:
    key = jax.random.key(seed)
    ks = jax.random.split(key, 24)

    def nrm(k, shape, fan_in):
        return jax.random.normal(k, shape, jnp.float32) * (fan_in ** -0.5)

    def gain(k, shape):
        return 1.0 + 0.02 * jax.random.normal(k, shape, jnp.float32)

    f_bias = (jnp.linspace(3.0, 6.0, MLSTM_HEADS, dtype=jnp.float32)[None, :]
              + 0.1 * jax.random.normal(ks[10], (DEPTH, MLSTM_HEADS), jnp.float32))
    return {
        "x": jax.random.normal(ks[0], (BATCH, SEQ, D_MODEL), jnp.float32),
        "norm1_g": gain(ks[1], (DEPTH, D_MODEL)),
        "w_in": nrm(ks[2], (DEPTH, D_MODEL, D_IN), D_MODEL),
        "gla_a_up": nrm(ks[3], (DEPTH, GLA_LOWRANK, GLA_K), GLA_LOWRANK),
        "gla_a_b": 0.02 * jax.random.normal(ks[4], (DEPTH, GLA_K), jnp.float32),
        "gla_norm_g": gain(ks[5], (DEPTH, GLA_DV)),
        "moba_qn_g": gain(ks[6], (DEPTH, MOBA_HD)),
        "moba_kn_g": gain(ks[7], (DEPTH, MOBA_HD)),
        "mlstm_conv_w": nrm(ks[8], (DEPTH, MLSTM_CONV, 2 * MLSTM_QK), MLSTM_CONV),
        "mlstm_i_b": 0.1 * jax.random.normal(ks[9], (DEPTH, MLSTM_HEADS), jnp.float32),
        "mlstm_f_b": f_bias,
        "mlstm_norm_g": gain(ks[11], (DEPTH, MLSTM_DV)),
        "gate_b": 0.02 * jax.random.normal(ks[12], (DEPTH, N_BRANCH * D_MODEL), jnp.float32),
        "w_br_gla": nrm(ks[13], (DEPTH, GLA_V, D_MODEL), GLA_V),
        "w_br_moba": nrm(ks[14], (DEPTH, MOBA_W, D_MODEL), MOBA_W),
        "w_br_mlstm": nrm(ks[15], (DEPTH, MLSTM_V, D_MODEL), MLSTM_V),
        "w_out": nrm(ks[16], (DEPTH, D_MODEL, D_MODEL), D_MODEL),
        "norm2_g": gain(ks[17], (DEPTH, D_MODEL)),
        "w_ff1": nrm(ks[18], (DEPTH, D_MODEL, D_FF), D_MODEL),
        "w_ff2": nrm(ks[19], (DEPTH, D_FF, D_MODEL), D_FF),
    }

def first_block(x, norm1_g, w_in, gla_a_up, gla_a_b, gla_norm_g, moba_qn_g, moba_kn_g, mlstm_conv_w,
              mlstm_i_b, mlstm_f_b, mlstm_norm_g, gate_b, w_br_gla, w_br_moba, w_br_mlstm, w_out,
              norm2_g, w_ff1, w_ff2):
    cos, sin = rope_tables(x.shape[1], MOBA_HD)
    for l in range(DEPTH):
        x = hybrid_layer(x, cos, sin, norm1_g[l], w_in[l], gla_a_up[l], gla_a_b[l], gla_norm_g[l],
                         moba_qn_g[l], moba_kn_g[l], mlstm_conv_w[l], mlstm_i_b[l], mlstm_f_b[l],
                         mlstm_norm_g[l], gate_b[l], w_br_gla[l], w_br_moba[l], w_br_mlstm[l], w_out[l],
                         norm2_g[l], w_ff1[l], w_ff2[l])
    return x


MIX_WIDTH = D_MODEL
CONV_WIDTH = MIX_WIDTH // 2
CONV_GROUPS = 4
CONV_WIN = 31
DN_WIDTH = MIX_WIDTH - CONV_WIDTH
DN_HEADS = 4
DN_HEAD_DIM = DN_WIDTH // DN_HEADS
SHORT_CONV = 4
CHUNK = 64
D_FF_DENSE = 2816
N_EXPERTS = 8
TOP_K = 2
D_FF_EXPERT = 3584
N_DENSE = (DEPTH + 1) // 2
N_MOE = DEPTH // 2
DEEPNORM_ALPHA = (2 * DEPTH) ** 0.25
DEEPNORM_BETA = (8 * DEPTH) ** -0.25
LN_EPS = 1e-5
RMS_EPS = 1e-6
L2_EPS = 1e-6
IN_SIZES = (CONV_WIDTH, CONV_WIDTH, DN_WIDTH, DN_WIDTH, DN_WIDTH, DN_WIDTH, DN_HEADS, DN_HEADS)
IN_COLS = sum(IN_SIZES)
IN_SPLITS_2 = tuple(int(s) for s in np.cumsum(IN_SIZES)[:-1])


def layer_norm(x, g, b):
    xf = x.astype(jnp.float32)
    mu = xf.mean(-1, keepdims=True)
    var = jnp.square(xf - mu).mean(-1, keepdims=True)
    return ((xf - mu) * lax.rsqrt(var + LN_EPS) * g + b).astype(x.dtype)

def causal_depthwise_conv(x, w):
    width = w.shape[0]
    return lax.conv_general_dilated(
        x, w[:, None, :].astype(x.dtype), (1,), ((width - 1, 0),),
        dimension_numbers=("NWC", "WIO", "NWC"), feature_group_count=x.shape[-1])

def conformer_conv(h_val, h_gate, dw_w, dw_b, ln_g, ln_b):
    h = h_val * jax.nn.sigmoid(h_gate)
    h = causal_depthwise_conv(h, dw_w) + dw_b
    h = layer_norm(h, ln_g, ln_b)
    return jax.nn.silu(h)

def l2norm(t):
    return t * lax.rsqrt(jnp.sum(t * t, -1, keepdims=True) + L2_EPS)

def chunk_gated_delta_rule(q, k, v, g, beta):
    B, S, H, Dk = q.shape
    Dv = v.shape[-1]
    N = S // CHUNK
    q = q * (Dk ** -0.5)
    to_chunks = lambda t: t.reshape(B, N, CHUNK, H, t.shape[-1]).transpose(0, 3, 1, 2, 4)
    q, k, v = to_chunks(q), to_chunks(k), to_chunks(v)
    g = g.reshape(B, N, CHUNK, H).transpose(0, 3, 1, 2)
    beta = beta.reshape(B, N, CHUNK, H).transpose(0, 3, 1, 2)
    g = jnp.cumsum(g, axis=-1)
    kb = k * beta[..., None]
    vb = v * beta[..., None]
    causal = jnp.tril(jnp.ones((CHUNK, CHUNK), bool))
    strict = jnp.tril(jnp.ones((CHUNK, CHUNK), bool), -1)
    decay = jnp.exp(jnp.where(causal, g[..., :, None] - g[..., None, :], -jnp.inf))
    lower = jnp.where(strict, jnp.einsum('bhncd,bhnjd->bhncj', kb, k) * decay, 0.0)
    eye = jnp.eye(CHUNK, dtype=jnp.float32)
    rhs = jnp.concatenate([vb, kb * jnp.exp(g)[..., None]], axis=-1)
    sol = lax.linalg.triangular_solve(eye + lower, rhs, left_side=True, lower=True, unit_diagonal=True)
    u, w = sol[..., :Dv], sol[..., Dv:]
    attn = jnp.einsum('bhncd,bhnjd->bhncj', q, k) * decay

    def step(state, inp):
        qc, kc, uc, wc, gc, ac = inp
        v_new = uc - jnp.einsum('bhcd,bhde->bhce', wc, state)
        o = jnp.einsum('bhcd,bhde->bhce', qc * jnp.exp(gc)[..., None], state) \
            + jnp.einsum('bhcj,bhje->bhce', ac, v_new)
        g_last = gc[..., -1]
        k_dec = kc * jnp.exp(g_last[..., None] - gc)[..., None]
        state = state * jnp.exp(g_last)[..., None, None] + jnp.einsum('bhcd,bhce->bhde', k_dec, v_new)
        return state, o

    lead = lambda t: jnp.moveaxis(t, 2, 0)
    s0 = jnp.zeros((B, H, Dk, Dv), jnp.float32)
    _, o = lax.scan(step, s0, (lead(q), lead(k), lead(u), lead(w), lead(g), lead(attn)))
    o = jnp.moveaxis(o, 0, 2)
    return o.transpose(0, 2, 3, 1, 4).reshape(B, S, H, Dv)

def gated_deltanet(q, k, v, z, b_logit, a_logit, sc_w, a_log, dt_bias, on_g):
    B, S, _ = q.shape
    qkv = jax.nn.silu(causal_depthwise_conv(jnp.concatenate([q, k, v], -1), sc_w))
    q, k, v = jnp.split(qkv, 3, axis=-1)
    heads = lambda t: t.reshape(B, S, DN_HEADS, DN_HEAD_DIM).astype(jnp.float32)
    q, k, v = l2norm(heads(q)), l2norm(heads(k)), heads(v)
    beta = jax.nn.sigmoid(b_logit.astype(jnp.float32))
    g = -jnp.exp(a_log.astype(jnp.float32)) * jax.nn.softplus(
        a_logit.astype(jnp.float32) + dt_bias.astype(jnp.float32))
    o = chunk_gated_delta_rule(q, k, v, g, beta)
    o = o * lax.rsqrt(jnp.mean(o * o, -1, keepdims=True) + RMS_EPS) * on_g.astype(jnp.float32)
    o = o * jax.nn.silu(heads(z))
    return o.reshape(B, S, DN_WIDTH).astype(z.dtype)

def hybrid_mixer(x, w_in, dw_w, dw_b, cln_g, cln_b, sc_w, a_log, dt_bias, on_g, w_out):
    h = x @ w_in
    c_val, c_gate, q, k, v, z, b_logit, a_logit = jnp.split(h, IN_SPLITS_2, axis=-1)
    y_conv = conformer_conv(c_val, c_gate, dw_w, dw_b, cln_g, cln_b)
    y_dn = gated_deltanet(q, k, v, z, b_logit, a_logit, sc_w, a_log, dt_bias, on_g)
    return jnp.concatenate([y_conv, y_dn], axis=-1) @ w_out

def swiglu(x, w_gate, w_up, w_down):
    return (jax.nn.silu(x @ w_gate) * (x @ w_up)) @ w_down

def moe_swiglu(x, router_w, w_gate, w_up, w_down):
    logits = (x @ router_w).astype(jnp.float32)
    top_v, top_i = lax.top_k(logits, TOP_K)
    gates = jax.nn.softmax(top_v, axis=-1)
    combine = jnp.sum(jax.nn.one_hot(top_i, N_EXPERTS, dtype=jnp.float32) * gates[..., None], axis=-2)
    y = jnp.zeros_like(x)
    for e in range(N_EXPERTS):
        y = y + combine[..., e:e + 1].astype(x.dtype) * swiglu(x, w_gate[e], w_up[e], w_down[e])
    return y

def second_inputs(seed: int = 0) -> dict:
    key = jax.random.key(seed)
    ks = jax.random.split(key, 24)
    f32 = jnp.float32
    nrm = lambda k, shape, scale: jax.random.normal(k, shape, f32) * scale
    dt = jnp.exp(jax.random.uniform(ks[8], (DEPTH, DN_HEADS), f32, np.log(1e-3), np.log(1e-1)))
    return {
        "x": nrm(ks[0], (BATCH, SEQ, D_MODEL), 1.0),
        "w_in": nrm(ks[1], (DEPTH, D_MODEL, IN_COLS), D_MODEL ** -0.5),
        "conv_dw_w": nrm(ks[2], (DEPTH, CONV_WIN, CONV_WIDTH), CONV_WIN ** -0.5),
        "conv_dw_b": nrm(ks[3], (DEPTH, CONV_WIDTH), 0.02),
        "conv_ln_g": 1.0 + nrm(ks[4], (DEPTH, CONV_WIDTH), 0.02),
        "conv_ln_b": nrm(ks[5], (DEPTH, CONV_WIDTH), 0.02),
        "short_conv_w": nrm(ks[6], (DEPTH, SHORT_CONV, 3 * DN_WIDTH), SHORT_CONV ** -0.5),
        "a_log": jnp.log(jax.random.uniform(ks[7], (DEPTH, DN_HEADS), f32, 1.0, 16.0)),
        "dt_bias": dt + jnp.log(-jnp.expm1(-dt)),
        "out_norm_g": 1.0 + nrm(ks[9], (DEPTH, DN_HEAD_DIM), 0.02),
        "w_out": nrm(ks[10], (DEPTH, MIX_WIDTH, D_MODEL), MIX_WIDTH ** -0.5 * DEEPNORM_BETA),
        "ln_mix_g": 1.0 + nrm(ks[11], (DEPTH, D_MODEL), 0.02),
        "ln_mix_b": nrm(ks[12], (DEPTH, D_MODEL), 0.02),
        "ffn_w_gate": nrm(ks[13], (N_DENSE, D_MODEL, D_FF_DENSE), D_MODEL ** -0.5),
        "ffn_w_up": nrm(ks[14], (N_DENSE, D_MODEL, D_FF_DENSE), D_MODEL ** -0.5),
        "ffn_w_down": nrm(ks[15], (N_DENSE, D_FF_DENSE, D_MODEL), D_FF_DENSE ** -0.5 * DEEPNORM_BETA),
        "router_w": nrm(ks[16], (N_MOE, D_MODEL, N_EXPERTS), D_MODEL ** -0.5),
        "moe_w_gate": nrm(ks[17], (N_MOE, N_EXPERTS, D_MODEL, D_FF_EXPERT), D_MODEL ** -0.5),
        "moe_w_up": nrm(ks[18], (N_MOE, N_EXPERTS, D_MODEL, D_FF_EXPERT), D_MODEL ** -0.5),
        "moe_w_down": nrm(ks[19], (N_MOE, N_EXPERTS, D_FF_EXPERT, D_MODEL), D_FF_EXPERT ** -0.5 * DEEPNORM_BETA),
        "ln_ffn_g": 1.0 + nrm(ks[20], (DEPTH, D_MODEL), 0.02),
        "ln_ffn_b": nrm(ks[21], (DEPTH, D_MODEL), 0.02),
    }

def second_block(x, w_in, conv_dw_w, conv_dw_b, conv_ln_g, conv_ln_b, short_conv_w, a_log, dt_bias,
              out_norm_g, w_out, ln_mix_g, ln_mix_b, ffn_w_gate, ffn_w_up, ffn_w_down, router_w,
              moe_w_gate, moe_w_up, moe_w_down, ln_ffn_g, ln_ffn_b):
    for layer in range(DEPTH):
        m = hybrid_mixer(x, w_in[layer], conv_dw_w[layer], conv_dw_b[layer], conv_ln_g[layer],
                         conv_ln_b[layer], short_conv_w[layer], a_log[layer], dt_bias[layer],
                         out_norm_g[layer], w_out[layer])
        x = layer_norm(DEEPNORM_ALPHA * x + m, ln_mix_g[layer], ln_mix_b[layer])
        j = layer // 2
        if layer % 2 == 0:
            f = swiglu(x, ffn_w_gate[j], ffn_w_up[j], ffn_w_down[j])
        else:
            f = moe_swiglu(x, router_w[j], moe_w_gate[j], moe_w_up[j], moe_w_down[j])
        x = layer_norm(DEEPNORM_ALPHA * x + f, ln_ffn_g[layer], ln_ffn_b[layer])
    return x


def setup_inputs(seed=0):
    out = dict(first_inputs(seed))
    for name, value in second_inputs(seed + 1).items():
        if name != "x":
            out[name + "_2"] = value
    return out


def reference(
    x, norm1_g, w_in, gla_a_up, gla_a_b, gla_norm_g, moba_qn_g, moba_kn_g, mlstm_conv_w,
    mlstm_i_b, mlstm_f_b, mlstm_norm_g, gate_b, w_br_gla, w_br_moba, w_br_mlstm, w_out, norm2_g,
    w_ff1, w_ff2, w_in_2, conv_dw_w_2, conv_dw_b_2, conv_ln_g_2, conv_ln_b_2, short_conv_w_2,
    a_log_2, dt_bias_2, out_norm_g_2, w_out_2, ln_mix_g_2, ln_mix_b_2, ffn_w_gate_2, ffn_w_up_2,
    ffn_w_down_2, router_w_2, moe_w_gate_2, moe_w_up_2, moe_w_down_2, ln_ffn_g_2, ln_ffn_b_2,
):
    x = first_block(
        x, norm1_g, w_in, gla_a_up, gla_a_b, gla_norm_g, moba_qn_g, moba_kn_g, mlstm_conv_w,
        mlstm_i_b, mlstm_f_b, mlstm_norm_g, gate_b, w_br_gla, w_br_moba, w_br_mlstm, w_out,
        norm2_g, w_ff1, w_ff2,
    )
    return second_block(
        x, w_in_2, conv_dw_w_2, conv_dw_b_2, conv_ln_g_2, conv_ln_b_2, short_conv_w_2, a_log_2,
        dt_bias_2, out_norm_g_2, w_out_2, ln_mix_g_2, ln_mix_b_2, ffn_w_gate_2, ffn_w_up_2,
        ffn_w_down_2, router_w_2, moe_w_gate_2, moe_w_up_2, moe_w_down_2, ln_ffn_g_2,
        ln_ffn_b_2,
    )


_drawn_inputs = setup_inputs


def setup_inputs(seed=0):
    import zlib

    import numpy as np

    out = dict(_drawn_inputs(seed))
    spreads = {}
    factors = {'gla_a_b': 5.412,
     'gla_norm_g': 4.364,
     'moba_qn_g': 8.0,
     'moba_kn_g': 8.0,
     'mlstm_i_b': 8.0,
     'mlstm_norm_g': 4.551,
     'gate_b': 5.23,
     'conv_dw_b_2': 4.65,
     'conv_ln_g_2': 7.84,
     'conv_ln_b_2': 8.0,
     'a_log_2': 2.718,
     'out_norm_g_2': 8.0}
    for name, (base, spread) in spreads.items():
        noise = np.random.default_rng([zlib.crc32(name.encode()), seed]).standard_normal(out[name].shape)
        drawn = base * np.exp(spread * noise) if base else spread * noise
        out[name] = __import__('jax').numpy.asarray(drawn.astype(out[name].dtype))
    for name, factor in factors.items():
        out[name] = (out[name] * factor).astype(out[name].dtype)
    return out
```

```python
from contextlib import ExitStack

import concourse.bass as bass
from concourse import mybir

F32 = mybir.dt.float32
I32 = mybir.dt.int32
U32 = mybir.dt.uint32
ACT = mybir.ActivationFunctionType
ALU = mybir.AluOpType
AX = mybir.AxisListType

P = 128
T = 256
NT = T // P
D = 1024
KD = D // P
DEPTH = 2
CHUNK = 64
NCH = T // CHUNK
GLA_H = 4
LOWRANK = 16
GATE_NORM = 16.0
MOBA_H, HD = 8, 64
ML_H, ML_DK, ML_DV = 4, 64, 128
DFF1 = 4 * D
DFF_DENSE = 2816
NEXP = 8
DFF_EXP = 3584
CONV_WIN = 31
EPS = 1e-6
LN_EPS = 1e-5
ALPHA = (2 * DEPTH) ** 0.25
NEG = -1e30

SLOT = 2048
NSLOT = 6
UNIT = 256
PROJ1 = 32
SLOTS_L1 = PROJ1 + 6 + 4 + 2 * (DFF1 // UNIT)
SLOTS_MIX2 = 12 + 4
UNITS_DENSE = DFF_DENSE // UNIT
UNITS_EXP = DFF_EXP // UNIT
SLOTS_DENSE = 3 * UNITS_DENSE
SLOTS_EXP = 3 * UNITS_EXP

RUN_FIRST = True
RUN_SECOND = True


def columns(spec):
    at, out = 0, {}
    for name, n in spec:
        out[name] = (at, at + n)
        at += n
    return out, at


PAR1, NP1 = columns([("n1", 8), ("n2", 8), ("ab", 4), ("gn", 1), ("mn", 1), ("gateb", 24), ("convw", 16),
                     ("wga", KD * LOWRANK), ("wli", KD * 4), ("wlf", KD * 4), ("qng", HD), ("kng", HD),
                     ("aup", 512), ("ifb", 2)])
PAR2, NP2 = columns([("wb", KD * 4), ("wa", KD * 4), ("sconv", 48), ("dww", 4 * CONV_WIN), ("dwb", 4),
                     ("clng", 4), ("clnb", 4), ("ong", 1), ("gpar", 2), ("router", KD * NEXP),
                     ("lnmg", D), ("lnmb", D), ("lnfg", D), ("lnfb", D)])
CON, NC = columns([("ident", P), ("ones", P), ("keep", P), ("neg", P), ("moba", 384), ("m8", P),
                   ("off", 3 * P), ("sel", 512), ("selp", 256), ("cos", 64), ("sin", 64), ("iota", 8)])


class Steps:

    def __init__(self, known):
        self.n, self.names, self.known = 0, {}, known

    def step(self, name=None):
        self.n += 1
        if name is not None:
            assert name not in self.names, name
            self.names[name] = self.n
        return 1

    def at(self, name):
        return self.known.get(name, 1)

    def segment(self):
        self.n = 0


def build(nc, x_d, stream, par1_d, par2_d, con_d, out, known):
    ctx = ExitStack()
    with ctx:
        def sb(name, shape, dt=F32):
            return ctx.enter_context(nc.sbuf_tensor(name, shape, dt))

        def sem(name):
            return ctx.enter_context(nc.semaphore(name))

        ring = sb("ring", [P, NSLOT, SLOT])
        con = sb("con", [P, NC])
        par = sb("par", [P, max(NP1, NP2)])
        X = sb("X", [P, NT, D])
        xT = sb("xT", [P, KD, T])
        scr = sb("scr", [P, NT, D])
        big = sb("big", [P, 16896])
        eps_rms = sb("eps_rms", [P, 1])
        eps_ln = sb("eps_ln", [P, 1])
        reset = sb("reset", [P, 4 * T])
        small = sb("small", [P, 512])
        PS = [ctx.enter_context(nc.psum_tensor(f"bank{i}", [P, 512], F32)) for i in range(8)]

        slot_landed = [sem(f"slot_landed{i}") for i in range(NSLOT)]
        slots_used = sem("slots_used")
        pe_done = sem("pe_done")
        act_done = sem("act_done")
        vec_done = sem("vec_done")
        par_loaded = sem("par_loaded")
        con_loaded = sem("con_loaded")
        x_loaded = sem("x_loaded")
        out_stored = sem("out_stored")
        consts_ready = sem("consts_ready")
        pool_turns = sem("pool_turns")
        turns = sem("turns")
        arrived = sem("arrived")
        cleared = sem("cleared")
        block = ctx.enter_context(nc.Block())

        PE, AC, VE = (Steps(known.setdefault(k, {})) for k in ("pe", "act", "vec"))
        known["now"] = (PE, AC, VE)

        def c(name, rows=P):
            a, b = CON[name]
            return con[0:rows, a:b]

        def p1(name, rows=P):
            a, b = PAR1[name]
            return par[0:rows, a:b]

        def p2(name, rows=P):
            a, b = PAR2[name]
            return par[0:rows, a:b]

        ident = c("ident")

        def fm(at, blocks):
            return big[:, at:at + blocks * T].rearrange("p (b t) -> p b t", t=T)

        def tm(at, cols):
            return big[:, at:at + NT * cols].rearrange("p (t c) -> p t c", t=NT)

        segs = []
        if RUN_FIRST:
            segs.append(("l1", SLOTS_L1, DEPTH))
        if RUN_SECOND:
            segs += [("mixA", SLOTS_MIX2, 1), ("dense", SLOTS_DENSE, 1), ("mixB", SLOTS_MIX2, 1),
                     ("moe", SLOTS_EXP, NEXP), ("end", 0, 1)]
        else:
            segs += [("end", 0, 1)]
        first_slot, uses, seg_no = {}, {}, {}
        at, used, no = 0, [0] * NSLOT, 0
        for tag, n, loops in segs:
            first_slot[tag], uses[tag], seg_no[tag] = at, list(used), no
            per = [len(range(s, n, NSLOT)) for s in range(NSLOT)]
            used = [u + per[s] * loops for s, u in enumerate(used)]
            at += n * loops
            no += loops
        n_slots = dict((t, n) for t, n, _ in segs)
        total_slots = at

        class Ring:

            def __init__(self):
                self.k = 0

            def start(self, tag, it):
                self.tag, self.it, self.k = tag, it, 0

            def take(self, pe):
                s = self.k % NSLOT
                per = len(range(s, n_slots[self.tag], NSLOT))
                pe.wait_ge(slot_landed[s], self.it * (16 * per) + 16 * (uses[self.tag][s] + self.k // NSLOT + 1))
                self.k += 1
                return ring[:, s, :]

        rg = Ring()

        def for_segment(eng, tag, loops, body):
            def whole(it):
                body(it)
                if eng is not None and eng[0] != "pool":
                    e, steps, done = eng[1:]
                    if steps is not None and steps.n > 0:
                        e.wait_ge(done, steps.n)
                    if eng[0] == "pe":
                        e.wait_ge(slots_used, n_slots[tag])
                    e.sem_inc(arrived, 1)
                    e.wait_ge(cleared, it + (seg_no[tag] + 1))
                    e.sem_inc(turns, 1)
                    if steps is not None:
                        steps.segment()
            e = eng[1]
            if loops == 1:
                whole(0)
            else:
                with e.Fori(0, loops) as it:
                    whole(it)

        @block.gpsimd
        def _(pool):
            def body(tag):
                def f(it):
                    pool.wait_ge(arrived, it * 4 + 4 * (seg_no[tag] + 1))
                    pool.sem_inc(pool_turns, 1)
                    for s in (pe_done, act_done, vec_done, slots_used):
                        pool.sem_clear(s)
                    pool.sem_inc(cleared, 1)
                return f
            for tag, _, loops in segs[:-1]:
                for_segment(("pool", pool, None, None), tag, loops, body(tag))

        @block.sync
        def _(sp):
            sp.dma_start(X[:, :, :], x_d.rearrange("(t p) n -> p t n", p=P)).then_inc(x_loaded, 16)
            sp.dma_start(con[:, :], con_d).then_inc(con_loaded, 16)
            for k in range(NSLOT):
                sp.dma_start(ring[:, k, :], stream[k]).then_inc(slot_landed[k], 16)

            def body(tag):
                n = n_slots[tag]

                def f(it):
                    for k in range(NSLOT, n + NSLOT):
                        s = k % NSLOT if k < n else k - n
                        last = k - NSLOT if k < n else max(range(s, n, NSLOT))
                        sp.wait_ge(slots_used, last + 1)
                        if isinstance(it, int):
                            src = stream[first_slot[tag] + k]
                        else:
                            src = stream[bass.ds(it * n + (first_slot[tag] + k), 1)].rearrange("o p n -> p (o n)")
                        sp.dma_start(ring[:, s, :], src).then_inc(slot_landed[s], 16)
                return f
            for tag, _, loops in segs[:-1]:
                for_segment(("sp", sp, None, None), tag, loops, body(tag))
            for s in range(NSLOT):
                sp.wait_ge(slot_landed[s], 16 * (uses["end"][s] + 1))
            if RUN_SECOND:
                sp.wait_ge(vec_done, VE.at("final"))
            sp.dma_start(out.rearrange("(t p) n -> p t n", p=P), X[:, :, :]).then_inc(out_stored, 16)
            sp.wait_ge(out_stored, 16)

        def v_wait(v):
            v.wait_ge(vec_done, VE.n)

        def a_wait(act):
            act.wait_ge(act_done, AC.n)

        def v_rms(v, tag):
            ss = small[:, 0:NT]
            for t in range(NT):
                v.tensor_tensor(scr[:, t, :], X[:, t, :], X[:, t, :], ALU.mult).then_inc(vec_done, VE.step())
            v_wait(v)
            v.tensor_reduce(ss, scr[:, :, :], AX.X, ALU.add).then_inc(vec_done, VE.step(tag + ".ss"))
            act_sq = small[:, 2:2 + NT]
            v.wait_ge(act_done, AC.at(tag + ".root"))
            v.reciprocal(ss, act_sq).then_inc(vec_done, VE.step())
            v_wait(v)
            for t in range(NT):
                v.tensor_scalar(scr[:, t, :], X[:, t, :], ss[:, t:t + 1], None, ALU.mult)\
                 .then_inc(vec_done, VE.step(tag + f".hn{t}"))

        def a_rms(act, tag):
            act.wait_ge(vec_done, VE.at(tag + ".ss"))
            act.activation(small[:, 2:2 + NT], small[:, 0:NT], ACT.Sqrt, bias=eps_rms[:, 0:1], scale=1.0 / D)\
               .then_inc(act_done, AC.step(tag + ".root"))

        def t_transpose(pe, tag, src, waits):
            for w, n in waits:
                pe.wait_ge(w, n)
            for k in range(KD):
                for t in range(NT):
                    mm = pe.transpose(PS[k // 2][:, (k % 2) * T + t * P:(k % 2) * T + (t + 1) * P],
                                      src[:, t, k * P:(k + 1) * P], ident)
                if k % 2:
                    mm.then_inc(pe_done, PE.step(tag + f".tr{k // 2}"))

        def a_transposed(act, tag, gain):
            for j in (0, 2):
                act.wait_ge(pe_done, PE.at(tag + f".tr{j}"))
                for q in range(2):
                    k = 2 * j + q
                    act.activation(xT[:, k, :], PS[j][:, q * T:(q + 1) * T], ACT.Copy,
                                   scale=(1.0 if gain is None else gain[:, k:k + 1]))\
                       .then_inc(act_done, AC.step())
                    k = 2 * (j + 1) + q
            AC.names[tag + ".xT"] = AC.n

        def v_transposed(v, tag, gain):
            for j in (1, 3):
                v.wait_ge(pe_done, PE.at(tag + f".tr{j}"))
                for q in range(2):
                    k = 2 * j + q
                    if gain is None:
                        v.tensor_copy(xT[:, k, :], PS[j][:, q * T:(q + 1) * T]).then_inc(vec_done, VE.step())
                    else:
                        v.tensor_scalar(xT[:, k, :], PS[j][:, q * T:(q + 1) * T], gain[:, k:k + 1], None, ALU.mult)\
                         .then_inc(vec_done, VE.step())
            VE.names[tag + ".xT"] = VE.n

        def t_project(pe, tag, kinds):
            for n, kind in enumerate(kinds):
                w = rg.take(pe).rearrange("p (k n) -> p k n", n=UNIT)
                if n >= 4:
                    pe.wait_ge(*evac_of(tag, kinds, n - 4))
                elif n == 0:
                    pe.wait_ge(act_done, AC.at(tag + ".go"))
                    pe.wait_ge(vec_done, VE.at(tag + ".go"))
                bank = PS[4 + n % 4]
                for h in range(2):
                    for k in range(KD):
                        cols = slice(h * P, (h + 1) * P)
                        if kind == "fm":
                            mm = pe.matmul(bank[:, h * T:(h + 1) * T], w[:, k, cols], xT[:, k, :],
                                           start=(k == 0), stop=(k == KD - 1))
                        else:
                            mm = pe.matmul(bank[:, h * T:(h + 1) * T], xT[:, k, cols], w[:, k, :],
                                           start=(k == 0), stop=(k == KD - 1))
                mm.then_inc(slots_used, 1)

        def evac_of(tag, kinds, n):
            return (act_done, AC.at(tag + f".ev{n}")) if n % 2 == 0 else (vec_done, VE.at(tag + f".ev{n}"))

        def v_headnorm(v, tag, o, gain, gate, yT, t0):
            oh = o.rearrange("p t (h d) -> p (t h) d", d=P)
            sq = scr[:, :, :].rearrange("p t n -> p (t n)")[:, 0:1024].rearrange("p (g d) -> p g d", d=P)
            ss = small[:, 32:40]
            v.tensor_tensor(sq, oh, oh, ALU.mult).then_inc(vec_done, VE.step())
            v_wait(v)
            v.tensor_reduce(ss, sq, AX.X, ALU.add).then_inc(vec_done, VE.step(tag + ".hss"))
            v.wait_ge(act_done, AC.at(tag + ".hroot"))
            v.reciprocal(small[:, 48:56], small[:, 40:48]).then_inc(vec_done, VE.step())
            v_wait(v)
            v.tensor_tensor(oh, oh, small[:, 48:56].unsqueeze(2).to_broadcast([P, 8, P]), ALU.mult)\
             .then_inc(vec_done, VE.step(tag + ".hn"))
            yf = yT.rearrange("p b t -> p (b t)")
            gf = gate.rearrange("p b t -> p (b t)")
            for j in range(2):
                v.wait_ge(pe_done, PE.at(tag + f".htr{j}"))
                v.scalar_tensor_tensor(out=yf[:, j * 512:(j + 1) * 512], in0=PS[t0 + j][:, :], scalar=gain,
                                       in1=gf[:, j * 512:(j + 1) * 512], op0=ALU.mult, op1=ALU.mult)\
                 .then_inc(vec_done, VE.step(tag + f".y{j}"))

        def a_headnorm(act, tag):
            act.wait_ge(vec_done, VE.at(tag + ".hss"))
            act.activation(small[:, 40:48], small[:, 32:40], ACT.Sqrt, bias=eps_rms[:, 0:1], scale=1.0 / P)\
               .then_inc(act_done, AC.step(tag + ".hroot"))

        def t_headnorm(pe, tag, o, t0):
            pe.wait_ge(vec_done, VE.at(tag + ".hn"))
            for j in range(2):
                for q in range(2):
                    for t in range(NT):
                        h = 2 * j + q
                        mm = pe.transpose(PS[t0 + j][:, q * T + t * P:q * T + (t + 1) * P],
                                          o[:, t, h * P:(h + 1) * P], ident)
                mm.then_inc(pe_done, PE.step(tag + f".htr{j}"))

        def t_ffn(pe, tag, units, gated, down_start=True):
            ups = {}

            def up(u):
                b = 2 * (u % 2)
                if u >= 2:
                    pe.wait_ge(vec_done, VE.at(tag + f".h{u - 2}"))
                    if not gated:
                        pe.wait_ge(act_done, AC.at(tag + f".s{u - 2}"))
                for g in range(2 if gated else 1):
                    w = rg.take(pe).rearrange("p (k n) -> p k n", n=UNIT)
                    for h in range(2):
                        for k in range(KD):
                            mm = pe.matmul(PS[b + g][:, h * T:(h + 1) * T], w[:, k, h * P:(h + 1) * P],
                                           xT[:, k, :], start=(k == 0), stop=(k == KD - 1))
                    mm.then_inc(slots_used, 1)
                ups[u] = rg.k

            def down(u):
                w = rg.take(pe).rearrange("p (k n) -> p k n", n=D)
                pe.wait_ge(vec_done, VE.at(tag + f".h{u}"))
                for k in range(2):
                    for t in range(NT):
                        for f in range(2):
                            mm = pe.matmul(PS[4 + 2 * t + f][:, :], hid[u % 2][:, k, t * P:(t + 1) * P],
                                           w[:, k, f * 512:(f + 1) * 512], start=(u == 0 and k == 0),
                                           stop=(u == units - 1 and k == 1))
                mm.then_inc(slots_used, 1)

            pe.wait_ge(act_done, AC.at(tag + ".go"))
            pe.wait_ge(vec_done, VE.at(tag + ".go"))
            for u in range(units + 1):
                if u < units:
                    up(u)
                if u > 0:
                    down(u - 1)

        def slot_index(u, units, gated):
            n = 2 if gated else 1
            up = (u + 1) * n + max(u - 1, 0) if u < units else None
            dn = min(u + 2, units) * n + u + 1
            return up, dn

        hid = [scr[:, 1, 0:512].rearrange("p (b t) -> p b t", t=T),
               scr[:, 1, 512:1024].rearrange("p (b t) -> p b t", t=T)]
        hidf = [scr[:, 1, 0:512], scr[:, 1, 512:1024]]
        silf = [scr[:, 0, 0:512], scr[:, 0, 512:1024]]

        def a_ffn(act, tag, units, gated, base):
            for u in range(units):
                up, _ = slot_index(u, units, gated)
                act.wait_ge(slots_used, base + up)
                if u >= 2:
                    act.wait_ge(vec_done, VE.at(tag + f".h{u - 2}"))
                act.activation(silf[u % 2], PS[2 * (u % 2)][:, :], ACT.Silu if gated else ACT.Relu)\
                   .then_inc(act_done, AC.step(tag + f".s{u}"))

        def v_ffn(v, tag, units, gated, base):
            for u in range(units):
                v.wait_ge(act_done, AC.at(tag + f".s{u}"))
                if u >= 2:
                    v.wait_ge(slots_used, base + slot_index(u - 2, units, gated)[1])
                v.tensor_tensor(hidf[u % 2], silf[u % 2], PS[2 * (u % 2) + 1][:, :] if gated else silf[u % 2],
                                ALU.mult).then_inc(vec_done, VE.step(tag + f".h{u}"))

        def t_out(pe, tag, srcs):
            for s in range(4):
                w = rg.take(pe).rearrange("p (k n) -> p k n", n=D)
                for kk in range(2):
                    k = 2 * s + kk
                    for t in range(NT):
                        for f in range(2):
                            mm = pe.matmul(PS[4 + 2 * t + f][:, :], srcs(k)[:, t * P:(t + 1) * P],
                                           w[:, kk, f * 512:(f + 1) * 512], start=(k == 0), stop=(k == KD - 1))
                mm.then_inc(slots_used, 1)

        def v_residual(v, slots, alpha, name):
            v.wait_ge(slots_used, slots)
            for t in range(NT):
                for f in range(2):
                    cols = slice(f * 512, (f + 1) * 512)
                    v.scalar_tensor_tensor(out=X[:, t, cols], in0=X[:, t, cols], scalar=alpha,
                                           in1=PS[4 + 2 * t + f][:, :], op0=ALU.mult, op1=ALU.add)\
                     .then_inc(vec_done, VE.step())
            VE.names[name] = VE.n

        GQ, GK, GG, LO, LQK = 0, 1024, 2048, 3072, 4096
        GV, MQ, MK, MV, LV = 5136, 6160, 7184, 8208, 9232
        GATES = 10272
        W3 = T + 3
        gq, gk, gg, lo = fm(GQ, 4), fm(GK, 4), fm(GG, 4), fm(LO, 4)
        lqk = big[:, LQK:LQK + 4 * W3].rearrange("p (b t) -> p b t", t=W3)
        gv, mq, mk, mv = tm(GV, 512), tm(MQ, 512), tm(MK, 512), tm(MV, 512)
        lv = big[:, LV:LV + 2 * 4 * 129].rearrange("p (t h d) -> p t h d", t=NT, h=4)
        gates = fm(GATES, 24)
        KINDS1 = ["fm"] * 2 + ["fm"] * 2 + ["fm"] * 2 + ["tm"] * 2 + ["tm"] * 6 + ["fm"] * 2 + ["tm"] * 2 \
            + ["fm"] * 2 + ["fm"] * 12
        NAMES1 = ["gq", "gq", "gk", "gk", "gg", "gg", "gv", "gv", "mq", "mq", "mk", "mk", "mv", "mv",
                  "lqk", "lqk", "lv", "lv", "lo", "lo"] + ["gate"] * 12

        def evac_tile(n):
            name, h = NAMES1[n], n % 2
            if name in ("gq", "gk", "gg", "lo"):
                return {"gq": gq, "gk": gk, "gg": gg, "lo": lo}[name][:, 2 * h:2 * h + 2, :]
            if name == "lqk":
                return lqk[:, 2 * h:2 * h + 2, 3:W3]
            if name in ("gv", "mq", "mk", "mv"):
                return {"gv": gv, "mq": mq, "mk": mk, "mv": mv}[name][:, :, h * T:(h + 1) * T]
            if name == "lv":
                return lv[:, :, 2 * h:2 * h + 2, 0:128]

        def bank_view(n):
            b = PS[4 + n % 4][:, :]
            if NAMES1[n] == "lv":
                return b.rearrange("p (t h d) -> p t h d", t=2, h=2)
            return b.rearrange("p (a b) -> p a b", a=2)

        yg = fm(GQ, 4)
        ym = fm(MQ, 4)
        yl = fm(LQK, 4)
        BC = scr[:, 0, :]
        TMP = scr[:, 1, :]
        sg = sb("sg", [P, 3, 512])
        attn = sb("attn", [P, NT, 512])
        keT = sb("keT", [P, NT, 512])
        o_tm = sb("o_tm", [P, NT, 512])
        smb = sb("smb", [4, 2048])
        rows = [smb[:, i * T:(i + 1) * T] for i in range(8)]
        st = sb("st", [P, 3, 2, 129])
        keep_i = c("keep").bitcast(I32)
        PHASE = []

        def l1_tensor(pe, it):
            rg.start("l1", it)
            t_transpose(pe, "n1", scr, [(vec_done, VE.at("n1.hn1"))])
            pe.wait_ge(act_done, AC.at("n1.xT"))
            pe.wait_ge(vec_done, VE.at("n1.xT"))
            t_project(pe, "pj", KINDS1)
            w = p1("wga").rearrange("p (k n) -> p k n", n=LOWRANK)
            for k in range(KD):
                mm = pe.matmul(PS[0][0:LOWRANK, 0:T], w[:, k, :], xT[:, k, :], start=(k == 0), stop=(k == KD - 1))
            mm.then_inc(pe_done, PE.step("ga"))
            for n, name in enumerate(("wli", "wlf")):
                w = p1(name).rearrange("p (k n) -> p k n", n=4)
                for k in range(KD):
                    mm = pe.matmul(PS[1][0:4, n * T:(n + 1) * T], w[:, k, :], xT[:, k, :],
                                   start=(k == 0), stop=(k == KD - 1))
            mm.then_inc(pe_done, PE.step("lif"))
            pe.wait_ge(act_done, AC.at("gaT"))
            aup = p1("aup", LOWRANK)
            for h in range(4):
                mm = pe.matmul(PS[2 + h // 2][:, (h % 2) * T:(h % 2 + 1) * T], aup[:, h * P:(h + 1) * P],
                               small[0:LOWRANK, 256:512], start=True, stop=True)
            mm.then_inc(pe_done, PE.step("z"))
            pe.wait_ge(vec_done, VE.at("g.kend"))
            pe.wait_ge(act_done, AC.at("pj.ev30"))
            pe.wait_ge(vec_done, VE.at("pj.ev31"))
            for t in range(NT):
                for h in range(4):
                    mm = pe.matmul(PS[4 + t][:, h * P:(h + 1) * P], gk[:, h, t * P:(t + 1) * P],
                                   gq[:, h, t * P:(t + 1) * P], start=True, stop=True)
                mm.then_inc(pe_done, PE.step(f"g.s{t}"))
            for t in range(NT):
                for h in range(4):
                    mm = pe.transpose(PS[6 + t][:, h * P:(h + 1) * P],
                                      BC[:, h * T + t * P:h * T + (t + 1) * P], ident)
                mm.then_inc(pe_done, PE.step(f"g.ke{t}"))
            pe.wait_ge(act_done, AC.at("g.keT1"))
            for cc in range(3):
                t, r = cc // 2, slice(CHUNK * (cc % 2), CHUNK * (cc % 2) + CHUNK)
                for h in range(4):
                    mm = pe.matmul(PS[cc][:, h * P:(h + 1) * P], keT[r, t, h * P:(h + 1) * P],
                                   gv[r, t, h * P:(h + 1) * P], start=True, stop=True)
                mm.then_inc(pe_done, PE.step(f"g.kv{cc}"))
            pe.wait_ge(vec_done, VE.at("g.S"))
            for t in range(NT):
                for h in range(4):
                    pe.matmul(PS[6 + t][:, h * P:(h + 1) * P], attn[:, t, h * P:(h + 1) * P],
                              gv[:, t, h * P:(h + 1) * P], start=True, stop=False, skip_group_check=True)
                    for cc in (2 * t, 2 * t + 1):
                        if cc == 0:
                            continue
                        r = CHUNK * (cc % 2)
                        mm = pe.matmul(PS[6 + t][r:r + CHUNK, h * P:(h + 1) * P],
                                       gq[:, h, cc * CHUNK:(cc + 1) * CHUNK], sg[:, cc - 1, h * P:(h + 1) * P],
                                       start=False, stop=True, skip_group_check=True)
                mm.then_inc(pe_done, PE.step(f"g.o{t}"))
            t_headnorm(pe, "g", o_tm, 0)
            pe.wait_ge(vec_done, VE.at("m.rope"))
            for n, src in enumerate((mq, mk)):
                for t in range(NT):
                    for q in range(4):
                        mm = pe.transpose(PS[2 + 2 * n + t][:, q * P:(q + 1) * P], src[:, t, q * P:(q + 1) * P], ident)
                mm.then_inc(pe_done, PE.step(f"m.tr{n}"))
            pe.wait_ge(vec_done, VE.at("m.kT"))
            pe.wait_ge(act_done, AC.at("m.qT"))
            for i in range(MOBA_H + 2):
                if i < MOBA_H:
                    h, r = i, slice(HD * (i % 2), HD * (i % 2) + HD)
                    if h >= 2:
                        pe.wait_ge(vec_done, VE.at(f"m.s{h - 2}"))
                    bank = PS[h % 2]
                    pe.matmul(bank[:, 0:P], mqT[r, h // 2, 0:P], mkT[r, h // 2, 0:P], start=True, stop=True)
                    pe.matmul(bank[:, P:384], mqT[r, h // 2, P:T], mkT[r, h // 2, 0:T], start=True, stop=True)\
                      .then_inc(pe_done, PE.step(f"m.qk{h}"))
                if 1 <= i <= MOBA_H:
                    h = i - 1
                    pe.wait_ge(vec_done, VE.at(f"m.p{h}"))
                    if h >= 2:
                        pe.wait_ge(act_done, AC.at(f"m.pT{h - 2}"))
                    for n in range(3):
                        mm = pe.transpose(PS[2 + h % 2][:, n * P:(n + 1) * P], prob(h)[:, n * P:(n + 1) * P], ident)
                    mm.then_inc(pe_done, PE.step(f"m.ptr{h}"))
                if i >= 2:
                    h = i - 2
                    r = slice(HD * (h % 2), HD * (h % 2) + HD)
                    pe.wait_ge(act_done, AC.at(f"m.pT{h}"))
                    bank = PS[4 + h // 4][r, ((h // 2) % 2) * T:((h // 2) % 2 + 1) * T]
                    pe.matmul(bank, mv[:, 0, h * HD:(h + 1) * HD], probT(h)[:, 0:T],
                              start=True, stop=False, skip_group_check=True)
                    pe.matmul(bank[:, P:T], mv[:, 1, h * HD:(h + 1) * HD], probT(h)[:, T:384],
                              start=False, stop=True, skip_group_check=True)\
                      .then_inc(pe_done, PE.step(f"m.pv{h}"))
            pe.wait_ge(vec_done, VE.at("l.rows"))
            pe.wait_ge(act_done, AC.at("l.rows"))
            pe.wait_ge(act_done, AC.at("m.y"))
            for n, row in enumerate((rows[1], rows[4], rows[5])):
                for t in range(NT):
                    mm = pe.transpose(PS[0][:, (n * NT + t) * 4:(n * NT + t) * 4 + 4], row[:, t * P:(t + 1) * P],
                                      ident[0:4, 0:4])
            mm.then_inc(pe_done, PE.step("l.cols"))
            sel = c("sel", 4).rearrange("p (h n) -> p h n", n=P)
            selp = c("selp", 4).rearrange("p (h n) -> p h n", n=P)
            for h in range(4):
                mm = pe.matmul(PS[1 + h // 2][:, (h % 2) * T:(h % 2 + 1) * T], sel[:, h, :], rows[3],
                               start=True, stop=True)
            mm.then_inc(pe_done, PE.step("l.negM"))
            for q in range(2):
                mm = pe.matmul(PS[3][:, q * T:(q + 1) * T], selp[:, q, :], rows[6], start=True, stop=True)
            mm.then_inc(pe_done, PE.step("l.iw"))
            pe.wait_ge(vec_done, VE.at("l.negMread"))
            for q in range(2):
                mm = pe.matmul(PS[1][:, q * 4:q * 4 + 4], selp[:, q, :], rows[7][:, 0:4], start=True, stop=True)
            mm.then_inc(pe_done, PE.step("l.a"))
            pe.wait_ge(vec_done, VE.at("l.qkc"))
            for odd in range(2):
                r = slice(ML_DK * odd, ML_DK * odd + ML_DK)
                for t in range(NT):
                    for q in range(2):
                        mm = pe.matmul(PS[4 + odd][:, (2 * t + q) * P:(2 * t + q + 1) * P],
                                       lc[r, 2 + q, t * P:(t + 1) * P], lc[r, q, t * P:(t + 1) * P],
                                       start=True, stop=True)
                mm.then_inc(pe_done, PE.step(f"l.s{odd}"))
            for t in range(NT):
                for q in range(2):
                    mm = pe.transpose(PS[6][:, (t * 2 + q) * P:(t * 2 + q + 1) * P], lc[:, 2 + q, t * P:(t + 1) * P],
                                      ident)
            mm.then_inc(pe_done, PE.step("l.ktr"))
            pe.wait_ge(vec_done, VE.at("l.kw"))
            pe.wait_ge(vec_done, VE.at("l.qi"))
            pe.wait_ge(vec_done, VE.at("l.acol"))
            for cc in range(3):
                t, r = cc // 2, slice(CHUNK * (cc % 2), CHUNK * (cc % 2) + CHUNK)
                for h in range(4):
                    q = h // 2
                    mm = pe.matmul(PS[1 + cc][ML_DK * (h % 2):ML_DK * (h % 2) + ML_DK, q * 129:(q + 1) * 129],
                                   kw[r, t, h * ML_DK:(h + 1) * ML_DK], lv[r, t, h, :], start=True, stop=True,
                                   skip_group_check=True)
                mm.then_inc(pe_done, PE.step(f"l.kv{cc}"))
            pe.wait_ge(vec_done, VE.at("l.st"))
            pe.wait_ge(vec_done, VE.at("l.sm1"))
            for t in range(NT):
                for h in (0, 2, 1, 3):
                    bank = PS[4 + 2 * t + h % 2][:, (h // 2) * 129:(h // 2 + 1) * 129]
                    pe.matmul(bank, attn[:, t, h * P:(h + 1) * P], lv[:, t, h, :], start=True, stop=False,
                              skip_group_check=True)
                    rr = slice(ML_DK * (h % 2), ML_DK * (h % 2) + ML_DK)
                    for cc in (2 * t, 2 * t + 1):
                        if cc == 0:
                            continue
                        r = CHUNK * (cc % 2)
                        mm = pe.matmul(bank[r:r + CHUNK, :], lc[rr, h // 2, cc * CHUNK:(cc + 1) * CHUNK],
                                       st[rr, cc - 1, h // 2, :], start=False, stop=True, skip_group_check=True)
                    if h // 2:
                        mm.then_inc(pe_done, PE.step(f"l.o{t}{h % 2}"))
            t_headnorm(pe, "l", o_tm, 0)
            pe.wait_ge(vec_done, VE.at("l.y1"))
            n = 0
            for b, y in enumerate((yg, ym, yl)):
                for s in range(2):
                    w = rg.take(pe).rearrange("p (k n) -> p k n", n=512)
                    for q in range(2):
                        if n >= 4:
                            pe.wait_ge(vec_done, VE.at(f"br.g{n - 4}"))
                        for f in range(2):
                            for k in range(4):
                                cb = slice((2 * q + f) * P, (2 * q + f + 1) * P)
                                mm = pe.matmul(PS[2 + n % 4][:, f * T:(f + 1) * T], w[:, k, cb], y[:, k, :],
                                               start=(k == 0), stop=(k == 3))
                        if q == 0:
                            mm.then_inc(pe_done, PE.step(f"br.{n}"))
                        n += 1
                    mm.then_inc(slots_used, 1)
            pe.wait_ge(vec_done, VE.at("br.mix"))
            t_out(pe, "wo", lambda k: gates[:, k, :])
            t_transpose(pe, "n2", scr, [(vec_done, VE.at("n2.hn1"))])
            pe.wait_ge(act_done, AC.at("n2.xT"))
            pe.wait_ge(vec_done, VE.at("n2.xT"))
            t_ffn(pe, "f1", DFF1 // UNIT, False)

        mqT = sg[:, 0:2, :].rearrange("p a b -> p (a b)").rearrange("p (b t) -> p b t", t=T)
        mkT = keT[:, :, :].rearrange("p a b -> p (a b)").rearrange("p (b t) -> p b t", t=T)
        pr = big[:, GG:GG + 768].rearrange("p (n c) -> p n c", n=2)
        prT = big[:, GV:GV + 768].rearrange("p (n c) -> p n c", n=2)
        lc = fm(GK, 4)
        kw = keT[:, :, 0:256]
        ex = scr[:, 0, :]

        def prob(h):
            return pr[:, h % 2, :]

        def probT(h):
            return prT[:, h % 2, :]

        def a_sp(act, z, out_ap, name):
            act.activation(out_ap, z, ACT.Abs).then_inc(act_done, AC.step())
            a_wait(act)
            act.activation(out_ap, out_ap, ACT.Exp, scale=-1.0).then_inc(act_done, AC.step())
            a_wait(act)
            act.activation(out_ap, out_ap, ACT.Ln, bias=1.0).then_inc(act_done, AC.step(name))

        def l1_scalar(act, it):
            act.dma_start(par[:, 0:NP1], par1_d[bass.ds(it, 1)].rearrange("o p n -> p (o n)")
                          if not isinstance(it, int) else par1_d[it]).then_inc(par_loaded, 16)
            act.wait_ge(x_loaded, 16)
            a_rms(act, "n1")
            act.wait_ge(par_loaded, it * 16 + 16)
            a_transposed(act, "n1", p1("n1"))
            AC.names["pj.go"] = AC.n
            gb = p1("gateb")
            act.wait_ge(vec_done, VE.at("l.pad"))
            for n in range(0, PROJ1, 2):
                act.wait_ge(slots_used, n + 1)
                if NAMES1[n] == "gate":
                    for q in range(2):
                        b = 2 * (n - 20) + q
                        ins = act.activation(gates[:, b, :], PS[4 + n % 4][:, q * T:(q + 1) * T], ACT.Sigmoid,
                                             bias=gb[:, b:b + 1])
                        ins.then_inc(act_done, AC.step(f"pj.ev{n}" if q else None))
                else:
                    func = {"gg": ACT.Silu, "lo": ACT.Sigmoid}.get(NAMES1[n], ACT.Copy)
                    act.activation(evac_tile(n), bank_view(n), func).then_inc(act_done, AC.step(f"pj.ev{n}"))
            act.wait_ge(vec_done, VE.at("pj.ev31"))
            act.activation(gg[:, 2:4, :], gg[:, 2:4, :], ACT.Silu).then_inc(act_done, AC.step("ggs"))
            act.activation(lo[:, 2:4, :], lo[:, 2:4, :], ACT.Sigmoid).then_inc(act_done, AC.step("los"))
            for n in range(21, PROJ1, 2):
                b = 2 * (n - 20)
                act.activation(gates[:, b:b + 2, :], gates[:, b:b + 2, :], ACT.Sigmoid)\
                   .then_inc(act_done, AC.step())
            act.wait_ge(pe_done, PE.at("ga"))
            act.activation(small[0:LOWRANK, 256:512], PS[0][0:LOWRANK, 0:T], ACT.Copy)\
               .then_inc(act_done, AC.step("gaT"))
            act.wait_ge(vec_done, VE.at("g.z"))
            a_sp(act, BC, TMP, "g.sp")
            act.wait_ge(vec_done, VE.at("g.B"))
            act.activation(E1, BC, ACT.Exp, scale=1.0 / GATE_NORM).then_inc(act_done, AC.step("g.eb"))
            act.activation(E2, BC, ACT.Exp, scale=-1.0 / GATE_NORM).then_inc(act_done, AC.step("g.en"))
            act.wait_ge(vec_done, VE.at("g.diff"))
            act.activation(TMP, TMP, ACT.Exp, scale=1.0 / GATE_NORM).then_inc(act_done, AC.step("g.ek"))
            for t in range(NT):
                act.wait_ge(pe_done, PE.at(f"g.ke{t}"))
                act.activation(keT[:, t, :], PS[6 + t][:, :], ACT.Copy).then_inc(act_done, AC.step(f"g.keT{t}"))
            a_headnorm(act, "g")
            act.wait_ge(vec_done, VE.at("m.ss"))
            act.activation(small[:, 80:112], small[:, 80:112], ACT.Sqrt, bias=eps_rms[:, 0:1], scale=1.0 / HD)\
               .then_inc(act_done, AC.step("m.root"))
            act.wait_ge(pe_done, PE.at("m.tr0"))
            for t in range(NT):
                act.activation(mqT[:, :, t * P:(t + 1) * P], PS[2 + t][:, :].rearrange("p (q n) -> p q n", n=P),
                               ACT.Copy).then_inc(act_done, AC.step("m.qT" if t else None))
            for i in range(MOBA_H + 1):
                if i < MOBA_H:
                    h = i
                    act.wait_ge(vec_done, VE.at(f"m.mx{h}"))
                    nb = small[:, 112 + 2 * h:114 + 2 * h]
                    for n, cols in enumerate((slice(0, P), slice(P, 384))):
                        act.activation(prob(h)[:, cols], prob(h)[:, cols], ACT.Exp, bias=nb[:, n:n + 1],
                                       scale=HD ** -0.5, accum_out=small[:, 128 + 2 * h + n:129 + 2 * h + n])\
                           .then_inc(act_done, AC.step(f"m.e{h}" if n else None))
                if i >= 1:
                    h = i - 1
                    act.wait_ge(pe_done, PE.at(f"m.ptr{h}"))
                    if h >= 2:
                        act.wait_ge(pe_done, PE.at(f"m.pv{h - 2}"))
                    act.activation(probT(h), PS[2 + h % 2][:, 0:384], ACT.Copy)\
                       .then_inc(act_done, AC.step(f"m.pT{h}"))
            act.wait_ge(pe_done, PE.at("m.pv7"))
            for j in range(2):
                act.activation(ym[:, 2 * j:2 * j + 2, :], PS[4 + j][:, :].rearrange("p (b t) -> p b t", t=T),
                               ACT.Copy).then_inc(act_done, AC.step("m.y" if j else None))
            act.wait_ge(vec_done, VE.at("l.z"))
            a_sp(act, rows[2], rows[3], "l.sp")
            act.wait_ge(vec_done, VE.at("l.args"))
            act.activation(rows[4], rows[4], ACT.Exp).then_inc(act_done, AC.step())
            act.activation(rows[5], rows[5], ACT.Exp).then_inc(act_done, AC.step())
            act.activation(rows[6], rows[6], ACT.Exp).then_inc(act_done, AC.step())
            act.activation(rows[7][:, 0:4], rows[7][:, 0:4], ACT.Exp).then_inc(act_done, AC.step("l.rows"))
            act.wait_ge(vec_done, VE.at("l.ex"))
            act.activation(ex, ex, ACT.Exp).then_inc(act_done, AC.step("l.exp"))
            for t in range(NT):
                for q in range(2):
                    act.wait_ge(pe_done, PE.at(f"l.o{t}{q}"))
                    act.activation(oa[:, t, q:4:2, :],
                                   PS[4 + 2 * t + q][:, 0:258].rearrange("p (h d) -> p h d", d=129),
                                   ACT.Copy).then_inc(act_done, AC.step("l.oa" if t and q else None))
            a_headnorm(act, "l")
            a_rms(act, "n2")
            a_transposed(act, "n2", p1("n2"))
            AC.names["f1.go"] = AC.n
            a_ffn(act, "f1", DFF1 // UNIT, False, PROJ1 + 6 + 4)

        E1 = attn[:, :, :].rearrange("p a b -> p (a b)")
        E2 = o_tm[:, :, :].rearrange("p a b -> p (a b)")
        oa = big[:, MK:MK + 2 * 4 * 129].rearrange("p (t h d) -> p t h d", t=NT, h=4)

        def l1_vector(v, it):
            v.wait_ge(x_loaded, 16)
            v.wait_ge(con_loaded, 16)
            v_rms(v, "n1")
            v.wait_ge(par_loaded, it * 16 + 16)
            v.memset(lqk[:, :, 0:3], 0.0).then_inc(vec_done, VE.step())
            v.memset(lv[:, :, :, 128:129], 1.0).then_inc(vec_done, VE.step("l.pad"))
            v_transposed(v, "n1", p1("n1"))
            VE.names["pj.go"] = VE.n
            gb = p1("gateb")
            for n in range(1, PROJ1, 2):
                v.wait_ge(slots_used, n + 1)
                if NAMES1[n] == "gate":
                    for q in range(2):
                        b = 2 * (n - 20) + q
                        v.tensor_scalar(gates[:, b, :], PS[4 + n % 4][:, q * T:(q + 1) * T], gb[:, b:b + 1], None,
                                        ALU.add).then_inc(vec_done, VE.step(f"pj.ev{n}" if q else None))
                else:
                    v.tensor_copy(evac_tile(n), bank_view(n)).then_inc(vec_done, VE.step(f"pj.ev{n}"))
            v.wait_ge(pe_done, PE.at("lif"))
            ib = p1("ifb", 4)
            v.tensor_scalar(rows[0], PS1[0:4, 0:T], ib[:, 0:1], None, ALU.add).then_inc(vec_done, VE.step())
            v.tensor_scalar(rows[2], PS1[0:4, T:2 * T], ib[:, 1:2], None, ALU.add)\
             .then_inc(vec_done, VE.step("l.z"))
            v.wait_ge(pe_done, PE.at("z"))
            ab = p1("ab")
            for h in range(4):
                v.tensor_scalar(BC[:, h * T:(h + 1) * T], PS[2 + h // 2][:, (h % 2) * T:(h % 2 + 1) * T],
                                ab[:, h:h + 1], None, ALU.add).then_inc(vec_done, VE.step("g.z" if h == 3 else None))
            v.wait_ge(act_done, AC.at("g.sp"))
            v.scalar_tensor_tensor(out=E1, in0=BC, scalar=0.0, in1=TMP, op0=ALU.min, op1=ALU.subtract)\
             .then_inc(vec_done, VE.step())
            v_wait(v)
            v.tensor_tensor_scan(BC, reset[:, :], E1, 0.0, ALU.mult, ALU.add).then_inc(vec_done, VE.step("g.B"))
            v_wait(v)
            b3 = BC.rearrange("p (g l) -> p g l", l=CHUNK)
            v.tensor_tensor(TMP.rearrange("p (g l) -> p g l", l=CHUNK),
                            b3[:, :, CHUNK - 1:CHUNK].to_broadcast([P, 16, CHUNK]), b3, ALU.subtract)\
             .then_inc(vec_done, VE.step("g.diff"))
            gqf, gkf = (y.rearrange("p b t -> p (b t)") for y in (gq, gk))
            v.wait_ge(act_done, AC.at("g.eb"))
            v.scalar_tensor_tensor(out=gqf, in0=gqf, scalar=float(P) ** -0.5, in1=E1, op0=ALU.mult, op1=ALU.mult)\
             .then_inc(vec_done, VE.step())
            dec = small[:, 56:72]
            v.tensor_copy(dec, E1.rearrange("p (g l) -> p g l", l=CHUNK)[:, :, CHUNK - 1])\
             .then_inc(vec_done, VE.step("g.dec"))
            v.wait_ge(act_done, AC.at("g.ek"))
            v.tensor_tensor(BC, gkf, TMP, ALU.mult).then_inc(vec_done, VE.step())
            v_wait(v)
            v.tensor_tensor(gkf, gkf, E2, ALU.mult).then_inc(vec_done, VE.step("g.kend"))
            v_wait(v)
            v.memset(attn[:, :, :], 0.0).then_inc(vec_done, VE.step())
            v_wait(v)
            for t in range(NT):
                v.wait_ge(pe_done, PE.at(f"g.s{t}"))
                v.copy_predicated(attn[:, t, :].rearrange("p (h n) -> p h n", n=P),
                                  keep_i.unsqueeze(1).to_broadcast([P, 4, P]),
                                  PS[4 + t][:, :].rearrange("p (h n) -> p h n", n=P)).then_inc(vec_done, VE.step())
            v.wait_ge(pe_done, PE.at("g.kv0"))
            v.tensor_copy(sg[:, 0, :], PS[0][:, :]).then_inc(vec_done, VE.step())
            for cc in (1, 2):
                v_wait(v)
                v.wait_ge(pe_done, PE.at(f"g.kv{cc}"))
                for h in range(4):
                    v.scalar_tensor_tensor(out=sg[:, cc, h * P:(h + 1) * P], in0=sg[:, cc - 1, h * P:(h + 1) * P],
                                           scalar=dec[:, h * NCH + cc:h * NCH + cc + 1],
                                           in1=PS[cc][:, h * P:(h + 1) * P], op0=ALU.mult, op1=ALU.add)\
                     .then_inc(vec_done, VE.step("g.S" if (cc, h) == (2, 3) else None))
            for t in range(NT):
                v.wait_ge(pe_done, PE.at(f"g.o{t}"))
                v.tensor_copy(o_tm[:, t, :], PS[6 + t][:, :]).then_inc(vec_done, VE.step())
            v_wait(v)
            v.wait_ge(act_done, AC.at("los"))
            v_headnorm(v, "g", o_tm[:, :, :], p1("gn"), gg, yg, 0)
            v_wait(v)
            qk3 = [y.rearrange("p t (h d) -> p (t h) d", d=HD) for y in (mq, mk)]
            for n in range(2):
                sq = scr[:, n, :].rearrange("p (g d) -> p g d", d=HD)
                v.tensor_tensor(sq, qk3[n], qk3[n], ALU.mult).then_inc(vec_done, VE.step())
            v_wait(v)
            for n in range(2):
                v.tensor_reduce(small[:, 80 + 16 * n:96 + 16 * n], scr[:, n, :].rearrange("p (g d) -> p g d", d=HD),
                                AX.X, ALU.add).then_inc(vec_done, VE.step("m.ss" if n else None))
            v.wait_ge(act_done, AC.at("m.root"))
            v.reciprocal(small[:, 144:176], small[:, 80:112]).then_inc(vec_done, VE.step())
            v_wait(v)
            cos = c("cos").rearrange("p (t d) -> p t d", t=NT).unsqueeze(2).to_broadcast([P, NT, MOBA_H, 32])
            sin = c("sin").rearrange("p (t d) -> p t d", t=NT).unsqueeze(2).to_broadcast([P, NT, MOBA_H, 32])
            for n in range(2):
                v.tensor_tensor(qk3[n], qk3[n], small[:, 144 + 16 * n:160 + 16 * n].unsqueeze(2)
                                .to_broadcast([P, 16, HD]), ALU.mult).then_inc(vec_done, VE.step())
                v_wait(v)
                v.tensor_tensor(qk3[n], qk3[n], p1("kng" if n else "qng").unsqueeze(1).to_broadcast([P, 16, HD]),
                                ALU.mult).then_inc(vec_done, VE.step())
                v_wait(v)
                y = (mk if n else mq).rearrange("p t (h d) -> p t h d", d=HD)
                a, b = y[:, :, :, 0:32], y[:, :, :, 32:64]
                t4 = [scr[:, i // 2, (i % 2) * 512:(i % 2 + 1) * 512].rearrange("p (t h d) -> p t h d", t=NT, d=32)
                      for i in range(4)]
                for i, (s, tab) in enumerate(((a, cos), (b, sin), (b, cos), (a, sin))):
                    v.tensor_tensor(t4[i], s, tab, ALU.mult).then_inc(vec_done, VE.step())
                v_wait(v)
                v.tensor_tensor(a, t4[0], t4[1], ALU.subtract).then_inc(vec_done, VE.step())
                v.tensor_tensor(b, t4[2], t4[3], ALU.add).then_inc(vec_done, VE.step("m.rope" if n else None))
                v_wait(v)
            v.wait_ge(pe_done, PE.at("m.tr1"))
            for t in range(NT):
                v.tensor_copy(mkT[:, :, t * P:(t + 1) * P], PS[4 + t][:, :].rearrange("p (q n) -> p q n", n=P))\
                 .then_inc(vec_done, VE.step("m.kT" if t else None))
            for i in range(MOBA_H + 1):
                if i < MOBA_H:
                    h = i
                    v.wait_ge(pe_done, PE.at(f"m.qk{h}"))
                    if h >= 2:
                        v.wait_ge(pe_done, PE.at(f"m.ptr{h - 2}"))
                    v.tensor_tensor(prob(h), PS[h % 2][:, 0:384], c("moba"), ALU.add)\
                     .then_inc(vec_done, VE.step(f"m.s{h}"))
                    v_wait(v)
                    mx = small[:, 176 + 2 * h:178 + 2 * h]
                    for n, cols in enumerate((slice(0, P), slice(P, 384))):
                        v.tensor_reduce(mx[:, n:n + 1], prob(h)[:, cols], AX.X, ALU.max)\
                         .then_inc(vec_done, VE.step())
                    v_wait(v)
                    v.tensor_scalar(small[:, 112 + 2 * h:114 + 2 * h], mx, -HD ** -0.5, None, ALU.mult)\
                     .then_inc(vec_done, VE.step(f"m.mx{h}"))
                if i >= 1:
                    h = i - 1
                    v.wait_ge(act_done, AC.at(f"m.e{h}"))
                    rs = small[:, 192 + 2 * h:194 + 2 * h]
                    v.reciprocal(rs, small[:, 128 + 2 * h:130 + 2 * h]).then_inc(vec_done, VE.step())
                    v_wait(v)
                    for n, cols in enumerate((slice(0, P), slice(P, 384))):
                        v.tensor_scalar(prob(h)[:, cols], prob(h)[:, cols], rs[:, n:n + 1], None, ALU.mult)\
                         .then_inc(vec_done, VE.step(f"m.p{h}" if n else None))
            cw = p1("convw")
            for w in range(4):
                for b in range(4):
                    src = lqk[:, b, w:w + T]
                    if w == 0:
                        v.tensor_scalar(lc[:, b, :], src, cw[:, 4 * b:4 * b + 1], None, ALU.mult)\
                         .then_inc(vec_done, VE.step())
                    else:
                        if b == 0:
                            v_wait(v)
                        v.scalar_tensor_tensor(out=lc[:, b, :], in0=src, scalar=cw[:, 4 * b + w:4 * b + w + 1],
                                               in1=lc[:, b, :], op0=ALU.mult, op1=ALU.add)\
                         .then_inc(vec_done, VE.step("l.qkc" if (w, b) == (3, 3) else None))
            v.wait_ge(act_done, AC.at("l.sp"))
            v.scalar_tensor_tensor(out=rows[3], in0=rows[2], scalar=0.0, in1=rows[3], op0=ALU.min, op1=ALU.subtract)\
             .then_inc(vec_done, VE.step())
            v_wait(v)
            v.tensor_tensor_scan(rows[2], reset[0:4, 0:T], rows[3], 0.0, ALU.mult, ALU.add)\
             .then_inc(vec_done, VE.step())
            v_wait(v)
            v.tensor_tensor(rows[1], rows[0], rows[2], ALU.subtract).then_inc(vec_done, VE.step())
            v.memset(rows[4], 0.0).then_inc(vec_done, VE.step())
            v_wait(v)
            ch = [r.rearrange("p (c l) -> p c l", l=CHUNK) for r in rows]
            v.tensor_copy(ch[4][:, 1:4, 0], ch[2][:, 0:3, CHUNK - 1]).then_inc(vec_done, VE.step())
            v_wait(v)
            v.tensor_tensor_scan(rows[0], rows[4], rows[1], 0.0, ALU.add, ALU.max).then_inc(vec_done, VE.step())
            v_wait(v)
            v.memset(rows[7][:, 0:8], 0.0).then_inc(vec_done, VE.step())
            v_wait(v)
            v.tensor_tensor(rows[7][:, 1:4], ch[2][:, 0:3, CHUNK - 1], ch[0][:, 0:3, CHUNK - 1], ALU.add)\
             .then_inc(vec_done, VE.step())
            v.tensor_copy(rows[7][:, 4:8], ch[0][:, :, CHUNK - 1]).then_inc(vec_done, VE.step())
            v.tensor_scalar(rows[3], rows[0], -1.0, None, ALU.mult).then_inc(vec_done, VE.step())
            v.scalar_tensor_tensor(out=rows[4], in0=rows[2], scalar=-1.0, in1=rows[0], op0=ALU.mult,
                                   op1=ALU.subtract).then_inc(vec_done, VE.step())
            v_wait(v)
            v.tensor_tensor(ch[5], ch[1], rows[7][:, 4:8].unsqueeze(2).to_broadcast([4, 4, CHUNK]), ALU.subtract)\
             .then_inc(vec_done, VE.step())
            v.tensor_tensor(ch[6], rows[7][:, 0:4].unsqueeze(2).to_broadcast([4, 4, CHUNK]), ch[0], ALU.subtract)\
             .then_inc(vec_done, VE.step())
            v_wait(v)
            v.tensor_tensor(rows[7][:, 0:4], rows[7][:, 0:4], rows[7][:, 4:8], ALU.subtract)\
             .then_inc(vec_done, VE.step("l.args"))
            VE.names["l.rows"] = VE.n
            cols = small[:, 208:232].rearrange("p (n t h) -> p n t h", n=3, t=NT)
            v.wait_ge(pe_done, PE.at("l.cols"))
            v.tensor_copy(small[:, 208:232], PS[0][:, 0:24]).then_inc(vec_done, VE.step())
            v_wait(v)
            v.wait_ge(pe_done, PE.at("l.negM"))
            for t in range(NT):
                for h in range(4):
                    v.scalar_tensor_tensor(out=ex[:, (t * 4 + h) * P:(t * 4 + h + 1) * P],
                                           in0=PS[1 + h // 2][:, (h % 2) * T + t * P:(h % 2) * T + (t + 1) * P],
                                           scalar=cols[:, 0, t, h:h + 1], in1=c("neg"), op0=ALU.add, op1=ALU.min)\
                     .then_inc(vec_done, VE.step())
            VE.names["l.ex"] = VE.names["l.negMread"] = VE.n
            v.wait_ge(pe_done, PE.at("l.a"))
            acol = small[:, 232:240].rearrange("p (q c) -> p q c", q=2)
            v.tensor_copy(small[:, 232:240], PS[1][:, 0:8]).then_inc(vec_done, VE.step("l.acol"))
            v.wait_ge(act_done, AC.at("l.exp"))
            for t in range(NT):
                v.wait_ge(pe_done, PE.at(f"l.s{t}"))
                def parity(y):
                    return y.rearrange("p (t q o n) -> p o t q n", t=NT, q=2, o=2)[:, t]
                v.scalar_tensor_tensor(out=parity(attn[:, :, :].rearrange("p t n -> p (t n)")),
                                       in0=PS[4 + t][:, :].rearrange("p (t q n) -> p t q n", t=NT, q=2),
                                       scalar=ML_DK ** -0.5, in1=parity(ex), op0=ALU.mult, op1=ALU.mult)\
                 .then_inc(vec_done, VE.step(f"l.sm{t}"))
            v.wait_ge(pe_done, PE.at("l.ktr"))
            v.scalar_tensor_tensor(out=kw.rearrange("p t (h d) -> p t h d", d=HD),
                                   in0=PS[6][:, :].rearrange("p (t h d) -> p t h d", t=NT, d=HD),
                                   scalar=ML_DK ** -0.5,
                                   in1=cols[:, 2, :, :].unsqueeze(3).to_broadcast([P, NT, 4, HD]),
                                   op0=ALU.mult, op1=ALU.mult).then_inc(vec_done, VE.step("l.kw"))
            v.wait_ge(pe_done, PE.at("l.iw"))
            v.tensor_tensor(lc[:, 0:2, :], lc[:, 0:2, :], PS[3][:, :].rearrange("p (b t) -> p b t", t=T), ALU.mult)\
             .then_inc(vec_done, VE.step("l.qi"))
            v.wait_ge(pe_done, PE.at("l.kv0"))
            v.tensor_copy(st[:, 0, :, :], PS[1][:, 0:258].rearrange("p (q d) -> p q d", d=129))\
             .then_inc(vec_done, VE.step())
            for cc in (1, 2):
                v_wait(v)
                v.wait_ge(pe_done, PE.at(f"l.kv{cc}"))
                for q in range(2):
                    v.scalar_tensor_tensor(out=st[:, cc, q, :], in0=st[:, cc - 1, q, :],
                                           scalar=acol[:, q, cc:cc + 1], in1=PS[1 + cc][:, q * 129:(q + 1) * 129],
                                           op0=ALU.mult, op1=ALU.add)\
                     .then_inc(vec_done, VE.step("l.st" if (cc, q) == (2, 1) else None))
            v.wait_ge(act_done, AC.at("l.oa"))
            den = oa[:, :, :, 128]
            dn = small[:, 240:248].rearrange("p (t h) -> p t h", t=NT)
            v.scalar_tensor_tensor(out=dn, in0=den, scalar=-1.0, in1=den, op0=ALU.mult, op1=ALU.max)\
             .then_inc(vec_done, VE.step())
            v_wait(v)
            v.tensor_tensor(dn, dn, cols[:, 1, :, :], ALU.max).then_inc(vec_done, VE.step())
            v_wait(v)
            v.reciprocal(small[:, 248:256], small[:, 240:248]).then_inc(vec_done, VE.step())
            v_wait(v)
            v.tensor_tensor(o_tm[:, :, :].rearrange("p t (h d) -> p t h d", d=P), oa[:, :, :, 0:128],
                            small[:, 248:256].rearrange("p (t h) -> p t h", t=NT).unsqueeze(3)
                            .to_broadcast([P, NT, 4, P]), ALU.mult).then_inc(vec_done, VE.step())
            v_wait(v)
            v_headnorm(v, "l", o_tm[:, :, :], p1("mn"), lo, yl, 0)
            gf = gates.rearrange("p b t -> p (b t)")
            for n in range(12):
                b, q = n // 4, n % 4
                if n % 2 == 0:
                    v.wait_ge(pe_done, PE.at(f"br.{n}"))
                else:
                    v.wait_ge(slots_used, PROJ1 + n // 2 + 1)
                own = gf[:, (b * 8 + 2 * q) * T:(b * 8 + 2 * q + 2) * T]
                v.tensor_tensor(own, own, PS[2 + n % 4][:, :], ALU.mult).then_inc(vec_done, VE.step(f"br.g{n}"))
                if b:
                    v_wait(v)
                    acc = gf[:, 2 * q * T:(2 * q + 2) * T]
                    v.tensor_tensor(acc, acc, own, ALU.add).then_inc(vec_done, VE.step("br.mix" if n == 11 else None))
            v_residual(v, PROJ1 + 6 + 4, 1.0, "x1")
            v_wait(v)
            v_rms(v, "n2")
            v_transposed(v, "n2", p1("n2"))
            VE.names["f1.go"] = VE.n
            v_ffn(v, "f1", DFF1 // UNIT, False, PROJ1 + 6 + 4)
            v_residual(v, SLOTS_L1, 1.0, "x2")

        PS1 = PS[1]

        PAD = CONV_WIN - 1
        cv = big[:, 0:4 * (PAD + T)].rearrange("p (b t) -> p b t", t=PAD + T)
        cg = fm(1144, 4)
        qkvr = big[:, 2168:2168 + 12 * W3].rearrange("p (b t) -> p b t", t=W3)
        zt = fm(5276, 4)
        qc = fm(6300, 12)
        dq, dk, dv = qc[:, 0:4, :], qc[:, 4:8, :], qc[:, 8:12, :]
        ca = fm(9372, 4)
        caf = big[:, 9372:9372 + 1024]
        kbT, qg = fm(10396, 4), fm(11420, 4)
        kbTf, qgf = big[:, 10396:11420], big[:, 11420:12444]
        vb, kbg, kdec = tm(13468, 512), tm(14492, 512), tm(15516, 512)
        mA_T, mA, mNT, mN, mQ = (tm(1024 * i, 512) for i in range(5))
        mN2, mIN2, mN2T = scr[:, 1, 0:512], scr[:, 1, 512:1024], keT
        mIN4, mP1, mU = mNT, mN, mQ
        nw = fm(0, 4)
        vn = tm(1024, 512)
        S = sg[:, 0, :]
        comb = sb("comb", [P, NT, NEXP])
        ccol = sb("ccol", [P, NT])
        Y = big[:, 0:2 * D].rearrange("p (t n) -> p t n", t=NT)
        KINDS2 = ["fm"] * 12

        def hh(ap):
            return ap.rearrange("p (h n) -> p h n", n=P)

        def over_heads(mask):
            return mask.unsqueeze(1).to_broadcast([P, 4, P])

        def evac2(n):
            if n < 2:
                return cv[:, 2 * n:2 * n + 2, PAD:PAD + T]
            if n < 4:
                return cg[:, 2 * n - 4:2 * n - 2, :]
            if n < 10:
                return qkvr[:, 2 * (n - 4):2 * (n - 4) + 2, 3:W3]
            return zt[:, 2 * (n - 10):2 * (n - 10) + 2, :]

        def t_ln(pe, tag):
            t_transpose(pe, tag, X, [(vec_done, VE.at(tag + ".x"))])

        def mix_tensor(pe, tag, layer, last):
            rg.start("mix" + tag, 0)
            t_ln(pe, tag + "n1")
            pe.wait_ge(act_done, AC.at(tag + "n1.xT"))
            pe.wait_ge(vec_done, VE.at(tag + "n1.xT"))
            t_project(pe, tag + "pj", KINDS2)
            pe.wait_ge(par_loaded, 16 * ((DEPTH if RUN_FIRST else 0) + layer + 1))
            for n, name in enumerate(("wb", "wa")):
                w = p2(name).rearrange("p (k n) -> p k n", n=4)
                for k in range(KD):
                    mm = pe.matmul(PS[0][0:4, n * T:(n + 1) * T], w[:, k, :], xT[:, k, :],
                                   start=(k == 0), stop=(k == KD - 1))
            mm.then_inc(pe_done, PE.step(tag + "ba"))
            pe.wait_ge(vec_done, VE.at(tag + "sq"))
            for i in range(4):
                mm = pe.matmul(PS[1 + i][:, :], c("ones"), scr[:, i // 2, (i % 2) * 512:(i % 2 + 1) * 512],
                               start=True, stop=True)
            mm.then_inc(pe_done, PE.step(tag + "ssq"))
            pe.wait_ge(vec_done, VE.at(tag + "rows"))
            pe.wait_ge(act_done, AC.at(tag + "rows"))
            pe.wait_ge(vec_done, VE.at(tag + "l2"))
            for n, row in enumerate((rows[0], rows[1], rows[2], rows[3])):
                for t in range(NT):
                    mm = pe.transpose(PS[0][:, (n * NT + t) * 4:(n * NT + t) * 4 + 4], row[:, t * P:(t + 1) * P],
                                      ident[0:4, 0:4])
            mm.then_inc(pe_done, PE.step(tag + "cols"))
            sel = c("sel", 4).rearrange("p (h n) -> p h n", n=P)
            for n, row in enumerate((rows[0], rows[1], rows[4])):
                for h in range(4):
                    mm = pe.matmul(PS[1 + 2 * n + h // 2][:, (h % 2) * T:(h % 2 + 1) * T], sel[:, h, :], row,
                                   start=True, stop=True)
                mm.then_inc(pe_done, PE.step(tag + f"bc{n}"))
            for h in range(4):
                mm = pe.matmul(PS[7][:, h * 4:h * 4 + 4], sel[:, h, :], rows[5][:, 0:4], start=True, stop=True)
            mm.then_inc(pe_done, PE.step(tag + "egl"))
            pe.wait_ge(vec_done, VE.at(tag + "bcs"))
            for i, (src, dst) in enumerate(((dv, "v"), (dk, "k"))):
                for t in range(NT):
                    for h in range(4):
                        mm = pe.transpose(PS[2 * i + t][:, h * P:(h + 1) * P], src[:, h, t * P:(t + 1) * P], ident)
                    mm.then_inc(pe_done, PE.step(tag + f"tr{dst}{t}"))
            for t in range(NT):
                for i, src in enumerate((kbT, dq)):
                    for h in range(4):
                        mm = pe.matmul(PS[4 + 2 * t + i][:, h * P:(h + 1) * P], dk[:, h, t * P:(t + 1) * P],
                                       src[:, h, t * P:(t + 1) * P], start=True, stop=True)
                mm.then_inc(pe_done, PE.step(tag + f"kk{t}"))

            def per_head(t, bank, lhs, rhs, name):
                for h in range(4):
                    hc = slice(h * P, (h + 1) * P)
                    mm = pe.matmul(PS[bank][:, hc], lhs[:, hc], rhs[:, hc], start=True, stop=True)
                mm.then_inc(pe_done, PE.step(tag + name + str(t)))

            def turn(t, bank, src, name):
                for h in range(4):
                    hc = slice(h * P, (h + 1) * P)
                    mm = pe.transpose(PS[bank][:, hc], src[:, hc], ident)
                mm.then_inc(pe_done, PE.step(tag + name + str(t)))
            for t in range(NT):
                pe.wait_ge(vec_done, VE.at(tag + "kdec"))
                pe.wait_ge(vec_done, VE.at(tag + f"Q{t}"))
                turn(t, 0, mA_T[:, t, :], "A")
                turn(t, 1, mNT[:, t, :], "N")
                pe.wait_ge(act_done, AC.at(tag + f"N{t}"))
                per_head(t, 2, mNT[:, t, :], mN[:, t, :], "N2")
                per_head(t, 3, mN[:, t, :], mNT[:, t, :], "N2T")
                pe.wait_ge(vec_done, VE.at(tag + f"IN2{t}"))
                pe.wait_ge(act_done, AC.at(tag + f"N2T{t}"))
                per_head(t, 0, mN2T[:, t, :], mN2, "N4")
                per_head(t, 1, mIN2, mQ[:, t, :], "P1")
                pe.wait_ge(vec_done, VE.at(tag + f"IN4{t}"))
                pe.wait_ge(act_done, AC.at(tag + f"P1{t}"))
                per_head(t, 2, mIN4[:, t, :], mP1[:, t, :], "U")
                for lev in range(3):
                    pe.wait_ge(vec_done, VE.at(tag + f"U{lev}{t}"))
                    per_head(t, 3, mN2T[:, t, :], mU[:, t, :], f"X{lev}")
                    turn(t, 0, mU[:, t, :], f"T{lev}")
                    pe.wait_ge(vec_done, VE.at(tag + f"T{lev}{t}"))
                    pe.wait_ge(act_done, AC.at(tag + f"X{lev}{t}"))
                    per_head(t, 2, mN2, mIN2, f"UX{lev}")
                pe.wait_ge(vec_done, VE.at(tag + f"U3{t}"))
            for t in range(NT):
                per_head(t, t, kbg[:, t, :], mU[:, t, :], "w")
            pe.wait_ge(vec_done, VE.at(tag + "w"))
            for cc in range(NCH):
                t, r = cc // 2, slice(CHUNK * (cc % 2), CHUNK * (cc % 2) + CHUNK)
                b = 2 + 3 * (cc % 2)
                tok = slice(cc * CHUNK, (cc + 1) * CHUNK)
                if cc:
                    pe.wait_ge(vec_done, VE.at(tag + f"S{cc - 1}"))
                if cc >= 2:
                    pe.wait_ge(act_done, AC.at(tag + f"o{cc - 2}"))
                for h in range(4):
                    hc = slice(h * P, (h + 1) * P)
                    mm = pe.matmul(PS[b][r, hc], mU[r, t, h * P + r.start:h * P + r.stop], vb[r, t, hc],
                                   start=True, stop=(cc == 0))
                    if cc:
                        mm = pe.matmul(PS[b][r, hc], nw[:, h, tok], S[:, hc], start=False, stop=True)
                mm.then_inc(pe_done, PE.step(tag + f"vn{cc}"))
                pe.wait_ge(vec_done, VE.at(tag + f"vn{cc}"))
                for h in range(4):
                    hc = slice(h * P, (h + 1) * P)
                    if cc:
                        pe.matmul(PS[b + 1][r, hc], qg[:, h, tok], S[:, hc], start=True, stop=False)
                    mm = pe.matmul(PS[b + 1][r, hc], attn[r, t, h * P + r.start:h * P + r.stop], vn[r, t, hc],
                                   start=(cc == 0), stop=True)
                mm.then_inc(pe_done, PE.step(tag + f"o{cc}"))
                if cc < NCH - 1:
                    for h in range(4):
                        hc = slice(h * P, (h + 1) * P)
                        bank = PS[4] if cc % 2 == 0 else PS[7]
                        mm = pe.matmul(bank[:, hc], kdec[r, t, hc], vn[r, t, hc], start=True, stop=True)
                    mm.then_inc(pe_done, PE.step(tag + f"dS{cc}"))
            t_headnorm(pe, tag + "d", o_tm, 0)
            pe.wait_ge(vec_done, VE.at(tag + "cc"))
            for b in range(4):
                mm = pe.matmul(PS[2][:, 0:T], c("ones"), ca[:, b, :], start=(b == 0), stop=(b == 3))
            mm.then_inc(pe_done, PE.step(tag + "cmu"))
            pe.wait_ge(vec_done, VE.at(tag + "csq"))
            for b in range(4):
                mm = pe.matmul(PS[3][:, 0:T], c("ones"), scr[:, 0, b * T:(b + 1) * T], start=(b == 0), stop=(b == 3))
            mm.then_inc(pe_done, PE.step(tag + "cvar"))
            pe.wait_ge(act_done, AC.at(tag + "cy"))
            pe.wait_ge(vec_done, VE.at(tag + "d.y1"))
            pe.wait_ge(act_done, AC.at(tag + "o3"))
            t_out(pe, tag + "wo", lambda k: ca[:, k, :] if k < 4 else dq[:, k - 4, :])
            t_ln(pe, tag + "n2")
            if last:
                pe.wait_ge(act_done, AC.at(tag + "n2.xT"))
                pe.wait_ge(vec_done, VE.at(tag + "n2.xT"))
                w = p2("router").rearrange("p (k n) -> p k n", n=NEXP)
                for t in range(NT):
                    for k in range(KD):
                        mm = pe.matmul(PS[0][:, t * NEXP:(t + 1) * NEXP], xT[:, k, t * P:(t + 1) * P], w[:, k, :],
                                       start=(k == 0), stop=(k == KD - 1))
                mm.then_inc(pe_done, PE.step(tag + "route"))

        def mix_scalar(act, tag, layer, last):
            act.dma_start(par[:, 0:NP2], par2_d[layer]).then_inc(par_loaded, 16)
            a_transposed(act, tag + "n1", None)
            AC.names[tag + "pj.go"] = AC.n
            act.wait_ge(vec_done, VE.at(tag + "pad"))
            for n in range(0, 12, 2):
                act.wait_ge(slots_used, n + 1)
                act.activation(evac2(n), PS[4 + n % 4][:, :].rearrange("p (a b) -> p a b", a=2),
                               ACT.Sigmoid if n == 2 else ACT.Silu if n == 10 else ACT.Copy)\
                   .then_inc(act_done, AC.step(tag + f"pj.ev{n}"))
            act.wait_ge(vec_done, VE.at(tag + "pj.ev11"))
            act.activation(cg[:, 2:4, :], cg[:, 2:4, :], ACT.Sigmoid).then_inc(act_done, AC.step(tag + "cg"))
            act.activation(zt[:, 2:4, :], zt[:, 2:4, :], ACT.Silu).then_inc(act_done, AC.step())
            act.wait_ge(vec_done, VE.at(tag + "qkv"))
            act.activation(qc[:, :, :], qc[:, :, :], ACT.Silu).then_inc(act_done, AC.step(tag + "qkv"))
            act.wait_ge(vec_done, VE.at(tag + "z"))
            act.activation(rows[1], rows[1], ACT.Sigmoid).then_inc(act_done, AC.step())
            a_sp(act, rows[2], rows[3], tag + "sp")
            act.activation(small[0:4, 0:1], small[0:4, 0:1], ACT.Exp).then_inc(act_done, AC.step(tag + "ea"))
            act.wait_ge(vec_done, VE.at(tag + "gc"))
            act.activation(rows[4], rows[0], ACT.Exp).then_inc(act_done, AC.step())
            act.activation(rows[3], rows[3], ACT.Exp).then_inc(act_done, AC.step())
            act.activation(rows[5][:, 0:4], rows[5][:, 0:4], ACT.Exp).then_inc(act_done, AC.step(tag + "rows"))
            act.wait_ge(pe_done, PE.at(tag + "ssq"))
            for i in range(4):
                act.activation(scr[:, i // 2, (i % 2) * 512:(i % 2 + 1) * 512], PS[1 + i][:, :], ACT.Sqrt,
                               bias=eps_rms[:, 0:1]).then_inc(act_done, AC.step(tag + "l2r" if i == 3 else None))
            act.wait_ge(vec_done, VE.at(tag + "ex"))
            act.activation(scr[:, 0, :], scr[:, 0, :], ACT.Exp).then_inc(act_done, AC.step(tag + "ET"))
            for t in range(NT):
                def copy(dst, bank, name, pe_name=None):
                    act.wait_ge(pe_done, PE.at(tag + (pe_name or name) + str(t)))
                    act.activation(dst, PS[bank][:, :], ACT.Copy).then_inc(act_done, AC.step(tag + name + str(t)))
                copy(mA[:, t, :], 0, "A")
                copy(mN[:, t, :], 1, "N")
                copy(mN2T[:, t, :], 3, "N2T")
                copy(mP1[:, t, :], 1, "P1")
                for lev in range(3):
                    copy(mIN2, 3, f"X{lev}")
            for cc in range(NCH):
                t, r = cc // 2, slice(CHUNK * (cc % 2), CHUNK * (cc % 2) + CHUNK)
                act.wait_ge(pe_done, PE.at(tag + f"o{cc}"))
                act.activation(o_tm[r, t, :], PS[3 + 3 * (cc % 2)][r, :], ACT.Copy)\
                   .then_inc(act_done, AC.step(tag + f"o{cc}"))
            a_headnorm(act, tag + "d")
            act.wait_ge(pe_done, PE.at(tag + "cvar"))
            act.activation(scr[:, 1, 0:T], PS[3][:, 0:T], ACT.Sqrt, bias=eps_ln[:, 0:1], scale=1.0 / 512)\
               .then_inc(act_done, AC.step(tag + "crs"))
            act.wait_ge(vec_done, VE.at(tag + "cn"))
            act.wait_ge(par_loaded, 16 * ((DEPTH if RUN_FIRST else 0) + layer + 1))
            for b in range(4):
                act.activation(ca[:, b, :], ca[:, b, :], ACT.Silu, bias=p2("clnb")[:, b:b + 1],
                               scale=p2("clng")[:, b:b + 1]).then_inc(act_done, AC.step(tag + "cy" if b == 3 else None))
            a_ln(act, tag + "m")
            a_transposed(act, tag + "n2", None)
            if last:
                act.wait_ge(vec_done, VE.at(tag + "d21"))
                act.activation(small[:, 40:42], small[:, 40:42], ACT.Exp).then_inc(act_done, AC.step(tag + "e21"))

        def v_ln(v, tag, gain, bias, name):
            for t in range(NT):
                for f in range(2):
                    v.bn_stats(small[:, 260 + 12 * t + 6 * f:266 + 12 * t + 6 * f], X[:, t, f * 512:(f + 1) * 512])\
                     .then_inc(vec_done, VE.step())
            v_wait(v)
            for t in range(NT):
                v.bn_aggr(small[:, 290 + 2 * t:292 + 2 * t], small[:, 260 + 12 * t:272 + 12 * t])\
                 .then_inc(vec_done, VE.step(tag + ".var" if t else None))
            v.wait_ge(act_done, AC.at(tag + ".root"))
            v.reciprocal(small[:, 296:298], small[:, 294:296]).then_inc(vec_done, VE.step())
            for t in range(NT):
                v_wait(v)
                v.tensor_scalar(X[:, t, :], X[:, t, :], small[:, 290 + 2 * t:291 + 2 * t],
                                small[:, 296 + t:297 + t], ALU.subtract, ALU.mult).then_inc(vec_done, VE.step())
            for op, y in ((ALU.mult, gain), (ALU.add, bias)):
                v_wait(v)
                for t in range(NT):
                    v.tensor_tensor(X[:, t, :], X[:, t, :], y, op).then_inc(vec_done, VE.step())
            VE.names[name] = VE.n

        def a_ln(act, tag):
            act.wait_ge(vec_done, VE.at(tag + ".var"))
            act.activation(small[:, 294:296], small[:, 291:294:2], ACT.Sqrt, bias=eps_ln[:, 0:1])\
               .then_inc(act_done, AC.step(tag + ".root"))

        def mix_vector(v, tag, layer, last):
            v.wait_ge(x_loaded, 16)
            v.wait_ge(con_loaded, 16)
            v.memset(cv[:, :, 0:PAD], 0.0).then_inc(vec_done, VE.step())
            v.memset(qkvr[:, :, 0:3], 0.0).then_inc(vec_done, VE.step(tag + "pad"))
            VE.names[tag + "n1.x"] = VE.n
            v_transposed(v, tag + "n1", None)
            VE.names[tag + "pj.go"] = VE.n
            for n in range(1, 12, 2):
                v.wait_ge(slots_used, n + 1)
                v.tensor_copy(evac2(n), PS[4 + n % 4][:, :].rearrange("p (a b) -> p a b", a=2))\
                 .then_inc(vec_done, VE.step(tag + f"pj.ev{n}"))
            v.wait_ge(par_loaded, 16 * ((DEPTH if RUN_FIRST else 0) + layer + 1))
            v.wait_ge(act_done, AC.at(tag + "pj.ev10"))
            v_wait(v)
            sc = p2("sconv")
            for w in range(4):
                for b in range(12):
                    src = qkvr[:, b, w:w + T]
                    if w == 0:
                        v.tensor_scalar(qc[:, b, :], src, sc[:, 4 * b:4 * b + 1], None, ALU.mult)\
                         .then_inc(vec_done, VE.step())
                    else:
                        v.wait_ge(vec_done, VE.n - 11)
                        v.scalar_tensor_tensor(out=qc[:, b, :], in0=src, scalar=sc[:, 4 * b + w:4 * b + w + 1],
                                               in1=qc[:, b, :], op0=ALU.mult, op1=ALU.add)\
                         .then_inc(vec_done, VE.step(tag + "qkv" if (w, b) == (3, 11) else None))
            v.wait_ge(pe_done, PE.at(tag + "ba"))
            gp = p2("gpar", 4)
            v.tensor_copy(rows[1], PS[0][0:4, 0:T]).then_inc(vec_done, VE.step())
            v.tensor_copy(small[0:4, 0:1], gp[:, 0:1]).then_inc(vec_done, VE.step())
            v.tensor_scalar(rows[2], PS[0][0:4, T:2 * T], gp[:, 1:2], None, ALU.add)\
             .then_inc(vec_done, VE.step(tag + "z"))
            v.wait_ge(act_done, AC.at(tag + "qkv"))
            qkf = big[:, 6300:6300 + 2048]
            scf = scr[:, :, :].rearrange("p t n -> p (t n)")
            v.tensor_tensor(scf, qkf, qkf, ALU.mult).then_inc(vec_done, VE.step(tag + "sq"))
            v.wait_ge(act_done, AC.at(tag + "ea"))
            v.scalar_tensor_tensor(out=rows[3], in0=rows[2], scalar=0.0, in1=rows[3], op0=ALU.max, op1=ALU.add)\
             .then_inc(vec_done, VE.step())
            v_wait(v)
            v.tensor_scalar(rows[2], rows[3], small[0:4, 0:1], -1.0, ALU.mult, ALU.mult)\
             .then_inc(vec_done, VE.step())
            v_wait(v)
            v.tensor_tensor_scan(rows[0], reset[0:4, 0:T], rows[2], 0.0, ALU.mult, ALU.add)\
             .then_inc(vec_done, VE.step())
            v_wait(v)
            ch = [r.rearrange("p (c l) -> p c l", l=CHUNK) for r in rows]
            v.tensor_tensor(ch[3], ch[0][:, :, CHUNK - 1:CHUNK].to_broadcast([4, 4, CHUNK]), ch[0], ALU.subtract)\
             .then_inc(vec_done, VE.step())
            v.tensor_copy(rows[5][:, 0:4], ch[0][:, :, CHUNK - 1]).then_inc(vec_done, VE.step(tag + "gc"))
            v.wait_ge(act_done, AC.at(tag + "rows"))
            v.tensor_tensor(rows[2], rows[1], rows[4], ALU.mult).then_inc(vec_done, VE.step(tag + "rows"))
            v.wait_ge(act_done, AC.at(tag + "l2r"))
            v.reciprocal(scf, scf).then_inc(vec_done, VE.step())
            v_wait(v)
            v.scalar_tensor_tensor(out=qkf[:, 0:1024], in0=qkf[:, 0:1024], scalar=float(P) ** -0.5,
                                   in1=scf[:, 0:1024], op0=ALU.mult, op1=ALU.mult).then_inc(vec_done, VE.step())
            v.tensor_tensor(qkf[:, 1024:2048], qkf[:, 1024:2048], scf[:, 1024:2048], ALU.mult)\
             .then_inc(vec_done, VE.step(tag + "l2"))
            col = small[:, 80:112].rearrange("p (n t h) -> p n t h", n=4, t=NT)
            v.wait_ge(pe_done, PE.at(tag + "cols"))
            v.tensor_copy(small[:, 80:112], PS[0][:, 0:32]).then_inc(vec_done, VE.step())
            v_wait(v)
            v.wait_ge(pe_done, PE.at(tag + "bc0"))
            for t in range(NT):
                for h in range(4):
                    v.scalar_tensor_tensor(out=scr[:, 0, (t * 4 + h) * P:(t * 4 + h + 1) * P],
                                           in0=PS[1 + h // 2][:, (h % 2) * T + t * P:(h % 2) * T + (t + 1) * P],
                                           scalar=col[:, 0, t, h:h + 1], in1=c("neg"), op0=ALU.subtract,
                                           op1=ALU.min).then_inc(vec_done, VE.step())
            VE.names[tag + "ex"] = VE.n
            v.wait_ge(pe_done, PE.at(tag + "bc1"))
            for i in range(2):
                v.tensor_tensor(kbTf[:, i * 512:(i + 1) * 512], qkf[:, 1024 + i * 512:1536 + i * 512],
                                PS[3 + i][:, :], ALU.mult).then_inc(vec_done, VE.step())
            v.wait_ge(pe_done, PE.at(tag + "bc2"))
            for i in range(2):
                v.tensor_tensor(qgf[:, i * 512:(i + 1) * 512], qkf[:, i * 512:(i + 1) * 512],
                                PS[5 + i][:, :], ALU.mult).then_inc(vec_done, VE.step())
            v.wait_ge(pe_done, PE.at(tag + "egl"))
            egl = small[:, 112:128].rearrange("p (h c) -> p h c", h=4)
            v.tensor_copy(small[:, 112:128], PS[7][:, 0:16]).then_inc(vec_done, VE.step(tag + "bcs"))
            for t in range(NT):
                v.wait_ge(pe_done, PE.at(tag + f"trv{t}"))
                v.tensor_tensor(hh(vb[:, t, :]), hh(PS[t][:, :]), col[:, 1, t, :].unsqueeze(2)
                                .to_broadcast([P, 4, P]), ALU.mult).then_inc(vec_done, VE.step())
            for t in range(NT):
                v.wait_ge(pe_done, PE.at(tag + f"trk{t}"))
                for n, dst in ((2, kbg), (3, kdec)):
                    v.tensor_tensor(hh(dst[:, t, :]), hh(PS[2 + t][:, :]), col[:, n, t, :].unsqueeze(2)
                                    .to_broadcast([P, 4, P]), ALU.mult).then_inc(vec_done, VE.step())
            VE.names[tag + "kdec"] = VE.n
            v.wait_ge(act_done, AC.at(tag + "cg"))
            v.tensor_tensor(cv[:, :, PAD:PAD + T], cv[:, :, PAD:PAD + T], cg[:, :, :], ALU.mult)\
             .then_inc(vec_done, VE.step())
            v_wait(v)
            dw = p2("dww")
            for w in range(CONV_WIN):
                for b in range(4):
                    tap = dw[:, b * CONV_WIN + w:b * CONV_WIN + w + 1]
                    if w == 0:
                        v.tensor_scalar(ca[:, b, :], cv[:, b, w:w + T], tap, p2("dwb")[:, b:b + 1], ALU.mult,
                                        ALU.add).then_inc(vec_done, VE.step())
                    else:
                        v.wait_ge(vec_done, VE.n - 3)
                        v.scalar_tensor_tensor(out=ca[:, b, :], in0=cv[:, b, w:w + T], scalar=tap,
                                               in1=ca[:, b, :], op0=ALU.mult, op1=ALU.add)\
                         .then_inc(vec_done, VE.step())
            VE.names[tag + "cc"] = VE.n
            v_wait(v)
            v.wait_ge(act_done, AC.at(tag + "ET"))
            for t in range(NT):
                v.wait_ge(pe_done, PE.at(tag + f"kk{t}"))
                v.tensor_tensor(mA_T[:, t, :], PS[4 + 2 * t][:, :], scr[:, 0, t * 512:(t + 1) * 512], ALU.mult)\
                 .then_inc(vec_done, VE.step())
                v.tensor_tensor(attn[:, t, :], PS[5 + 2 * t][:, :], scr[:, 0, t * 512:(t + 1) * 512], ALU.mult)\
                 .then_inc(vec_done, VE.step())
            v_wait(v)
            for t in range(NT):
                v.tensor_tensor(hh(mNT[:, t, :]), hh(mA_T[:, t, :]), over_heads(c("m8")), ALU.mult)\
                 .then_inc(vec_done, VE.step())
                v_wait(v)
                v.tensor_tensor(hh(mQ[:, t, :]), hh(mNT[:, t, :]), over_heads(ident), ALU.add)\
                 .then_inc(vec_done, VE.step(tag + f"Q{t}"))
            off = c("off").rearrange("p (l n) -> p l n", l=3)
            for t in range(NT):
                if t:
                    v.wait_ge(pe_done, PE.at(tag + f"UX2{t - 1}"))
                v.wait_ge(pe_done, PE.at(tag + f"N2{t}"))
                v.tensor_copy(mN2, PS[2][:, :]).then_inc(vec_done, VE.step())
                v.tensor_tensor(hh(mIN2), hh(PS[2][:, :]), over_heads(ident), ALU.add)\
                 .then_inc(vec_done, VE.step(tag + f"IN2{t}"))
                v.wait_ge(pe_done, PE.at(tag + f"N4{t}"))
                v.tensor_tensor(hh(mIN4[:, t, :]), hh(PS[0][:, :]), over_heads(ident), ALU.add)\
                 .then_inc(vec_done, VE.step(tag + f"IN4{t}"))
                v.wait_ge(pe_done, PE.at(tag + f"U{t}"))
                v.tensor_copy(mU[:, t, :], PS[2][:, :]).then_inc(vec_done, VE.step())
                v.wait_ge(act_done, AC.at(tag + f"A{t}"))
                for lev in range(3):
                    v.tensor_tensor(hh(mN2T[:, t, :]), hh(mA[:, t, :]), over_heads(off[:, lev, :]), ALU.mult)\
                     .then_inc(vec_done, VE.step(tag + f"U{lev}{t}"))
                    v.wait_ge(pe_done, PE.at(tag + f"T{lev}{t}"))
                    v.tensor_copy(mN2, PS[0][:, :]).then_inc(vec_done, VE.step(tag + f"T{lev}{t}"))
                    v.wait_ge(pe_done, PE.at(tag + f"UX{lev}{t}"))
                    v.tensor_tensor(mU[:, t, :], mU[:, t, :], PS[2][:, :], ALU.subtract)\
                     .then_inc(vec_done, VE.step(tag + f"U3{t}" if lev == 2 else None))
            for t in range(NT):
                v.wait_ge(pe_done, PE.at(tag + f"w{t}"))
                v.tensor_scalar(nw[:, :, t * P:(t + 1) * P], hh(PS[t][:, :]), -1.0, None, ALU.mult)\
                 .then_inc(vec_done, VE.step(tag + "w" if t else None))
            for cc in range(NCH):
                t, r = cc // 2, slice(CHUNK * (cc % 2), CHUNK * (cc % 2) + CHUNK)
                v.wait_ge(pe_done, PE.at(tag + f"vn{cc}"))
                v.tensor_copy(vn[r, t, :], PS[2 + 3 * (cc % 2)][r, :]).then_inc(vec_done, VE.step(tag + f"vn{cc}"))
                if cc < NCH - 1:
                    v.wait_ge(pe_done, PE.at(tag + f"dS{cc}"))
                    bank = PS[4] if cc % 2 == 0 else PS[7]
                    if cc == 0:
                        v.tensor_copy(S, bank[:, :]).then_inc(vec_done, VE.step(tag + "S0"))
                    else:
                        v_wait(v)
                        for h in range(4):
                            hc = slice(h * P, (h + 1) * P)
                            v.scalar_tensor_tensor(out=S[:, hc], in0=S[:, hc], scalar=egl[:, h, cc:cc + 1],
                                                   in1=bank[:, hc], op0=ALU.mult, op1=ALU.add)\
                             .then_inc(vec_done, VE.step(tag + f"S{cc}" if h == 3 else None))
            v.wait_ge(act_done, AC.at(tag + "o3"))
            v_headnorm(v, tag + "d", o_tm[:, :, :], p2("ong"), zt, dq, 0)
            v.wait_ge(pe_done, PE.at(tag + "cmu"))
            for b in range(4):
                v.scalar_tensor_tensor(out=ca[:, b, :], in0=PS[2][:, 0:T], scalar=-1.0 / 512, in1=ca[:, b, :],
                                       op0=ALU.mult, op1=ALU.add).then_inc(vec_done, VE.step())
            v_wait(v)
            v.tensor_tensor(scr[:, 0, :], caf, caf, ALU.mult).then_inc(vec_done, VE.step(tag + "csq"))
            v.wait_ge(act_done, AC.at(tag + "crs"))
            v.reciprocal(scr[:, 1, T:2 * T], scr[:, 1, 0:T]).then_inc(vec_done, VE.step())
            v_wait(v)
            v.tensor_tensor(ca[:, :, :], ca[:, :, :], scr[:, 1, T:2 * T].unsqueeze(1).to_broadcast([P, 4, T]),
                            ALU.mult).then_inc(vec_done, VE.step(tag + "cn"))
            v_residual(v, SLOTS_MIX2, ALPHA, tag + "x1")
            v_wait(v)
            v_ln(v, tag + "m", p2("lnmg"), p2("lnmb"), tag + "n2.x")
            v_transposed(v, tag + "n2", None)
            if last:
                v.memset(Y[:, :, :], 0.0).then_inc(vec_done, VE.step())
                v.wait_ge(pe_done, PE.at(tag + "route"))
                lg = small[:, 0:16]
                v.tensor_copy(lg, PS[0][:, 0:16]).then_inc(vec_done, VE.step())
                v_wait(v)
                for t in range(NT):
                    v.max(top[:, t, :], lg[:, t * 8:(t + 1) * 8]).then_inc(vec_done, VE.step())
                v_wait(v)
                for t in range(NT):
                    v.max_index(topi[:, t, :], top[:, t, :], lg[:, t * 8:(t + 1) * 8]).then_inc(vec_done, VE.step())
                v.tensor_tensor(small[:, 40:42], top[:, :, 1], top[:, :, 0], ALU.subtract)\
                 .then_inc(vec_done, VE.step(tag + "d21"))
                v_wait(v)
                v.tensor_copy(topf[:, :, :], topi[:, :, :]).then_inc(vec_done, VE.step())
                v.wait_ge(act_done, AC.at(tag + "e21"))
                v.tensor_scalar(small[:, 42:44], small[:, 40:42], 1.0, None, ALU.add).then_inc(vec_done, VE.step())
                v_wait(v)
                v.reciprocal(small[:, 44:46], small[:, 42:44]).then_inc(vec_done, VE.step())
                v_wait(v)
                v.tensor_tensor(small[:, 46:48], small[:, 40:42], small[:, 44:46], ALU.mult)\
                 .then_inc(vec_done, VE.step())
                v_wait(v)
                for t in range(NT):
                    v.tensor_scalar(comb[:, t, :], c("iota"), topf[:, t, 0:1], small[:, 44 + t:45 + t],
                                    ALU.is_equal, ALU.mult).then_inc(vec_done, VE.step())
                    v.tensor_scalar(comb2[:, t, :], c("iota"), topf[:, t, 1:2], small[:, 46 + t:47 + t],
                                    ALU.is_equal, ALU.mult).then_inc(vec_done, VE.step())
                v_wait(v)
                v.tensor_tensor(comb[:, :, :], comb[:, :, :], comb2[:, :, :], ALU.add).then_inc(vec_done, VE.step())

        comb2 = sb("comb2", [P, NT, NEXP])
        top = sb("top", [P, NT, 8])
        topf = sb("topf", [P, NT, 8])
        topi = sb("topi", [P, NT, 8], U32)

        def second_tensor(pe):
            eng = ("pe", pe, PE, pe_done)
            for_segment(eng, "mixA", 1, lambda it: mix_tensor(pe, "A", 0, False))

            def dense(it):
                rg.start("dense", it)
                t_ffn(pe, "fd", UNITS_DENSE, True)
            for_segment(eng, "dense", 1, dense)
            for_segment(eng, "mixB", 1, lambda it: mix_tensor(pe, "B", 1, True))

            def expert(it):
                rg.start("moe", it)
                t_ffn(pe, "fe", UNITS_EXP, True)
            for_segment(eng, "moe", NEXP, expert)

        def second_scalar(act):
            eng = ("act", act, AC, act_done)
            for_segment(eng, "mixA", 1, lambda it: mix_scalar(act, "A", 0, False))

            def dense(it):
                AC.names["fd.go"] = 0
                a_ffn(act, "fd", UNITS_DENSE, True, 0)
                a_ln(act, "fdn")
            for_segment(eng, "dense", 1, dense)
            for_segment(eng, "mixB", 1, lambda it: mix_scalar(act, "B", 1, True))

            def expert(it):
                AC.names["fe.go"] = 0
                a_ffn(act, "fe", UNITS_EXP, True, 0)
            for_segment(eng, "moe", NEXP, expert)
            a_ln(act, "fin")

        def second_vector(v):
            eng = ("vec", v, VE, vec_done)
            for_segment(eng, "mixA", 1, lambda it: mix_vector(v, "A", 0, False))

            def dense(it):
                VE.names["fd.go"] = 0
                v_ffn(v, "fd", UNITS_DENSE, True, 0)
                v_residual(v, SLOTS_DENSE, ALPHA, "xd")
                v_wait(v)
                v_ln(v, "fdn", p2("lnfg"), p2("lnfb"), "fdx")
            for_segment(eng, "dense", 1, dense)
            for_segment(eng, "mixB", 1, lambda it: mix_vector(v, "B", 1, True))

            def expert(it):
                VE.names["fe.go"] = 0
                e = it if isinstance(it, int) else it
                v.tensor_copy(ccol[:, :].unsqueeze(2), comb[:, :, bass.ds(e, 1)]).then_inc(vec_done, VE.step())
                v_ffn(v, "fe", UNITS_EXP, True, 0)
                v.wait_ge(slots_used, SLOTS_EXP)
                for t in range(NT):
                    for f in range(2):
                        cols = slice(f * 512, (f + 1) * 512)
                        v.scalar_tensor_tensor(out=Y[:, t, cols], in0=PS[4 + 2 * t + f][:, :],
                                               scalar=ccol[:, t:t + 1], in1=Y[:, t, cols], op0=ALU.mult,
                                               op1=ALU.add).then_inc(vec_done, VE.step())
            for_segment(eng, "moe", NEXP, expert)
            for t in range(NT):
                v.scalar_tensor_tensor(out=X[:, t, :], in0=X[:, t, :], scalar=ALPHA, in1=Y[:, t, :],
                                       op0=ALU.mult, op1=ALU.add).then_inc(vec_done, VE.step())
            v_wait(v)
            v_ln(v, "fin", p2("lnfg"), p2("lnfb"), "final")

        @block.tensor
        def _(pe):
            pe.wait_ge(con_loaded, 16)
            if RUN_FIRST:
                for_segment(("pe", pe, PE, pe_done), "l1", DEPTH, lambda it: l1_tensor(pe, it))
            if RUN_SECOND:
                second_tensor(pe)

        @block.scalar
        def _(act):
            act.wait_ge(consts_ready, 4)
            if RUN_FIRST:
                for_segment(("act", act, AC, act_done), "l1", DEPTH, lambda it: l1_scalar(act, it))
            if RUN_SECOND:
                second_scalar(act)

        @block.vector
        def _(v):
            v.memset(eps_rms[:, :], EPS).then_inc(consts_ready, 1)
            v.memset(eps_ln[:, :], LN_EPS).then_inc(consts_ready, 1)
            v.memset(reset[:, :], 1.0).then_inc(consts_ready, 1)
            v.wait_ge(consts_ready, 3)
            v.memset(reset[:, 0:4 * T:CHUNK], 0.0).then_inc(consts_ready, 1)
            v.wait_ge(consts_ready, 4)
            if RUN_FIRST:
                for_segment(("vec", v, VE, vec_done), "l1", DEPTH, lambda it: l1_vector(v, it))
            if RUN_SECOND:
                second_vector(v)


def _pack(cols, total, parts):
    import numpy as np
    out = np.zeros((128, total), np.float32)
    for name, a in parts.items():
        lo, hi = cols[name]
        assert a.shape[1] == hi - lo, (name, a.shape)
        out[:a.shape[0], lo:hi] = a
    return out


def _constants():
    import numpy as np
    i, j = np.arange(128)[:, None], np.arange(128)[None, :]
    keep = (i // CHUNK == j // CHUNK) & (j >= i)
    causal = np.where(j <= i, 0.0, NEG)
    sel = np.zeros((4, 4, 128), np.float32)
    selp = np.zeros((4, 2, 128), np.float32)
    for h in range(4):
        sel[h, h] = 1.0
        selp[h, h // 2, 64 * (h % 2):64 * (h % 2) + 64] = 1.0
    off = [((i // (2 * b) == j // (2 * b)) & (i % (2 * b) >= b) & (j % (2 * b) < b)) for b in (8, 16, 32)]
    inv = (1.0 / (np.float32(10000.0) ** (np.arange(0, HD, 2, dtype=np.float32) / np.float32(HD)))).astype(np.float32)
    ang = np.arange(T, dtype=np.float32)[:, None] * inv[None, :]
    tab = lambda a: a.reshape(NT, 128, 32).transpose(1, 0, 2).reshape(128, 64)
    return _pack(CON, NC, {
        "ident": np.eye(128), "ones": np.ones((128, 128)), "keep": keep, "neg": np.where(keep, 0.0, NEG),
        "moba": np.concatenate([causal, np.zeros((128, 128)), causal], 1),
        "m8": -1.0 * ((i // 8 == j // 8) & (j > i)), "off": np.concatenate(off, 1),
        "sel": sel.reshape(4, 512), "selp": selp.reshape(4, 256), "cos": tab(np.cos(ang)), "sin": tab(np.sin(ang)),
        "iota": np.broadcast_to(np.arange(8), (128, 8))})


def kernel(**inputs):
    import numpy as np
    import concourse.bacc as bacc
    from concourse.bass_utils import run_bass_kernel_spmd

    a = {k: np.asarray(v) for k, v in inputs.items()}

    def by_feature(v):
        return v.reshape(-1, 128).T

    def taps(w):
        return w.T.reshape(-1, 128, w.shape[0]).transpose(1, 0, 2).reshape(128, -1)

    def ktile(w):
        return w.reshape(-1, 128, w.shape[1]).transpose(1, 0, 2).reshape(128, -1)

    slots = []

    def by_columns(w, n):
        for c in range(0, w.shape[1], n):
            slots.append(ktile(w[:, c:c + n]))

    def by_rows(w):
        for r in range(0, w.shape[0], 256):
            slots.append(ktile(w[r:r + 256]))

    par1, par2 = [], []
    if RUN_FIRST:
        for l in range(DEPTH):
            w = a["w_in"][l]
            at = np.cumsum([0, 512, 512, 512, 512, 16, 512, 512, 512, 256, 256, 512, 512, 4, 4, 3072])
            g_q, g_k, g_v, g_g, g_a, m_q, m_k, m_v, l_q, l_k, l_v, l_o, l_i, l_f, br = (
                w[:, at[i]:at[i + 1]] for i in range(15))
            for y in (g_q, g_k, g_g, g_v, m_q, m_k, m_v, l_q, l_k, l_v, l_o, br):
                by_columns(y, 256)
            for name in ("w_br_gla", "w_br_moba", "w_br_mlstm"):
                by_columns(a[name][l], 512)
            by_rows(a["w_out"][l])
            ff2 = a["w_ff2"][l]
            for u in range(0, 4096 // 256 + 1):
                if u < 16:
                    by_columns(a["w_ff1"][l][:, u * 256:(u + 1) * 256], 256)
                if u > 0:
                    by_rows(ff2[(u - 1) * 256:u * 256])
            par1.append(_pack(PAR1, NP1, {
                "n1": by_feature(a["norm1_g"][l]), "n2": by_feature(a["norm2_g"][l]),
                "ab": by_feature(a["gla_a_b"][l]), "gn": by_feature(a["gla_norm_g"][l]),
                "mn": by_feature(a["mlstm_norm_g"][l]), "gateb": by_feature(a["gate_b"][l]),
                "convw": taps(a["mlstm_conv_w"][l]), "wga": ktile(g_a), "wli": ktile(l_i), "wlf": ktile(l_f),
                "qng": np.broadcast_to(a["moba_qn_g"][l], (128, HD)),
                "kng": np.broadcast_to(a["moba_kn_g"][l], (128, HD)),
                "aup": a["gla_a_up"][l], "ifb": np.stack([a["mlstm_i_b"][l], a["mlstm_f_b"][l]], 1)}))
    else:
        par1 = [np.zeros((128, NP1), np.float32)] * DEPTH
    if RUN_SECOND:
        for l in range(DEPTH):
            w = a["w_in_2"][l]
            by_columns(w[:, :3072], 256)
            by_rows(a["w_out_2"][l])
            if l % 2 == 0:
                ffns = [(a["ffn_w_gate_2"][0], a["ffn_w_up_2"][0], a["ffn_w_down_2"][0])]
            else:
                ffns = [(a["moe_w_gate_2"][0][e], a["moe_w_up_2"][0][e], a["moe_w_down_2"][0][e])
                        for e in range(NEXP)]
            for gate, up, down in ffns:
                units = gate.shape[1] // 256
                for u in range(units + 1):
                    if u < units:
                        by_columns(gate[:, u * 256:(u + 1) * 256], 256)
                        by_columns(up[:, u * 256:(u + 1) * 256], 256)
                    if u > 0:
                        by_rows(down[(u - 1) * 256:u * 256])
            wide = lambda v: np.broadcast_to(v, (128, D))
            parts = {
                "wb": ktile(w[:, 3072:3076]), "wa": ktile(w[:, 3076:3080]), "sconv": taps(a["short_conv_w_2"][l]),
                "dww": taps(a["conv_dw_w_2"][l]), "dwb": by_feature(a["conv_dw_b_2"][l]),
                "clng": by_feature(a["conv_ln_g_2"][l]), "clnb": by_feature(a["conv_ln_b_2"][l]),
                "ong": by_feature(a["out_norm_g_2"][l]),
                "gpar": np.stack([a["a_log_2"][l], a["dt_bias_2"][l]], 1),
                "lnmg": wide(a["ln_mix_g_2"][l]), "lnmb": wide(a["ln_mix_b_2"][l]),
                "lnfg": wide(a["ln_ffn_g_2"][l]), "lnfb": wide(a["ln_ffn_b_2"][l])}
            if l % 2:
                parts["router"] = ktile(a["router_w_2"][0])
            par2.append(_pack(PAR2, NP2, parts))
    else:
        par2 = [np.zeros((128, NP2), np.float32)] * DEPTH
    slots += [np.zeros((128, SLOT), np.float32)] * NSLOT
    arrays = {"x": a["x"][0], "stream": np.stack(slots), "par1": np.stack(par1), "par2": np.stack(par2),
              "con": _constants()}

    def program(known):
        nc = bacc.Bacc("TRN2", target_bir_lowering=False, num_devices=1)
        ins = [nc.dram_tensor("in_" + name, v.shape, F32, kind="ExternalInput").ap() for name, v in arrays.items()]
        y = nc.dram_tensor("out_y", (T, D), F32, kind="ExternalOutput").ap()
        build(nc, *ins, y, known)
        return nc, known

    _, known = program({})
    nc, _ = program({k: s.names for k, s in zip(("pe", "act", "vec"), known["now"])})
    r = run_bass_kernel_spmd(nc, [{"in_" + k: np.ascontiguousarray(v) for k, v in arrays.items()}], core_ids=[0])
    return r.results[0]["out_y"][None]
```

```python
from contextlib import ExitStack

import concourse.bass as bass
from concourse import mybir

F32 = mybir.dt.float32
F32R = mybir.dt.float32r
I32 = mybir.dt.int32
U32 = mybir.dt.uint32
ACT = mybir.ActivationFunctionType
ALU = mybir.AluOpType
AX = mybir.AxisListType

P = 128
T = 256
NT = T // P
D = 1024
KD = D // P
DEPTH = 2
CHUNK = 64
NCH = T // CHUNK
GLA_H = 4
LOWRANK = 16
GATE_NORM = 16.0
MOBA_H, HD = 8, 64
ML_H, ML_DK, ML_DV = 4, 64, 128
DFF1 = 4 * D
DFF_DENSE = 2816
NEXP = 8
DFF_EXP = 3584
CONV_WIN = 31
EPS = 1e-6
LN_EPS = 1e-5
ALPHA = (2 * DEPTH) ** 0.25
NEG = -1e30
CAP = 128
NPASS = NEXP + (2 * T) // (CAP + 1)

SLOT = 2048
NSLOT = 6
UNIT = 256
PROJ1 = 32
SLOTS_L1 = PROJ1 + 6 + 4 + 2 * (DFF1 // UNIT)
SLOTS_MIX2 = 12 + 4
UNITS_DENSE = DFF_DENSE // UNIT
UNITS_EXP = DFF_EXP // UNIT
SLOTS_DENSE = 3 * UNITS_DENSE
SLOTS_EXP = 3 * UNITS_EXP

RUN_FIRST = True
RUN_SECOND = True


def columns(spec):
    at, out = 0, {}
    for name, n in spec:
        out[name] = (at, at + n)
        at += n
    return out, at


PAR1, NP1 = columns([("n1", 8), ("n2", 8), ("ab", 4), ("gn", 1), ("mn", 1), ("gateb", 24), ("convw", 16),
                     ("wga", KD * LOWRANK), ("wli", KD * 4), ("wlf", KD * 4), ("qng", HD), ("kng", HD),
                     ("aup", 512), ("ifb", 2)])
PAR2, NP2 = columns([("wb", KD * 4), ("wa", KD * 4), ("sconv", 48), ("dww", 4 * CONV_WIN), ("dwb", 4),
                     ("clng", 4), ("clnb", 4), ("ong", 1), ("gpar", 2), ("router", KD * NEXP),
                     ("lnmg", D), ("lnmb", D), ("lnfg", D), ("lnfb", D)])
CON, NC = columns([("ident", P), ("ones", P), ("keep", P), ("neg", P), ("moba", 384), ("m8", P),
                   ("off", 3 * P), ("sel", 512), ("selp", 256), ("cos", 64), ("sin", 64), ("iota", P), ("before", P)])


class Steps:

    def __init__(self, known):
        self.n, self.names, self.known = 0, {}, known

    def step(self, name=None):
        self.n += 1
        if name is not None:
            assert name not in self.names, name
            self.names[name] = self.n
        return 1

    def at(self, name):
        return self.known.get(name, 1)

    def segment(self):
        self.n = 0


def build(nc, x_d, stream, par1_d, par2_d, con_d, out, known):
    ctx = ExitStack()
    with ctx:
        def sb(name, shape, dt=F32):
            return ctx.enter_context(nc.sbuf_tensor(name, shape, dt))

        def sem(name):
            return ctx.enter_context(nc.semaphore(name))

        with ExitStack() as shared:
            whi, wlo = (shared.enter_context(nc.sbuf_tensor(n, [P, 3, SLOT], F32R)) for n in ("whi", "wlo"))
            xhi, xlo = (shared.enter_context(nc.sbuf_tensor(n, [P, KD, T], F32R)) for n in ("xhi", "xlo"))
            hhi, hlo = (shared.enter_context(nc.sbuf_tensor(n, [P, 2, 2, T], F32R)) for n in ("hhi", "hlo"))
        big = sb("big", [P, 16896])
        attn = sb("attn", [P, NT, 512])
        keT = sb("keT", [P, NT, 512])
        o_tm = sb("o_tm", [P, NT, 512])
        ring = sb("ring", [P, NSLOT, SLOT])
        con = sb("con", [P, NC])
        par = sb("par", [P, max(NP1, NP2)])
        X = sb("X", [P, NT, D])
        xT = sb("xT", [P, KD, T])
        scr = sb("scr", [P, NT, D])
        eps_rms = sb("eps_rms", [P, 1])
        eps_ln = sb("eps_ln", [P, 1])
        reset = sb("reset", [P, 4 * T])
        table = sb("table", [1, NPASS + 2], I32)
        small = sb("small", [P, 512])
        PS = [ctx.enter_context(nc.psum_tensor(f"bank{i}", [P, 512], F32)) for i in range(8)]

        slot_landed = [sem(f"slot_landed{i}") for i in range(NSLOT)]
        slots_used = sem("slots_used")
        slots_split = sem("slots_split")
        pe_done = sem("pe_done")
        act_done = sem("act_done")
        vec_done = sem("vec_done")
        par_loaded = sem("par_loaded")
        con_loaded = sem("con_loaded")
        x_loaded = sem("x_loaded")
        out_stored = sem("out_stored")
        consts_ready = sem("consts_ready")
        pool_turns = sem("pool_turns")
        turns = sem("turns")
        arrived = sem("arrived")
        cleared = sem("cleared")
        block = ctx.enter_context(nc.Block())

        PE, AC, VE = (Steps(known.setdefault(k, {})) for k in ("pe", "act", "vec"))
        known["now"] = (PE, AC, VE)

        def c(name, rows=P):
            a, b = CON[name]
            return con[0:rows, a:b]

        def p1(name, rows=P):
            a, b = PAR1[name]
            return par[0:rows, a:b]

        def p2(name, rows=P):
            a, b = PAR2[name]
            return par[0:rows, a:b]

        ident = c("ident")

        def fm(at, blocks):
            return big[:, at:at + blocks * T].rearrange("p (b t) -> p b t", t=T)

        def tm(at, cols):
            return big[:, at:at + NT * cols].rearrange("p (t c) -> p t c", t=NT)

        segs = []
        if RUN_FIRST:
            segs.append(("l1", SLOTS_L1, DEPTH))
        if RUN_SECOND:
            segs += [("mixA", SLOTS_MIX2, 1), ("dense", SLOTS_DENSE, 1), ("mixB", SLOTS_MIX2, 1),
                     ("moe", SLOTS_EXP, NEXP), ("end", 0, 1)]
        else:
            segs += [("end", 0, 1)]
        first_slot, uses, seg_no = {}, {}, {}
        at, used, no = 0, [0] * NSLOT, 0
        for tag, n, loops in segs:
            first_slot[tag], uses[tag], seg_no[tag] = at, list(used), no
            per = [len(range(s, n, NSLOT)) for s in range(NSLOT)]
            used = [u + per[s] * loops for s, u in enumerate(used)]
            at += n * loops
            no += loops
        n_slots = dict((t, n) for t, n, _ in segs)
        total_slots = at

        def split_from(tag):
            return {"l1": PROJ1 + 10, "dense": 0}.get(tag, n_slots[tag])

        class Ring:

            def __init__(self):
                self.k = 0

            def start(self, tag, it):
                self.tag, self.it, self.k = tag, it, 0

            def take(self, pe):
                s = self.k % NSLOT
                per = len(range(s, n_slots[self.tag], NSLOT))
                pe.wait_ge(slot_landed[s], self.it * (16 * per) + 16 * (uses[self.tag][s] + self.k // NSLOT + 1))
                self.k += 1
                return ring[:, s, :]

        rg, rga, rgv = Ring(), Ring(), Ring()

        def for_segment(eng, tag, loops, body):
            def whole(it):
                body(it)
                if eng is not None and eng[0] != "pool":
                    e, steps, done = eng[1:]
                    if steps is not None and steps.n > 0:
                        e.wait_ge(done, steps.n)
                    if eng[0] == "pe" and split_from(tag):
                        e.wait_ge(slots_used, split_from(tag))
                    if eng[0] == "vec" and split_from(tag) < n_slots[tag]:
                        e.wait_ge(slots_split, n_slots[tag] - split_from(tag))
                    e.sem_inc(arrived, 1)
                    e.wait_ge(cleared, it + (seg_no[tag] + 1))
                    e.sem_inc(turns, 1)
                    if steps is not None:
                        steps.segment()
            e = eng[1]
            if loops == 1:
                whole(0)
            else:
                if tag == "moe":
                    loops = e.value_load(table[0:1, NPASS + 1:NPASS + 2], min_val=NEXP, max_val=NPASS)
                with e.Fori(0, loops) as it:
                    whole(it)

        @block.sync
        def _(sp):
            sp.dma_start(X[:, :, :], x_d.rearrange("(t p) n -> p t n", p=P)).then_inc(x_loaded, 16)
            sp.dma_start(con[:, :], con_d).then_inc(con_loaded, 16)
            for k in range(NSLOT):
                sp.dma_start(ring[:, k, :], stream[k]).then_inc(slot_landed[k], 16)

            def body(tag):
                n = n_slots[tag]

                def f(it):
                    if tag == "moe":
                        expert, following = (sp.value_load(table[0:1, bass.ds(it + q, 1)], min_val=0,
                                                           max_val=NEXP - 1) for q in range(2))
                    for k in range(NSLOT, n + NSLOT):
                        s = k % NSLOT if k < n else k - n
                        last = k - NSLOT if k < n else max(range(s, n, NSLOT))
                        if last >= split_from(tag):
                            sp.wait_ge(slots_split, last - split_from(tag) + 1)
                        else:
                            sp.wait_ge(slots_used, last + 1)
                        if isinstance(it, int):
                            src = stream[first_slot[tag] + k]
                        elif tag == "moe":
                            e = expert if k < n else following
                            src = stream[bass.ds(e * n + (first_slot[tag] + k % n), 1)]\
                                .rearrange("o p n -> p (o n)")
                        else:
                            src = stream[bass.ds(it * n + (first_slot[tag] + k), 1)].rearrange("o p n -> p (o n)")
                        sp.dma_start(ring[:, s, :], src).then_inc(slot_landed[s], 16)
                return f
            for tag, _, loops in segs[:-1]:
                for_segment(("sp", sp, None, None), tag, loops, body(tag))
            passes = sp.value_load(table[0:1, NPASS + 1:NPASS + 2], min_val=NEXP, max_val=NPASS) if RUN_SECOND else 0
            for s in range(NSLOT):
                per = len(range(s, SLOTS_EXP, NSLOT))
                before = uses["moe"][s] if RUN_SECOND else uses["end"][s]
                sp.wait_ge(slot_landed[s], passes * (16 * per) + 16 * (before + 1))
                sp.sem_inc(turns, 1)
            if RUN_SECOND:
                sp.wait_ge(vec_done, VE.at("final"))
            sp.dma_start(out.rearrange("(t p) n -> p t n", p=P), X[:, :, :]).then_inc(out_stored, 16)
            sp.wait_ge(out_stored, 16)

        def v_wait(v):
            v.wait_ge(vec_done, VE.n)

        def a_wait(act):
            act.wait_ge(act_done, AC.n)

        def v_rms(v, tag):
            ss = small[:, 0:NT]
            for t in range(NT):
                v.tensor_tensor(scr[:, t, :], X[:, t, :], X[:, t, :], ALU.mult).then_inc(vec_done, VE.step())
            v_wait(v)
            v.tensor_reduce(ss, scr[:, :, :], AX.X, ALU.add).then_inc(vec_done, VE.step(tag + ".ss"))
            act_sq = small[:, 2:2 + NT]
            v.wait_ge(act_done, AC.at(tag + ".root"))
            v.reciprocal(ss, act_sq).then_inc(vec_done, VE.step())
            v_wait(v)
            for t in range(NT):
                v.tensor_scalar(scr[:, t, :], X[:, t, :], ss[:, t:t + 1], None, ALU.mult)\
                 .then_inc(vec_done, VE.step(tag + f".hn{t}"))

        def a_rms(act, tag):
            act.wait_ge(vec_done, VE.at(tag + ".ss"))
            act.activation(small[:, 2:2 + NT], small[:, 0:NT], ACT.Sqrt, bias=eps_rms[:, 0:1], scale=1.0 / D)\
               .then_inc(act_done, AC.step(tag + ".root"))

        def t_transpose(pe, tag, src, waits):
            for w, n in waits:
                pe.wait_ge(w, n)
            for k in range(KD):
                for t in range(NT):
                    mm = pe.transpose(PS[k // 2][:, (k % 2) * T + t * P:(k % 2) * T + (t + 1) * P],
                                      src[:, t, k * P:(k + 1) * P], ident)
                if k % 2:
                    mm.then_inc(pe_done, PE.step(tag + f".tr{k // 2}"))

        def a_transposed(act, tag, gain):
            for j in (0, 2):
                act.wait_ge(pe_done, PE.at(tag + f".tr{j}"))
                for q in range(2):
                    k = 2 * j + q
                    act.activation(xT[:, k, :], PS[j][:, q * T:(q + 1) * T], ACT.Copy,
                                   scale=(1.0 if gain is None else gain[:, k:k + 1]))\
                       .then_inc(act_done, AC.step())
                    k = 2 * (j + 1) + q
            AC.names[tag + ".xT"] = AC.n

        def v_transposed(v, tag, gain):
            for j in (1, 3):
                v.wait_ge(pe_done, PE.at(tag + f".tr{j}"))
                for q in range(2):
                    k = 2 * j + q
                    if gain is None:
                        v.tensor_copy(xT[:, k, :], PS[j][:, q * T:(q + 1) * T]).then_inc(vec_done, VE.step())
                    else:
                        v.tensor_scalar(xT[:, k, :], PS[j][:, q * T:(q + 1) * T], gain[:, k:k + 1], None, ALU.mult)\
                         .then_inc(vec_done, VE.step())
            VE.names[tag + ".xT"] = VE.n

        def t_project(pe, tag, kinds):
            for n, kind in enumerate(kinds):
                w = rg.take(pe).rearrange("p (k n) -> p k n", n=UNIT)
                if n >= 4:
                    pe.wait_ge(*evac_of(tag, kinds, n - 4))
                elif n == 0:
                    pe.wait_ge(act_done, AC.at(tag + ".go"))
                    pe.wait_ge(vec_done, VE.at(tag + ".go"))
                bank = PS[4 + n % 4]
                for h in range(2):
                    for k in range(KD):
                        cols = slice(h * P, (h + 1) * P)
                        if kind == "fm":
                            mm = pe.matmul(bank[:, h * T:(h + 1) * T], w[:, k, cols], xT[:, k, :],
                                           start=(k == 0), stop=(k == KD - 1))
                        else:
                            mm = pe.matmul(bank[:, h * T:(h + 1) * T], xT[:, k, cols], w[:, k, :],
                                           start=(k == 0), stop=(k == KD - 1))
                mm.then_inc(slots_used, 1)

        def evac_of(tag, kinds, n):
            return (act_done, AC.at(tag + f".ev{n}")) if n % 2 == 0 else (vec_done, VE.at(tag + f".ev{n}"))

        def v_headnorm(v, tag, o, gain, gate, yT, t0):
            oh = o.rearrange("p t (h d) -> p (t h) d", d=P)
            sq = scr[:, :, :].rearrange("p t n -> p (t n)")[:, 0:1024].rearrange("p (g d) -> p g d", d=P)
            ss = small[:, 32:40]
            v.tensor_tensor(sq, oh, oh, ALU.mult).then_inc(vec_done, VE.step())
            v_wait(v)
            v.tensor_reduce(ss, sq, AX.X, ALU.add).then_inc(vec_done, VE.step(tag + ".hss"))
            v.wait_ge(act_done, AC.at(tag + ".hroot"))
            v.reciprocal(small[:, 48:56], small[:, 40:48]).then_inc(vec_done, VE.step())
            v_wait(v)
            v.tensor_tensor(oh, oh, small[:, 48:56].unsqueeze(2).to_broadcast([P, 8, P]), ALU.mult)\
             .then_inc(vec_done, VE.step(tag + ".hn"))
            yf = yT.rearrange("p b t -> p (b t)")
            gf = gate.rearrange("p b t -> p (b t)")
            for j in range(2):
                v.wait_ge(pe_done, PE.at(tag + f".htr{j}"))
                v.scalar_tensor_tensor(out=yf[:, j * 512:(j + 1) * 512], in0=PS[t0 + j][:, :], scalar=gain,
                                       in1=gf[:, j * 512:(j + 1) * 512], op0=ALU.mult, op1=ALU.mult)\
                 .then_inc(vec_done, VE.step(tag + f".y{j}"))

        def a_headnorm(act, tag):
            act.wait_ge(vec_done, VE.at(tag + ".hss"))
            act.activation(small[:, 40:48], small[:, 32:40], ACT.Sqrt, bias=eps_rms[:, 0:1], scale=1.0 / P)\
               .then_inc(act_done, AC.step(tag + ".hroot"))

        def t_headnorm(pe, tag, o, t0):
            pe.wait_ge(vec_done, VE.at(tag + ".hn"))
            for j in range(2):
                for q in range(2):
                    for t in range(NT):
                        h = 2 * j + q
                        mm = pe.transpose(PS[t0 + j][:, q * T + t * P:q * T + (t + 1) * P],
                                          o[:, t, h * P:(h + 1) * P], ident)
                mm.then_inc(pe_done, PE.step(tag + f".htr{j}"))

        def slot_index(u, units, gated):
            n = 2 if gated else 1
            up = (u + 1) * n + max(u - 1, 0) if u < units else None
            dn = min(u + 2, units) * n + u + 1
            return up, dn

        hid = [scr[:, 1, 0:512].rearrange("p (b t) -> p b t", t=T),
               scr[:, 1, 512:1024].rearrange("p (b t) -> p b t", t=T)]
        hidf = [scr[:, 1, 0:512], scr[:, 1, 512:1024]]
        silf = [scr[:, 0, 0:512], scr[:, 0, 512:1024]]

        def split_order(units, gated):
            last = {u: slot_index(u, units, gated)[0] - 1 for u in range(units)}
            return {last[u] + 2: u for u in last}, {last[u] + 3: u for u in last}

        def t_ffn3(pe, tag, units, gated):
            k = 0

            def products(out, pairs, start, stop):
                for n, (left, right) in enumerate(pairs):
                    mm = pe.matmul(out, left, right, start=start and n == 0, stop=stop and n == len(pairs) - 1)
                return mm

            def up(u):
                nonlocal k
                b = 2 * (u % 2)
                if u >= 2:
                    pe.wait_ge(vec_done, VE.at(tag + f".m{u - 2}"))
                for g in range(2 if gated else 1):
                    pe.wait_ge(slots_split, k + 1)
                    hi, lo_ = (w[:, k % 3, :].rearrange("p (k n) -> p k n", n=UNIT) for w in (whi, wlo))
                    for h in range(2):
                        cols = slice(h * P, (h + 1) * P)
                        for kk in range(KD):
                            mm = products(PS[b + g][:, h * T:(h + 1) * T],
                                          ((hi[:, kk, cols], xhi[:, kk, :]), (hi[:, kk, cols], xlo[:, kk, :]),
                                           (lo_[:, kk, cols], xhi[:, kk, :])), kk == 0, kk == KD - 1)
                    mm.then_inc(pe_done, PE.step(tag + f".p{k}"))
                    k += 1

            def down(u):
                nonlocal k
                pe.wait_ge(slots_split, k + 1)
                pe.wait_ge(vec_done, VE.at(tag + f".hl{u}"))
                hi, lo_ = (w[:, k % 3, :].rearrange("p (k n) -> p k n", n=D) for w in (whi, wlo))
                for kk in range(2):
                    for t in range(NT):
                        tok = slice(t * P, (t + 1) * P)
                        for f in range(2):
                            cols = slice(f * 512, (f + 1) * 512)
                            mm = products(PS[4 + 2 * t + f][:, :],
                                          ((hhi[:, u % 2, kk, tok], hi[:, kk, cols]),
                                           (hhi[:, u % 2, kk, tok], lo_[:, kk, cols]),
                                           (hlo[:, u % 2, kk, tok], hi[:, kk, cols])),
                                          u == 0 and kk == 0, u == units - 1 and kk == 1)
                mm.then_inc(pe_done, PE.step(tag + f".p{k}"))
                k += 1

            pe.wait_ge(vec_done, VE.at(tag + ".x3"))
            for u in range(units + 1):
                if u < units:
                    up(u)
                if u > 0:
                    down(u - 1)
            PE.names[tag + ".end"] = PE.n

        def a_split(act, tag, k, rg_):
            src = rg_.take(act)
            if k >= 3:
                act.wait_ge(pe_done, PE.at(tag + f".p{k - 3}"))
            act.activation(whi[:, k % 3, :], src, ACT.Copy).then_inc(act_done, AC.step(tag + f".w{k}"))

        def v_split(v, tag, k, rg_):
            src = rg_.take(v)
            v.wait_ge(act_done, AC.at(tag + f".w{k}"))
            v.tensor_tensor(wlo[:, k % 3, :], src, whi[:, k % 3, :].bitcast(F32), ALU.subtract)\
             .then_inc(slots_split, 1)

        def a_splitx(act, tag):
            for j in range(4):
                act.activation(xhi[:, 2 * j:2 * j + 2, :], xT[:, 2 * j:2 * j + 2, :], ACT.Copy)\
                   .then_inc(act_done, AC.step(tag + f".x{j}"))

        def v_splitx(v, tag):
            for j in range(4):
                v.wait_ge(act_done, AC.at(tag + f".x{j}"))
                v.tensor_tensor(xlo[:, 2 * j:2 * j + 2, :], xT[:, 2 * j:2 * j + 2, :],
                                xhi[:, 2 * j:2 * j + 2, :].bitcast(F32), ALU.subtract)\
                 .then_inc(vec_done, VE.step(tag + f".x{j}"))

        def dn_slot(u, units, gated):
            return slot_index(u, units, gated)[1] - 1

        def a_ffn3(act, tag, units, gated, rg_, first):
            after, later = split_order(units, gated)
            n = (3 if gated else 2) * units
            for k in range(first, n + 3):
                if k < n:
                    a_split(act, tag, k, rg_)
                if k in after:
                    u = after[k]
                    act.wait_ge(pe_done, PE.at(tag + f".p{slot_index(u, units, gated)[0] - 1}"))
                    if u >= 2:
                        act.wait_ge(vec_done, VE.at(tag + f".m{u - 2}"))
                    act.activation(silf[u % 2], PS[2 * (u % 2)][:, :], ACT.Silu if gated else ACT.Relu)\
                       .then_inc(act_done, AC.step(tag + f".s{u}"))
                if k in later:
                    u = later[k]
                    act.wait_ge(vec_done, VE.at(tag + f".m{u}"))
                    if u >= 2:
                        act.wait_ge(pe_done, PE.at(tag + f".p{dn_slot(u - 2, units, gated)}"))
                    act.activation(hhi[:, u % 2, :, :], hid[u % 2], ACT.Copy)\
                       .then_inc(act_done, AC.step(tag + f".hh{u}"))

        def v_ffn3(v, tag, units, gated, rg_, first):
            after, later = split_order(units, gated)
            n = (3 if gated else 2) * units
            for k in range(first, n + 3):
                if k < n:
                    v_split(v, tag, k, rg_)
                if k in after:
                    u = after[k]
                    v.wait_ge(act_done, AC.at(tag + f".s{u}"))
                    if u >= 2:
                        v.wait_ge(vec_done, VE.at(tag + f".hl{u - 2}"))
                    v.tensor_tensor(hidf[u % 2], silf[u % 2], PS[2 * (u % 2) + 1][:, :] if gated else silf[u % 2],
                                    ALU.mult).then_inc(vec_done, VE.step(tag + f".m{u}"))
                if k in later:
                    u = later[k]
                    v.wait_ge(act_done, AC.at(tag + f".hh{u}"))
                    v.tensor_tensor(hlo[:, u % 2, :, :], hid[u % 2], hhi[:, u % 2, :, :].bitcast(F32), ALU.subtract)\
                     .then_inc(vec_done, VE.step(tag + f".hl{u}"))

        def t_out(pe, tag, srcs):
            for s in range(4):
                w = rg.take(pe).rearrange("p (k n) -> p k n", n=D)
                for kk in range(2):
                    k = 2 * s + kk
                    for t in range(NT):
                        for f in range(2):
                            mm = pe.matmul(PS[4 + 2 * t + f][:, :], srcs(k)[:, t * P:(t + 1) * P],
                                           w[:, kk, f * 512:(f + 1) * 512], start=(k == 0), stop=(k == KD - 1))
                mm.then_inc(slots_used, 1)

        def v_residual(v, slots, alpha, name):
            if isinstance(slots, str):
                v.wait_ge(pe_done, PE.at(slots))
            else:
                v.wait_ge(slots_used, slots)
            for t in range(NT):
                for f in range(2):
                    cols = slice(f * 512, (f + 1) * 512)
                    v.scalar_tensor_tensor(out=X[:, t, cols], in0=X[:, t, cols], scalar=alpha,
                                           in1=PS[4 + 2 * t + f][:, :], op0=ALU.mult, op1=ALU.add)\
                     .then_inc(vec_done, VE.step())
            VE.names[name] = VE.n

        GQ, GK, GG, LO, LQK = 0, 1024, 2048, 3072, 4096
        GV, MQ, MK, MV, LV = 5136, 6160, 7184, 8208, 9232
        GATES = 10272
        W3 = T + 3
        gq, gk, gg, lo = fm(GQ, 4), fm(GK, 4), fm(GG, 4), fm(LO, 4)
        lqk = big[:, LQK:LQK + 4 * W3].rearrange("p (b t) -> p b t", t=W3)
        gv, mq, mk, mv = tm(GV, 512), tm(MQ, 512), tm(MK, 512), tm(MV, 512)
        lv = big[:, LV:LV + 2 * 4 * 129].rearrange("p (t h d) -> p t h d", t=NT, h=4)
        gates = fm(GATES, 24)
        KINDS1 = ["fm"] * 2 + ["fm"] * 2 + ["fm"] * 2 + ["tm"] * 2 + ["tm"] * 6 + ["fm"] * 2 + ["tm"] * 2 \
            + ["fm"] * 2 + ["fm"] * 12
        NAMES1 = ["gq", "gq", "gk", "gk", "gg", "gg", "gv", "gv", "mq", "mq", "mk", "mk", "mv", "mv",
                  "lqk", "lqk", "lv", "lv", "lo", "lo"] + ["gate"] * 12

        def evac_tile(n):
            name, h = NAMES1[n], n % 2
            if name in ("gq", "gk", "gg", "lo"):
                return {"gq": gq, "gk": gk, "gg": gg, "lo": lo}[name][:, 2 * h:2 * h + 2, :]
            if name == "lqk":
                return lqk[:, 2 * h:2 * h + 2, 3:W3]
            if name in ("gv", "mq", "mk", "mv"):
                return {"gv": gv, "mq": mq, "mk": mk, "mv": mv}[name][:, :, h * T:(h + 1) * T]
            if name == "lv":
                return lv[:, :, 2 * h:2 * h + 2, 0:128]

        def bank_view(n):
            b = PS[4 + n % 4][:, :]
            if NAMES1[n] == "lv":
                return b.rearrange("p (t h d) -> p t h d", t=2, h=2)
            return b.rearrange("p (a b) -> p a b", a=2)

        yg = fm(GQ, 4)
        ym = fm(MQ, 4)
        yl = fm(LQK, 4)
        BC = scr[:, 0, :]
        TMP = scr[:, 1, :]
        sg = sb("sg", [P, 3, 512])
        smb = sb("smb", [4, 2048])
        rows = [smb[:, i * T:(i + 1) * T] for i in range(8)]
        st = sb("st", [P, 3, 2, 129])
        keep_i = c("keep").bitcast(I32)
        PHASE = []

        def t_gate(pe, i):
            w = rg.take(pe).rearrange("p (k n) -> p k n", n=UNIT)
            if i >= 2:
                pe.wait_ge(act_done, AC.at(f"gate{i - 2}"))
                pe.wait_ge(vec_done, VE.at("g.o"))
            for h in range(2):
                for k in range(KD):
                    mm = pe.matmul(PS[6 + i % 2][:, h * T:(h + 1) * T], w[:, k, h * P:(h + 1) * P], xT[:, k, :],
                                   start=(k == 0), stop=(k == KD - 1))
            mm.then_inc(slots_used, 1)

        def a_gate(act, i):
            act.wait_ge(slots_used, 20 + i + 1)
            for q in range(2):
                b = 2 * i + q
                act.activation(gates[:, b, :], PS[6 + i % 2][:, q * T:(q + 1) * T], ACT.Identity,
                               bias=p1("gateb")[:, b:b + 1]).then_inc(act_done, AC.step(f"gate{i}" if q else None))

        def l1_tensor(pe, it):
            rg.start("l1", it)
            t_transpose(pe, "n1", scr, [(vec_done, VE.at("n1.hn1"))])
            pe.wait_ge(act_done, AC.at("n1.xT"))
            pe.wait_ge(vec_done, VE.at("n1.xT"))
            t_project(pe, "pj", KINDS1[:20])
            w = p1("wga").rearrange("p (k n) -> p k n", n=LOWRANK)
            for k in range(KD):
                mm = pe.matmul(PS[0][0:LOWRANK, 0:T], w[:, k, :], xT[:, k, :], start=(k == 0), stop=(k == KD - 1))
            mm.then_inc(pe_done, PE.step("ga"))
            for n, name in enumerate(("wli", "wlf")):
                w = p1(name).rearrange("p (k n) -> p k n", n=4)
                for k in range(KD):
                    mm = pe.matmul(PS[1][0:4, n * T:(n + 1) * T], w[:, k, :], xT[:, k, :],
                                   start=(k == 0), stop=(k == KD - 1))
            mm.then_inc(pe_done, PE.step("lif"))
            pe.wait_ge(act_done, AC.at("gaT"))
            aup = p1("aup", LOWRANK)
            for h in range(4):
                mm = pe.matmul(PS[2 + h // 2][:, (h % 2) * T:(h % 2 + 1) * T], aup[:, h * P:(h + 1) * P],
                               small[0:LOWRANK, 256:512], start=True, stop=True)
            mm.then_inc(pe_done, PE.step("z"))
            pe.wait_ge(act_done, AC.at("pj.ev18"))
            pe.wait_ge(vec_done, VE.at("pj.ev19"))
            for i in range(2):
                t_gate(pe, i)
            pe.wait_ge(vec_done, VE.at("g.kend"))
            for t in range(NT):
                for h in range(4):
                    mm = pe.matmul(PS[4 + t][:, h * P:(h + 1) * P], gk[:, h, t * P:(t + 1) * P],
                                   gq[:, h, t * P:(t + 1) * P], start=True, stop=True)
                mm.then_inc(pe_done, PE.step(f"g.s{t}"))
            pe.wait_ge(act_done, AC.at("gate1"))
            for t in range(NT):
                for h in range(4):
                    mm = pe.transpose(PS[6 + t][:, h * P:(h + 1) * P],
                                      BC[:, h * T + t * P:h * T + (t + 1) * P], ident)
                mm.then_inc(pe_done, PE.step(f"g.ke{t}"))
            pe.wait_ge(act_done, AC.at("g.keT1"))
            for cc in range(3):
                t, r = cc // 2, slice(CHUNK * (cc % 2), CHUNK * (cc % 2) + CHUNK)
                for h in range(4):
                    mm = pe.matmul(PS[cc][:, h * P:(h + 1) * P], keT[r, t, h * P:(h + 1) * P],
                                   gv[r, t, h * P:(h + 1) * P], start=True, stop=True)
                mm.then_inc(pe_done, PE.step(f"g.kv{cc}"))
            pe.wait_ge(vec_done, VE.at("g.S"))
            for t in range(NT):
                for h in range(4):
                    pe.matmul(PS[6 + t][:, h * P:(h + 1) * P], attn[:, t, h * P:(h + 1) * P],
                              gv[:, t, h * P:(h + 1) * P], start=True, stop=False, skip_group_check=True)
                    for cc in (2 * t, 2 * t + 1):
                        if cc == 0:
                            continue
                        r = CHUNK * (cc % 2)
                        mm = pe.matmul(PS[6 + t][r:r + CHUNK, h * P:(h + 1) * P],
                                       gq[:, h, cc * CHUNK:(cc + 1) * CHUNK], sg[:, cc - 1, h * P:(h + 1) * P],
                                       start=False, stop=True, skip_group_check=True)
                mm.then_inc(pe_done, PE.step(f"g.o{t}"))
            t_headnorm(pe, "g", o_tm, 0)
            for i in range(2, 5):
                t_gate(pe, i)
            pe.wait_ge(vec_done, VE.at("m.rope"))
            for n, src in enumerate((mq, mk)):
                for t in range(NT):
                    for q in range(4):
                        mm = pe.transpose(PS[2 + 2 * n + t][:, q * P:(q + 1) * P], src[:, t, q * P:(q + 1) * P], ident)
                mm.then_inc(pe_done, PE.step(f"m.tr{n}"))
            pe.wait_ge(vec_done, VE.at("m.kT"))
            pe.wait_ge(act_done, AC.at("m.qT"))
            for i in range(MOBA_H + 2):
                if i < MOBA_H:
                    h, r = i, slice(HD * (i % 2), HD * (i % 2) + HD)
                    if h >= 2:
                        pe.wait_ge(vec_done, VE.at(f"m.s{h - 2}"))
                    bank = PS[h % 2]
                    pe.matmul(bank[:, 0:P], mqT[r, h // 2, 0:P], mkT[r, h // 2, 0:P], start=True, stop=True)
                    pe.matmul(bank[:, P:384], mqT[r, h // 2, P:T], mkT[r, h // 2, 0:T], start=True, stop=True)\
                      .then_inc(pe_done, PE.step(f"m.qk{h}"))
                if 1 <= i <= MOBA_H:
                    h = i - 1
                    pe.wait_ge(vec_done, VE.at(f"m.p{h}"))
                    if h >= 2:
                        pe.wait_ge(act_done, AC.at(f"m.pT{h - 2}"))
                    for n in range(3):
                        mm = pe.transpose(PS[2 + h % 2][:, n * P:(n + 1) * P], prob(h)[:, n * P:(n + 1) * P], ident)
                    mm.then_inc(pe_done, PE.step(f"m.ptr{h}"))
                if i >= 2:
                    h = i - 2
                    r = slice(HD * (h % 2), HD * (h % 2) + HD)
                    pe.wait_ge(act_done, AC.at(f"m.pT{h}"))
                    bank = PS[4 + h // 4][r, ((h // 2) % 2) * T:((h // 2) % 2 + 1) * T]
                    pe.matmul(bank, mv[:, 0, h * HD:(h + 1) * HD], probT(h)[:, 0:T],
                              start=True, stop=False, skip_group_check=True)
                    pe.matmul(bank[:, P:T], mv[:, 1, h * HD:(h + 1) * HD], probT(h)[:, T:384],
                              start=False, stop=True, skip_group_check=True)\
                      .then_inc(pe_done, PE.step(f"m.pv{h}"))
                if i < 7:
                    t_gate(pe, 5 + i)
            pe.wait_ge(vec_done, VE.at("l.rows"))
            pe.wait_ge(act_done, AC.at("l.rows"))
            pe.wait_ge(act_done, AC.at("gate11"))
            pe.wait_ge(act_done, AC.at("m.y"))
            for n, row in enumerate((rows[1], rows[4], rows[5])):
                for t in range(NT):
                    mm = pe.transpose(PS[0][:, (n * NT + t) * 4:(n * NT + t) * 4 + 4], row[:, t * P:(t + 1) * P],
                                      ident[0:4, 0:4])
            mm.then_inc(pe_done, PE.step("l.cols"))
            sel = c("sel", 4).rearrange("p (h n) -> p h n", n=P)
            selp = c("selp", 4).rearrange("p (h n) -> p h n", n=P)
            for h in range(4):
                mm = pe.matmul(PS[1 + h // 2][:, (h % 2) * T:(h % 2 + 1) * T], sel[:, h, :], rows[3],
                               start=True, stop=True)
            mm.then_inc(pe_done, PE.step("l.negM"))
            for q in range(2):
                mm = pe.matmul(PS[3][:, q * T:(q + 1) * T], selp[:, q, :], rows[6], start=True, stop=True)
            mm.then_inc(pe_done, PE.step("l.iw"))
            pe.wait_ge(vec_done, VE.at("l.negMread"))
            for q in range(2):
                mm = pe.matmul(PS[1][:, q * 4:q * 4 + 4], selp[:, q, :], rows[7][:, 0:4], start=True, stop=True)
            mm.then_inc(pe_done, PE.step("l.a"))
            pe.wait_ge(vec_done, VE.at("l.qkc"))
            for odd in range(2):
                r = slice(ML_DK * odd, ML_DK * odd + ML_DK)
                for t in range(NT):
                    for q in range(2):
                        mm = pe.matmul(PS[4 + odd][:, (2 * t + q) * P:(2 * t + q + 1) * P],
                                       lc[r, 2 + q, t * P:(t + 1) * P], lc[r, q, t * P:(t + 1) * P],
                                       start=True, stop=True)
                mm.then_inc(pe_done, PE.step(f"l.s{odd}"))
            for t in range(NT):
                for q in range(2):
                    mm = pe.transpose(PS[6][:, (t * 2 + q) * P:(t * 2 + q + 1) * P], lc[:, 2 + q, t * P:(t + 1) * P],
                                      ident)
            mm.then_inc(pe_done, PE.step("l.ktr"))
            pe.wait_ge(vec_done, VE.at("l.kw"))
            pe.wait_ge(vec_done, VE.at("l.qi"))
            pe.wait_ge(vec_done, VE.at("l.acol"))
            for cc in range(3):
                t, r = cc // 2, slice(CHUNK * (cc % 2), CHUNK * (cc % 2) + CHUNK)
                for h in range(4):
                    q = h // 2
                    mm = pe.matmul(PS[1 + cc][ML_DK * (h % 2):ML_DK * (h % 2) + ML_DK, q * 129:(q + 1) * 129],
                                   kw[r, t, h * ML_DK:(h + 1) * ML_DK], lv[r, t, h, :], start=True, stop=True,
                                   skip_group_check=True)
                mm.then_inc(pe_done, PE.step(f"l.kv{cc}"))
            pe.wait_ge(vec_done, VE.at("l.st"))
            pe.wait_ge(vec_done, VE.at("l.sm1"))
            for t in range(NT):
                for h in (0, 2, 1, 3):
                    bank = PS[4 + 2 * t + h % 2][:, (h // 2) * 129:(h // 2 + 1) * 129]
                    pe.matmul(bank, attn[:, t, h * P:(h + 1) * P], lv[:, t, h, :], start=True, stop=False,
                              skip_group_check=True)
                    rr = slice(ML_DK * (h % 2), ML_DK * (h % 2) + ML_DK)
                    for cc in (2 * t, 2 * t + 1):
                        if cc == 0:
                            continue
                        r = CHUNK * (cc % 2)
                        mm = pe.matmul(bank[r:r + CHUNK, :], lc[rr, h // 2, cc * CHUNK:(cc + 1) * CHUNK],
                                       st[rr, cc - 1, h // 2, :], start=False, stop=True, skip_group_check=True)
                    if h // 2:
                        mm.then_inc(pe_done, PE.step(f"l.o{t}{h % 2}"))
            t_headnorm(pe, "l", o_tm, 0)
            pe.wait_ge(vec_done, VE.at("l.y1"))
            n = 0
            for b, y in enumerate((yg, ym, yl)):
                for s in range(2):
                    w = rg.take(pe).rearrange("p (k n) -> p k n", n=512)
                    for q in range(2):
                        if n >= 4:
                            pe.wait_ge(vec_done, VE.at(f"br.g{n - 4}"))
                        for f in range(2):
                            for k in range(4):
                                cb = slice((2 * q + f) * P, (2 * q + f + 1) * P)
                                mm = pe.matmul(PS[2 + n % 4][:, f * T:(f + 1) * T], w[:, k, cb], y[:, k, :],
                                               start=(k == 0), stop=(k == 3))
                        if q == 0:
                            mm.then_inc(pe_done, PE.step(f"br.{n}"))
                        n += 1
                    mm.then_inc(slots_used, 1)
            pe.wait_ge(vec_done, VE.at("br.mix"))
            t_out(pe, "wo", lambda k: gates[:, k, :])
            t_transpose(pe, "n2", scr, [(vec_done, VE.at("n2.hn1"))])
            pe.wait_ge(act_done, AC.at("n2.xT"))
            pe.wait_ge(vec_done, VE.at("n2.xT"))
            t_ffn3(pe, "f1", DFF1 // UNIT, False)

        mqT = sg[:, 0:2, :].rearrange("p a b -> p (a b)").rearrange("p (b t) -> p b t", t=T)
        mkT = keT[:, :, :].rearrange("p a b -> p (a b)").rearrange("p (b t) -> p b t", t=T)
        pr = big[:, GG:GG + 768].rearrange("p (n c) -> p n c", n=2)
        prT = big[:, GV:GV + 768].rearrange("p (n c) -> p n c", n=2)
        lc = fm(GK, 4)
        kw = keT[:, :, 0:256]
        ex = scr[:, 0, :]

        def prob(h):
            return pr[:, h % 2, :]

        def probT(h):
            return prT[:, h % 2, :]

        def a_sp(act, z, out_ap, name):
            act.activation(out_ap, z, ACT.Abs).then_inc(act_done, AC.step())
            a_wait(act)
            act.activation(out_ap, out_ap, ACT.Exp, scale=-1.0).then_inc(act_done, AC.step())
            a_wait(act)
            act.activation(out_ap, out_ap, ACT.Ln, bias=1.0).then_inc(act_done, AC.step(name))

        def l1_scalar(act, it):
            act.dma_start(par[:, 0:NP1], par1_d[bass.ds(it, 1)].rearrange("o p n -> p (o n)")
                          if not isinstance(it, int) else par1_d[it]).then_inc(par_loaded, 16)
            act.wait_ge(x_loaded, 16)
            a_rms(act, "n1")
            act.wait_ge(par_loaded, it * 16 + 16)
            a_transposed(act, "n1", p1("n1"))
            AC.names["pj.go"] = AC.n
            act.wait_ge(vec_done, VE.at("l.pad"))
            for n in range(0, 20, 2):
                act.wait_ge(slots_used, n + 1)
                func = {"gg": ACT.Silu, "lo": ACT.Sigmoid}.get(NAMES1[n], ACT.Copy)
                act.activation(evac_tile(n), bank_view(n), func).then_inc(act_done, AC.step(f"pj.ev{n}"))
            act.wait_ge(vec_done, VE.at("pj.ev19"))
            act.activation(lo[:, 2:4, :], lo[:, 2:4, :], ACT.Sigmoid).then_inc(act_done, AC.step("los"))
            act.activation(gg[:, 2:4, :], gg[:, 2:4, :], ACT.Silu).then_inc(act_done, AC.step("ggs"))
            act.wait_ge(pe_done, PE.at("ga"))
            act.activation(small[0:LOWRANK, 256:512], PS[0][0:LOWRANK, 0:T], ACT.Copy)\
               .then_inc(act_done, AC.step("gaT"))
            act.wait_ge(vec_done, VE.at("g.z"))
            a_sp(act, BC, TMP, "g.sp")
            act.wait_ge(vec_done, VE.at("g.B"))
            act.activation(E1, BC, ACT.Exp, scale=1.0 / GATE_NORM).then_inc(act_done, AC.step("g.eb"))
            act.activation(E2, BC, ACT.Exp, scale=-1.0 / GATE_NORM).then_inc(act_done, AC.step("g.en"))
            act.wait_ge(vec_done, VE.at("g.diff"))
            act.activation(TMP, TMP, ACT.Exp, scale=1.0 / GATE_NORM).then_inc(act_done, AC.step("g.ek"))
            for i in range(2):
                a_gate(act, i)
            for t in range(NT):
                act.wait_ge(pe_done, PE.at(f"g.ke{t}"))
                act.activation(keT[:, t, :], PS[6 + t][:, :], ACT.Copy).then_inc(act_done, AC.step(f"g.keT{t}"))
            a_headnorm(act, "g")
            act.wait_ge(vec_done, VE.at("m.ss"))
            act.activation(small[:, 80:112], small[:, 80:112], ACT.Sqrt, bias=eps_rms[:, 0:1], scale=1.0 / HD)\
               .then_inc(act_done, AC.step("m.root"))
            for i in range(2, 5):
                a_gate(act, i)
            act.wait_ge(pe_done, PE.at("m.tr0"))
            for t in range(NT):
                act.activation(mqT[:, :, t * P:(t + 1) * P], PS[2 + t][:, :].rearrange("p (q n) -> p q n", n=P),
                               ACT.Copy).then_inc(act_done, AC.step("m.qT" if t else None))
            for i in range(MOBA_H + 1):
                if i < MOBA_H:
                    h = i
                    act.wait_ge(vec_done, VE.at(f"m.mx{h}"))
                    nb = small[:, 112 + 2 * h:114 + 2 * h]
                    for n, cols in enumerate((slice(0, P), slice(P, 384))):
                        act.activation(prob(h)[:, cols], prob(h)[:, cols], ACT.Exp, bias=nb[:, n:n + 1],
                                       scale=HD ** -0.5, accum_out=small[:, 128 + 2 * h + n:129 + 2 * h + n])\
                           .then_inc(act_done, AC.step(f"m.e{h}" if n else None))
                if i >= 1:
                    h = i - 1
                    act.wait_ge(pe_done, PE.at(f"m.ptr{h}"))
                    if h >= 2:
                        act.wait_ge(pe_done, PE.at(f"m.pv{h - 2}"))
                    act.activation(probT(h), PS[2 + h % 2][:, 0:384], ACT.Copy)\
                       .then_inc(act_done, AC.step(f"m.pT{h}"))
                    if h < 7:
                        a_gate(act, 5 + h)
            act.wait_ge(pe_done, PE.at("m.pv7"))
            for j in range(2):
                act.activation(ym[:, 2 * j:2 * j + 2, :], PS[4 + j][:, :].rearrange("p (b t) -> p b t", t=T),
                               ACT.Copy).then_inc(act_done, AC.step("m.y" if j else None))
            act.wait_ge(vec_done, VE.at("l.z"))
            a_sp(act, rows[2], rows[3], "l.sp")
            act.wait_ge(vec_done, VE.at("l.args"))
            act.activation(rows[4], rows[4], ACT.Exp).then_inc(act_done, AC.step())
            act.activation(rows[5], rows[5], ACT.Exp).then_inc(act_done, AC.step())
            act.activation(rows[6], rows[6], ACT.Exp).then_inc(act_done, AC.step())
            act.activation(rows[7][:, 0:4], rows[7][:, 0:4], ACT.Exp).then_inc(act_done, AC.step("l.rows"))
            act.wait_ge(vec_done, VE.at("l.ex"))
            act.activation(ex, ex, ACT.Exp).then_inc(act_done, AC.step("l.exp"))
            act.activation(gates[:, :, :], gates[:, :, :], ACT.Sigmoid).then_inc(act_done, AC.step("gates"))
            for t in range(NT):
                for q in range(2):
                    act.wait_ge(pe_done, PE.at(f"l.o{t}{q}"))
                    act.activation(oa[:, t, q:4:2, :],
                                   PS[4 + 2 * t + q][:, 0:258].rearrange("p (h d) -> p h d", d=129),
                                   ACT.Copy).then_inc(act_done, AC.step("l.oa" if t and q else None))
            a_headnorm(act, "l")
            act.wait_ge(vec_done, VE.at("br.mix"))
            rga.start("l1", it)
            rga.k = split_from("l1")
            for k in range(2):
                a_split(act, "f1", k, rga)
            a_rms(act, "n2")
            a_transposed(act, "n2", p1("n2"))
            a_wait(act)
            act.wait_ge(vec_done, VE.at("n2.xT"))
            a_splitx(act, "f1")
            a_ffn3(act, "f1", DFF1 // UNIT, False, rga, 2)

        E1 = attn[:, :, :].rearrange("p a b -> p (a b)")
        E2 = o_tm[:, :, :].rearrange("p a b -> p (a b)")
        oa = big[:, MK:MK + 2 * 4 * 129].rearrange("p (t h d) -> p t h d", t=NT, h=4)

        def l1_vector(v, it):
            v.wait_ge(x_loaded, 16)
            v.wait_ge(con_loaded, 16)
            v_rms(v, "n1")
            v.wait_ge(par_loaded, it * 16 + 16)
            v.memset(lqk[:, :, 0:3], 0.0).then_inc(vec_done, VE.step())
            v.memset(lv[:, :, :, 128:129], 1.0).then_inc(vec_done, VE.step("l.pad"))
            v_transposed(v, "n1", p1("n1"))
            VE.names["pj.go"] = VE.n
            for n in range(1, 20, 2):
                v.wait_ge(slots_used, n + 1)
                v.tensor_copy(evac_tile(n), bank_view(n)).then_inc(vec_done, VE.step(f"pj.ev{n}"))
            v.wait_ge(pe_done, PE.at("lif"))
            ib = p1("ifb", 4)
            v.tensor_scalar(rows[0], PS1[0:4, 0:T], ib[:, 0:1], None, ALU.add).then_inc(vec_done, VE.step())
            v.tensor_scalar(rows[2], PS1[0:4, T:2 * T], ib[:, 1:2], None, ALU.add)\
             .then_inc(vec_done, VE.step("l.z"))
            v.wait_ge(pe_done, PE.at("z"))
            ab = p1("ab")
            for h in range(4):
                v.tensor_scalar(BC[:, h * T:(h + 1) * T], PS[2 + h // 2][:, (h % 2) * T:(h % 2 + 1) * T],
                                ab[:, h:h + 1], None, ALU.add).then_inc(vec_done, VE.step("g.z" if h == 3 else None))
            v.wait_ge(act_done, AC.at("g.sp"))
            v.scalar_tensor_tensor(out=E1, in0=BC, scalar=0.0, in1=TMP, op0=ALU.min, op1=ALU.subtract)\
             .then_inc(vec_done, VE.step())
            v_wait(v)
            v.tensor_tensor_scan(BC, reset[:, :], E1, 0.0, ALU.mult, ALU.add).then_inc(vec_done, VE.step("g.B"))
            v_wait(v)
            b3 = BC.rearrange("p (g l) -> p g l", l=CHUNK)
            v.tensor_tensor(TMP.rearrange("p (g l) -> p g l", l=CHUNK),
                            b3[:, :, CHUNK - 1:CHUNK].to_broadcast([P, 16, CHUNK]), b3, ALU.subtract)\
             .then_inc(vec_done, VE.step("g.diff"))
            gqf, gkf = (y.rearrange("p b t -> p (b t)") for y in (gq, gk))
            v.wait_ge(act_done, AC.at("g.eb"))
            v.scalar_tensor_tensor(out=gqf, in0=gqf, scalar=float(P) ** -0.5, in1=E1, op0=ALU.mult, op1=ALU.mult)\
             .then_inc(vec_done, VE.step())
            dec = small[:, 56:72]
            v.tensor_copy(dec, E1.rearrange("p (g l) -> p g l", l=CHUNK)[:, :, CHUNK - 1])\
             .then_inc(vec_done, VE.step("g.dec"))
            v.wait_ge(act_done, AC.at("g.ek"))
            v.tensor_tensor(BC, gkf, TMP, ALU.mult).then_inc(vec_done, VE.step())
            v_wait(v)
            v.tensor_tensor(gkf, gkf, E2, ALU.mult).then_inc(vec_done, VE.step("g.kend"))
            v_wait(v)
            v.memset(attn[:, :, :], 0.0).then_inc(vec_done, VE.step())
            v_wait(v)
            for t in range(NT):
                v.wait_ge(pe_done, PE.at(f"g.s{t}"))
                v.copy_predicated(attn[:, t, :].rearrange("p (h n) -> p h n", n=P),
                                  keep_i.unsqueeze(1).to_broadcast([P, 4, P]),
                                  PS[4 + t][:, :].rearrange("p (h n) -> p h n", n=P)).then_inc(vec_done, VE.step())
            v.wait_ge(pe_done, PE.at("g.kv0"))
            v.tensor_copy(sg[:, 0, :], PS[0][:, :]).then_inc(vec_done, VE.step())
            for cc in (1, 2):
                v_wait(v)
                v.wait_ge(pe_done, PE.at(f"g.kv{cc}"))
                for h in range(4):
                    v.scalar_tensor_tensor(out=sg[:, cc, h * P:(h + 1) * P], in0=sg[:, cc - 1, h * P:(h + 1) * P],
                                           scalar=dec[:, h * NCH + cc:h * NCH + cc + 1],
                                           in1=PS[cc][:, h * P:(h + 1) * P], op0=ALU.mult, op1=ALU.add)\
                     .then_inc(vec_done, VE.step("g.S" if (cc, h) == (2, 3) else None))
            for t in range(NT):
                v.wait_ge(pe_done, PE.at(f"g.o{t}"))
                v.tensor_copy(o_tm[:, t, :], PS[6 + t][:, :]).then_inc(vec_done, VE.step("g.o" if t else None))
            v_wait(v)
            v.wait_ge(act_done, AC.at("ggs"))
            v_headnorm(v, "g", o_tm[:, :, :], p1("gn"), gg, yg, 0)
            v_wait(v)
            qk3 = [y.rearrange("p t (h d) -> p (t h) d", d=HD) for y in (mq, mk)]
            for n in range(2):
                sq = scr[:, n, :].rearrange("p (g d) -> p g d", d=HD)
                v.tensor_tensor(sq, qk3[n], qk3[n], ALU.mult).then_inc(vec_done, VE.step())
            v_wait(v)
            for n in range(2):
                v.tensor_reduce(small[:, 80 + 16 * n:96 + 16 * n], scr[:, n, :].rearrange("p (g d) -> p g d", d=HD),
                                AX.X, ALU.add).then_inc(vec_done, VE.step("m.ss" if n else None))
            v.wait_ge(act_done, AC.at("m.root"))
            v.reciprocal(small[:, 144:176], small[:, 80:112]).then_inc(vec_done, VE.step())
            v_wait(v)
            cos = c("cos").rearrange("p (t d) -> p t d", t=NT).unsqueeze(2).to_broadcast([P, NT, MOBA_H, 32])
            sin = c("sin").rearrange("p (t d) -> p t d", t=NT).unsqueeze(2).to_broadcast([P, NT, MOBA_H, 32])
            for n in range(2):
                v.tensor_tensor(qk3[n], qk3[n], small[:, 144 + 16 * n:160 + 16 * n].unsqueeze(2)
                                .to_broadcast([P, 16, HD]), ALU.mult).then_inc(vec_done, VE.step())
                v_wait(v)
                v.tensor_tensor(qk3[n], qk3[n], p1("kng" if n else "qng").unsqueeze(1).to_broadcast([P, 16, HD]),
                                ALU.mult).then_inc(vec_done, VE.step())
                v_wait(v)
                y = (mk if n else mq).rearrange("p t (h d) -> p t h d", d=HD)
                a, b = y[:, :, :, 0:32], y[:, :, :, 32:64]
                t4 = [scr[:, i // 2, (i % 2) * 512:(i % 2 + 1) * 512].rearrange("p (t h d) -> p t h d", t=NT, d=32)
                      for i in range(4)]
                for i, (s, tab) in enumerate(((a, cos), (b, sin), (b, cos), (a, sin))):
                    v.tensor_tensor(t4[i], s, tab, ALU.mult).then_inc(vec_done, VE.step())
                v_wait(v)
                v.tensor_tensor(a, t4[0], t4[1], ALU.subtract).then_inc(vec_done, VE.step())
                v.tensor_tensor(b, t4[2], t4[3], ALU.add).then_inc(vec_done, VE.step("m.rope" if n else None))
                v_wait(v)
            v.wait_ge(pe_done, PE.at("m.tr1"))
            for t in range(NT):
                v.tensor_copy(mkT[:, :, t * P:(t + 1) * P], PS[4 + t][:, :].rearrange("p (q n) -> p q n", n=P))\
                 .then_inc(vec_done, VE.step("m.kT" if t else None))
            for i in range(MOBA_H + 1):
                if i < MOBA_H:
                    h = i
                    v.wait_ge(pe_done, PE.at(f"m.qk{h}"))
                    if h >= 2:
                        v.wait_ge(pe_done, PE.at(f"m.ptr{h - 2}"))
                    v.tensor_tensor(prob(h), PS[h % 2][:, 0:384], c("moba"), ALU.add)\
                     .then_inc(vec_done, VE.step(f"m.s{h}"))
                    v_wait(v)
                    mx = small[:, 176 + 2 * h:178 + 2 * h]
                    for n, cols in enumerate((slice(0, P), slice(P, 384))):
                        v.tensor_reduce(mx[:, n:n + 1], prob(h)[:, cols], AX.X, ALU.max)\
                         .then_inc(vec_done, VE.step())
                    v_wait(v)
                    v.tensor_scalar(small[:, 112 + 2 * h:114 + 2 * h], mx, -HD ** -0.5, None, ALU.mult)\
                     .then_inc(vec_done, VE.step(f"m.mx{h}"))
                if i >= 1:
                    h = i - 1
                    v.wait_ge(act_done, AC.at(f"m.e{h}"))
                    rs = small[:, 192 + 2 * h:194 + 2 * h]
                    v.reciprocal(rs, small[:, 128 + 2 * h:130 + 2 * h]).then_inc(vec_done, VE.step())
                    v_wait(v)
                    for n, cols in enumerate((slice(0, P), slice(P, 384))):
                        v.tensor_scalar(prob(h)[:, cols], prob(h)[:, cols], rs[:, n:n + 1], None, ALU.mult)\
                         .then_inc(vec_done, VE.step(f"m.p{h}" if n else None))
            cw = p1("convw")
            for w in range(4):
                for b in range(4):
                    src = lqk[:, b, w:w + T]
                    if w == 0:
                        v.tensor_scalar(lc[:, b, :], src, cw[:, 4 * b:4 * b + 1], None, ALU.mult)\
                         .then_inc(vec_done, VE.step())
                    else:
                        if b == 0:
                            v_wait(v)
                        v.scalar_tensor_tensor(out=lc[:, b, :], in0=src, scalar=cw[:, 4 * b + w:4 * b + w + 1],
                                               in1=lc[:, b, :], op0=ALU.mult, op1=ALU.add)\
                         .then_inc(vec_done, VE.step("l.qkc" if (w, b) == (3, 3) else None))
            v.wait_ge(act_done, AC.at("l.sp"))
            v.scalar_tensor_tensor(out=rows[3], in0=rows[2], scalar=0.0, in1=rows[3], op0=ALU.min, op1=ALU.subtract)\
             .then_inc(vec_done, VE.step())
            v_wait(v)
            v.tensor_tensor_scan(rows[2], reset[0:4, 0:T], rows[3], 0.0, ALU.mult, ALU.add)\
             .then_inc(vec_done, VE.step())
            v_wait(v)
            v.tensor_tensor(rows[1], rows[0], rows[2], ALU.subtract).then_inc(vec_done, VE.step())
            v.memset(rows[4], 0.0).then_inc(vec_done, VE.step())
            v_wait(v)
            ch = [r.rearrange("p (c l) -> p c l", l=CHUNK) for r in rows]
            v.tensor_copy(ch[4][:, 1:4, 0], ch[2][:, 0:3, CHUNK - 1]).then_inc(vec_done, VE.step())
            v_wait(v)
            v.tensor_tensor_scan(rows[0], rows[4], rows[1], 0.0, ALU.add, ALU.max).then_inc(vec_done, VE.step())
            v_wait(v)
            v.memset(rows[7][:, 0:8], 0.0).then_inc(vec_done, VE.step())
            v_wait(v)
            v.tensor_tensor(rows[7][:, 1:4], ch[2][:, 0:3, CHUNK - 1], ch[0][:, 0:3, CHUNK - 1], ALU.add)\
             .then_inc(vec_done, VE.step())
            v.tensor_copy(rows[7][:, 4:8], ch[0][:, :, CHUNK - 1]).then_inc(vec_done, VE.step())
            v.tensor_scalar(rows[3], rows[0], -1.0, None, ALU.mult).then_inc(vec_done, VE.step())
            v.scalar_tensor_tensor(out=rows[4], in0=rows[2], scalar=-1.0, in1=rows[0], op0=ALU.mult,
                                   op1=ALU.subtract).then_inc(vec_done, VE.step())
            v_wait(v)
            v.tensor_tensor(ch[5], ch[1], rows[7][:, 4:8].unsqueeze(2).to_broadcast([4, 4, CHUNK]), ALU.subtract)\
             .then_inc(vec_done, VE.step())
            v.tensor_tensor(ch[6], rows[7][:, 0:4].unsqueeze(2).to_broadcast([4, 4, CHUNK]), ch[0], ALU.subtract)\
             .then_inc(vec_done, VE.step())
            v_wait(v)
            v.tensor_tensor(rows[7][:, 0:4], rows[7][:, 0:4], rows[7][:, 4:8], ALU.subtract)\
             .then_inc(vec_done, VE.step("l.args"))
            VE.names["l.rows"] = VE.n
            cols = small[:, 208:232].rearrange("p (n t h) -> p n t h", n=3, t=NT)
            v.wait_ge(pe_done, PE.at("l.cols"))
            v.tensor_copy(small[:, 208:232], PS[0][:, 0:24]).then_inc(vec_done, VE.step())
            v_wait(v)
            v.wait_ge(pe_done, PE.at("l.negM"))
            for t in range(NT):
                for h in range(4):
                    v.scalar_tensor_tensor(out=ex[:, (t * 4 + h) * P:(t * 4 + h + 1) * P],
                                           in0=PS[1 + h // 2][:, (h % 2) * T + t * P:(h % 2) * T + (t + 1) * P],
                                           scalar=cols[:, 0, t, h:h + 1], in1=c("neg"), op0=ALU.add, op1=ALU.min)\
                     .then_inc(vec_done, VE.step())
            VE.names["l.ex"] = VE.names["l.negMread"] = VE.n
            v.wait_ge(pe_done, PE.at("l.a"))
            acol = small[:, 232:240].rearrange("p (q c) -> p q c", q=2)
            v.tensor_copy(small[:, 232:240], PS[1][:, 0:8]).then_inc(vec_done, VE.step("l.acol"))
            v.wait_ge(act_done, AC.at("l.exp"))
            for t in range(NT):
                v.wait_ge(pe_done, PE.at(f"l.s{t}"))
                def parity(y):
                    return y.rearrange("p (t q o n) -> p o t q n", t=NT, q=2, o=2)[:, t]
                v.scalar_tensor_tensor(out=parity(attn[:, :, :].rearrange("p t n -> p (t n)")),
                                       in0=PS[4 + t][:, :].rearrange("p (t q n) -> p t q n", t=NT, q=2),
                                       scalar=ML_DK ** -0.5, in1=parity(ex), op0=ALU.mult, op1=ALU.mult)\
                 .then_inc(vec_done, VE.step(f"l.sm{t}"))
            v.wait_ge(pe_done, PE.at("l.ktr"))
            v.scalar_tensor_tensor(out=kw.rearrange("p t (h d) -> p t h d", d=HD),
                                   in0=PS[6][:, :].rearrange("p (t h d) -> p t h d", t=NT, d=HD),
                                   scalar=ML_DK ** -0.5,
                                   in1=cols[:, 2, :, :].unsqueeze(3).to_broadcast([P, NT, 4, HD]),
                                   op0=ALU.mult, op1=ALU.mult).then_inc(vec_done, VE.step("l.kw"))
            v.wait_ge(pe_done, PE.at("l.iw"))
            v.tensor_tensor(lc[:, 0:2, :], lc[:, 0:2, :], PS[3][:, :].rearrange("p (b t) -> p b t", t=T), ALU.mult)\
             .then_inc(vec_done, VE.step("l.qi"))
            v.wait_ge(pe_done, PE.at("l.kv0"))
            v.tensor_copy(st[:, 0, :, :], PS[1][:, 0:258].rearrange("p (q d) -> p q d", d=129))\
             .then_inc(vec_done, VE.step())
            for cc in (1, 2):
                v_wait(v)
                v.wait_ge(pe_done, PE.at(f"l.kv{cc}"))
                for q in range(2):
                    v.scalar_tensor_tensor(out=st[:, cc, q, :], in0=st[:, cc - 1, q, :],
                                           scalar=acol[:, q, cc:cc + 1], in1=PS[1 + cc][:, q * 129:(q + 1) * 129],
                                           op0=ALU.mult, op1=ALU.add)\
                     .then_inc(vec_done, VE.step("l.st" if (cc, q) == (2, 1) else None))
            v.wait_ge(act_done, AC.at("l.oa"))
            den = oa[:, :, :, 128]
            dn = small[:, 240:248].rearrange("p (t h) -> p t h", t=NT)
            v.scalar_tensor_tensor(out=dn, in0=den, scalar=-1.0, in1=den, op0=ALU.mult, op1=ALU.max)\
             .then_inc(vec_done, VE.step())
            v_wait(v)
            v.tensor_tensor(dn, dn, cols[:, 1, :, :], ALU.max).then_inc(vec_done, VE.step())
            v_wait(v)
            v.reciprocal(small[:, 248:256], small[:, 240:248]).then_inc(vec_done, VE.step())
            v_wait(v)
            v.tensor_tensor(o_tm[:, :, :].rearrange("p t (h d) -> p t h d", d=P), oa[:, :, :, 0:128],
                            small[:, 248:256].rearrange("p (t h) -> p t h", t=NT).unsqueeze(3)
                            .to_broadcast([P, NT, 4, P]), ALU.mult).then_inc(vec_done, VE.step())
            v_wait(v)
            v_headnorm(v, "l", o_tm[:, :, :], p1("mn"), lo, yl, 0)
            v.wait_ge(act_done, AC.at("gates"))
            gf = gates.rearrange("p b t -> p (b t)")
            for n in range(12):
                b, q = n // 4, n % 4
                if n % 2 == 0:
                    v.wait_ge(pe_done, PE.at(f"br.{n}"))
                else:
                    v.wait_ge(slots_used, PROJ1 + n // 2 + 1)
                own = gf[:, (b * 8 + 2 * q) * T:(b * 8 + 2 * q + 2) * T]
                v.tensor_tensor(own, own, PS[2 + n % 4][:, :], ALU.mult).then_inc(vec_done, VE.step(f"br.g{n}"))
                if b:
                    v_wait(v)
                    acc = gf[:, 2 * q * T:(2 * q + 2) * T]
                    v.tensor_tensor(acc, acc, own, ALU.add).then_inc(vec_done, VE.step("br.mix" if n == 11 else None))
            rgv.start("l1", it)
            rgv.k = split_from("l1")
            for k in range(2):
                v_split(v, "f1", k, rgv)
            v_residual(v, PROJ1 + 6 + 4, 1.0, "x1")
            v_wait(v)
            v_rms(v, "n2")
            v_transposed(v, "n2", p1("n2"))
            v_splitx(v, "f1")
            v_ffn3(v, "f1", DFF1 // UNIT, False, rgv, 2)
            v_residual(v, "f1.end", 1.0, "x2")

        PS1 = PS[1]

        PAD = CONV_WIN - 1
        cv = big[:, 0:4 * (PAD + T)].rearrange("p (b t) -> p b t", t=PAD + T)
        cg = fm(1144, 4)
        qkvr = big[:, 2168:2168 + 12 * W3].rearrange("p (b t) -> p b t", t=W3)
        zt = fm(5276, 4)
        qc = fm(6300, 12)
        dq, dk, dv = qc[:, 0:4, :], qc[:, 4:8, :], qc[:, 8:12, :]
        ca = fm(9372, 4)
        caf = big[:, 9372:9372 + 1024]
        kbT, qg = fm(10396, 4), fm(11420, 4)
        kbTf, qgf = big[:, 10396:11420], big[:, 11420:12444]
        vb, kbg, kdec = tm(13468, 512), tm(14492, 512), tm(15516, 512)
        mA_T, mA, mNT, mN, mQ = (tm(i, 512) for i in (2168, 3192, 4216, 8348, 12444))
        mN2, mIN2, mN2T = scr[:, 1, 0:512], scr[:, 1, 512:1024], keT
        mIN4, mP1, mU = mNT, mN, mQ
        nw = fm(10396, 4)
        vn = tm(3192, 512)
        S = sg[:, 0, :]
        comb = sb("comb", [P, NT, NEXP])
        place = sb("place", [P, NT, NPASS + 1])
        wgt = sb("wgt", [P, NT, NPASS + 1])
        ccol = sb("ccol", [P, 2 * NT])
        og = big[:, 2048:3072]
        xg = big[:, 3072:4096].rearrange("p (k c) -> p k c", c=CAP)
        pick = big[:, 4096:4352].rearrange("p (t c) -> p t c", t=NT)
        pickw = big[:, 4352:4608].rearrange("p (t c) -> p t c", t=NT)
        put = big[:, 4608:4864].rearrange("p (t c) -> p t c", t=NT)
        Y = big[:, 0:2 * D].rearrange("p (t n) -> p t n", t=NT)
        KINDS2 = ["fm"] * 12

        def hh(ap):
            return ap.rearrange("p (h n) -> p h n", n=P)

        def over_heads(mask):
            return mask.unsqueeze(1).to_broadcast([P, 4, P])

        def evac2(n):
            if n < 2:
                return cv[:, 2 * n:2 * n + 2, PAD:PAD + T]
            if n < 4:
                return cg[:, 2 * n - 4:2 * n - 2, :]
            if n < 10:
                return qkvr[:, 2 * (n - 4):2 * (n - 4) + 2, 3:W3]
            return zt[:, 2 * (n - 10):2 * (n - 10) + 2, :]

        def t_ln(pe, tag):
            t_transpose(pe, tag, X, [(vec_done, VE.at(tag + ".x"))])

        def mix_tensor(pe, tag, layer, last):
            rg.start("mix" + tag, 0)
            t_ln(pe, tag + "n1")
            pe.wait_ge(act_done, AC.at(tag + "n1.xT"))
            pe.wait_ge(vec_done, VE.at(tag + "n1.xT"))
            t_project(pe, tag + "pj", KINDS2)
            pe.wait_ge(par_loaded, 16 * ((DEPTH if RUN_FIRST else 0) + layer + 1))
            for n, name in enumerate(("wb", "wa")):
                w = p2(name).rearrange("p (k n) -> p k n", n=4)
                for k in range(KD):
                    mm = pe.matmul(PS[0][0:4, n * T:(n + 1) * T], w[:, k, :], xT[:, k, :],
                                   start=(k == 0), stop=(k == KD - 1))
            mm.then_inc(pe_done, PE.step(tag + "ba"))
            pe.wait_ge(vec_done, VE.at(tag + "sq"))
            for i in range(4):
                mm = pe.matmul(PS[1 + i][:, :], c("ones"), scr[:, i // 2, (i % 2) * 512:(i % 2 + 1) * 512],
                               start=True, stop=True)
            mm.then_inc(pe_done, PE.step(tag + "ssq"))
            pe.wait_ge(vec_done, VE.at(tag + "rows"))
            pe.wait_ge(act_done, AC.at(tag + "rows"))
            pe.wait_ge(vec_done, VE.at(tag + "l2"))
            for n, row in enumerate((rows[0], rows[1], rows[2], rows[3])):
                for t in range(NT):
                    mm = pe.transpose(PS[0][:, (n * NT + t) * 4:(n * NT + t) * 4 + 4], row[:, t * P:(t + 1) * P],
                                      ident[0:4, 0:4])
            mm.then_inc(pe_done, PE.step(tag + "cols"))
            sel = c("sel", 4).rearrange("p (h n) -> p h n", n=P)
            for n, row in enumerate((rows[0], rows[1], rows[4])):
                for h in range(4):
                    mm = pe.matmul(PS[1 + 2 * n + h // 2][:, (h % 2) * T:(h % 2 + 1) * T], sel[:, h, :], row,
                                   start=True, stop=True)
                mm.then_inc(pe_done, PE.step(tag + f"bc{n}"))
            for h in range(4):
                mm = pe.matmul(PS[7][:, h * 4:h * 4 + 4], sel[:, h, :], rows[5][:, 0:4], start=True, stop=True)
            mm.then_inc(pe_done, PE.step(tag + "egl"))
            pe.wait_ge(vec_done, VE.at(tag + "bcs"))
            for i, (src, dst) in enumerate(((dv, "v"), (dk, "k"))):
                for t in range(NT):
                    for h in range(4):
                        mm = pe.transpose(PS[2 * i + t][:, h * P:(h + 1) * P], src[:, h, t * P:(t + 1) * P], ident)
                    mm.then_inc(pe_done, PE.step(tag + f"tr{dst}{t}"))
            for t in range(NT):
                for i, src in enumerate((kbT, dq)):
                    for h in range(4):
                        mm = pe.matmul(PS[4 + 2 * t + i][:, h * P:(h + 1) * P], dk[:, h, t * P:(t + 1) * P],
                                       src[:, h, t * P:(t + 1) * P], start=True, stop=True)
                mm.then_inc(pe_done, PE.step(tag + f"kk{t}"))

            def per_head(t, bank, lhs, rhs, name):
                for h in range(4):
                    hc = slice(h * P, (h + 1) * P)
                    mm = pe.matmul(PS[bank][:, hc], lhs[:, hc], rhs[:, hc], start=True, stop=True)
                mm.then_inc(pe_done, PE.step(tag + name + str(t)))

            def turn(t, bank, src, name):
                for h in range(4):
                    hc = slice(h * P, (h + 1) * P)
                    mm = pe.transpose(PS[bank][:, hc], src[:, hc], ident)
                mm.then_inc(pe_done, PE.step(tag + name + str(t)))
            for t in range(NT):
                pe.wait_ge(vec_done, VE.at(tag + "kdec"))
                pe.wait_ge(vec_done, VE.at(tag + f"Q{t}"))
                turn(t, 0, mA_T[:, t, :], "A")
                turn(t, 1, mNT[:, t, :], "N")
                pe.wait_ge(act_done, AC.at(tag + f"N{t}"))
                per_head(t, 2, mNT[:, t, :], mN[:, t, :], "N2")
                per_head(t, 3, mN[:, t, :], mNT[:, t, :], "N2T")
                pe.wait_ge(vec_done, VE.at(tag + f"IN2{t}"))
                pe.wait_ge(act_done, AC.at(tag + f"N2T{t}"))
                per_head(t, 0, mN2T[:, t, :], mN2, "N4")
                per_head(t, 1, mIN2, mQ[:, t, :], "P1")
                pe.wait_ge(vec_done, VE.at(tag + f"IN4{t}"))
                pe.wait_ge(act_done, AC.at(tag + f"P1{t}"))
                per_head(t, 2, mIN4[:, t, :], mP1[:, t, :], "U")
                for lev in range(3):
                    pe.wait_ge(vec_done, VE.at(tag + f"U{lev}{t}"))
                    per_head(t, 3, mN2T[:, t, :], mU[:, t, :], f"X{lev}")
                    turn(t, 0, mU[:, t, :], f"T{lev}")
                    pe.wait_ge(vec_done, VE.at(tag + f"T{lev}{t}"))
                    pe.wait_ge(act_done, AC.at(tag + f"X{lev}{t}"))
                    per_head(t, 2, mN2, mIN2, f"UX{lev}")
                pe.wait_ge(vec_done, VE.at(tag + f"U3{t}"))
            for t in range(NT):
                per_head(t, t, kbg[:, t, :], mU[:, t, :], "w")
            pe.wait_ge(vec_done, VE.at(tag + "w"))
            for cc in range(NCH):
                t, r = cc // 2, slice(CHUNK * (cc % 2), CHUNK * (cc % 2) + CHUNK)
                b = 2 + 3 * (cc % 2)
                tok = slice(cc * CHUNK, (cc + 1) * CHUNK)
                if cc:
                    pe.wait_ge(vec_done, VE.at(tag + f"S{cc - 1}"))
                if cc >= 2:
                    pe.wait_ge(act_done, AC.at(tag + f"o{cc - 2}"))
                for h in range(4):
                    hc = slice(h * P, (h + 1) * P)
                    mm = pe.matmul(PS[b][r, hc], mU[r, t, h * P + r.start:h * P + r.stop], vb[r, t, hc],
                                   start=True, stop=(cc == 0))
                    if cc:
                        mm = pe.matmul(PS[b][r, hc], nw[:, h, tok], S[:, hc], start=False, stop=True)
                mm.then_inc(pe_done, PE.step(tag + f"vn{cc}"))
                pe.wait_ge(vec_done, VE.at(tag + f"vn{cc}"))
                for h in range(4):
                    hc = slice(h * P, (h + 1) * P)
                    if cc:
                        pe.matmul(PS[b + 1][r, hc], qg[:, h, tok], S[:, hc], start=True, stop=False)
                    mm = pe.matmul(PS[b + 1][r, hc], attn[r, t, h * P + r.start:h * P + r.stop], vn[r, t, hc],
                                   start=(cc == 0), stop=True)
                mm.then_inc(pe_done, PE.step(tag + f"o{cc}"))
                if cc < NCH - 1:
                    for h in range(4):
                        hc = slice(h * P, (h + 1) * P)
                        bank = PS[4] if cc % 2 == 0 else PS[7]
                        mm = pe.matmul(bank[:, hc], kdec[r, t, hc], vn[r, t, hc], start=True, stop=True)
                    mm.then_inc(pe_done, PE.step(tag + f"dS{cc}"))
            t_headnorm(pe, tag + "d", o_tm, 0)
            pe.wait_ge(vec_done, VE.at(tag + "cc"))
            for b in range(4):
                mm = pe.matmul(PS[2][:, 0:T], c("ones"), ca[:, b, :], start=(b == 0), stop=(b == 3))
            mm.then_inc(pe_done, PE.step(tag + "cmu"))
            pe.wait_ge(vec_done, VE.at(tag + "csq"))
            for b in range(4):
                mm = pe.matmul(PS[3][:, 0:T], c("ones"), scr[:, 0, b * T:(b + 1) * T], start=(b == 0), stop=(b == 3))
            mm.then_inc(pe_done, PE.step(tag + "cvar"))
            pe.wait_ge(act_done, AC.at(tag + "cy"))
            pe.wait_ge(vec_done, VE.at(tag + "d.y1"))
            pe.wait_ge(act_done, AC.at(tag + "o3"))
            t_out(pe, tag + "wo", lambda k: ca[:, k, :] if k < 4 else dq[:, k - 4, :])
            t_ln(pe, tag + "n2")
            if last:
                pe.wait_ge(act_done, AC.at(tag + "n2.xT"))
                pe.wait_ge(vec_done, VE.at(tag + "n2.xT"))
                w = p2("router").rearrange("p (k n) -> p k n", n=NEXP)
                for t in range(NT):
                    for k in range(KD):
                        mm = pe.matmul(PS[0][:, t * NEXP:(t + 1) * NEXP], xT[:, k, t * P:(t + 1) * P], w[:, k, :],
                                       start=(k == 0), stop=(k == KD - 1))
                mm.then_inc(pe_done, PE.step(tag + "route"))
                pe.wait_ge(vec_done, VE.at(tag + "member"))
                pe.matmul(PS[0][:, 0:8], c("before"), member[:, 0, :], start=True, stop=True)
                pe.matmul(PS[0][:, 8:16], c("before"), member[:, 1, :], start=True, stop=False)
                pe.matmul(PS[0][:, 8:16], c("ones"), member[:, 0, :], start=False, stop=True)
                pe.matmul(PS[0][:, 16:24], c("ones"), member[:, 0, :], start=True, stop=False)
                pe.matmul(PS[0][:, 16:24], c("ones"), member[:, 1, :], start=False, stop=True)\
                  .then_inc(pe_done, PE.step(tag + "places"))
                pe.wait_ge(vec_done, VE.at(tag + "pick"))
                t_gather(pe, tag)

        def mix_scalar(act, tag, layer, last):
            act.dma_start(par[:, 0:NP2], par2_d[layer]).then_inc(par_loaded, 16)
            a_transposed(act, tag + "n1", None)
            AC.names[tag + "pj.go"] = AC.n
            act.wait_ge(vec_done, VE.at(tag + "pad"))
            for n in range(0, 12, 2):
                act.wait_ge(slots_used, n + 1)
                act.activation(evac2(n), PS[4 + n % 4][:, :].rearrange("p (a b) -> p a b", a=2),
                               ACT.Sigmoid if n == 2 else ACT.Silu if n == 10 else ACT.Copy)\
                   .then_inc(act_done, AC.step(tag + f"pj.ev{n}"))
            act.wait_ge(vec_done, VE.at(tag + "pj.ev11"))
            act.activation(cg[:, 2:4, :], cg[:, 2:4, :], ACT.Sigmoid).then_inc(act_done, AC.step(tag + "cg"))
            act.activation(zt[:, 2:4, :], zt[:, 2:4, :], ACT.Silu).then_inc(act_done, AC.step())
            act.wait_ge(vec_done, VE.at(tag + "qkv"))
            act.activation(qc[:, :, :], qc[:, :, :], ACT.Silu).then_inc(act_done, AC.step(tag + "qkv"))
            act.wait_ge(vec_done, VE.at(tag + "z"))
            act.activation(rows[1], rows[1], ACT.Sigmoid).then_inc(act_done, AC.step())
            a_sp(act, rows[2], rows[3], tag + "sp")
            act.activation(small[0:4, 0:1], small[0:4, 0:1], ACT.Exp).then_inc(act_done, AC.step(tag + "ea"))
            act.wait_ge(vec_done, VE.at(tag + "gc"))
            act.activation(rows[4], rows[0], ACT.Exp).then_inc(act_done, AC.step())
            act.activation(rows[3], rows[3], ACT.Exp).then_inc(act_done, AC.step())
            act.activation(rows[5][:, 0:4], rows[5][:, 0:4], ACT.Exp).then_inc(act_done, AC.step(tag + "rows"))
            act.wait_ge(pe_done, PE.at(tag + "ssq"))
            for i in range(4):
                act.activation(scr[:, i // 2, (i % 2) * 512:(i % 2 + 1) * 512], PS[1 + i][:, :], ACT.Sqrt,
                               bias=eps_rms[:, 0:1]).then_inc(act_done, AC.step(tag + "l2r" if i == 3 else None))
            act.wait_ge(vec_done, VE.at(tag + "ex"))
            act.activation(scr[:, 0, :], scr[:, 0, :], ACT.Exp).then_inc(act_done, AC.step(tag + "ET"))
            for t in range(NT):
                def copy(dst, bank, name, pe_name=None):
                    act.wait_ge(pe_done, PE.at(tag + (pe_name or name) + str(t)))
                    act.activation(dst, PS[bank][:, :], ACT.Copy).then_inc(act_done, AC.step(tag + name + str(t)))
                copy(mA[:, t, :], 0, "A")
                copy(mN[:, t, :], 1, "N")
                copy(mN2T[:, t, :], 3, "N2T")
                copy(mP1[:, t, :], 1, "P1")
                for lev in range(3):
                    copy(mIN2, 3, f"X{lev}")
            for cc in range(NCH):
                t, r = cc // 2, slice(CHUNK * (cc % 2), CHUNK * (cc % 2) + CHUNK)
                act.wait_ge(pe_done, PE.at(tag + f"o{cc}"))
                act.activation(o_tm[r, t, :], PS[3 + 3 * (cc % 2)][r, :], ACT.Copy)\
                   .then_inc(act_done, AC.step(tag + f"o{cc}"))
            a_headnorm(act, tag + "d")
            act.wait_ge(pe_done, PE.at(tag + "cvar"))
            act.activation(scr[:, 1, 0:T], PS[3][:, 0:T], ACT.Sqrt, bias=eps_ln[:, 0:1], scale=1.0 / 512)\
               .then_inc(act_done, AC.step(tag + "crs"))
            act.wait_ge(vec_done, VE.at(tag + "cn"))
            act.wait_ge(par_loaded, 16 * ((DEPTH if RUN_FIRST else 0) + layer + 1))
            for b in range(4):
                act.activation(ca[:, b, :], ca[:, b, :], ACT.Silu, bias=p2("clnb")[:, b:b + 1],
                               scale=p2("clng")[:, b:b + 1]).then_inc(act_done, AC.step(tag + "cy" if b == 3 else None))
            a_ln(act, tag + "m")
            a_transposed(act, tag + "n2", None)
            if last:
                act.wait_ge(vec_done, VE.at(tag + "d21"))
                act.activation(small[:, 40:42], small[:, 40:42], ACT.Exp).then_inc(act_done, AC.step(tag + "e21"))
                a_gather(act, tag)

        def v_ln(v, tag, gain, bias, name):
            for t in range(NT):
                for f in range(2):
                    v.bn_stats(small[:, 260 + 12 * t + 6 * f:266 + 12 * t + 6 * f], X[:, t, f * 512:(f + 1) * 512])\
                     .then_inc(vec_done, VE.step())
            v_wait(v)
            for t in range(NT):
                v.bn_aggr(small[:, 290 + 2 * t:292 + 2 * t], small[:, 260 + 12 * t:272 + 12 * t])\
                 .then_inc(vec_done, VE.step(tag + ".var" if t else None))
            v.wait_ge(act_done, AC.at(tag + ".root"))
            v.reciprocal(small[:, 296:298], small[:, 294:296]).then_inc(vec_done, VE.step())
            for t in range(NT):
                v_wait(v)
                v.tensor_scalar(X[:, t, :], X[:, t, :], small[:, 290 + 2 * t:291 + 2 * t],
                                small[:, 296 + t:297 + t], ALU.subtract, ALU.mult).then_inc(vec_done, VE.step())
            for op, y in ((ALU.mult, gain), (ALU.add, bias)):
                v_wait(v)
                for t in range(NT):
                    v.tensor_tensor(X[:, t, :], X[:, t, :], y, op).then_inc(vec_done, VE.step())
            VE.names[name] = VE.n

        def a_ln(act, tag):
            act.wait_ge(vec_done, VE.at(tag + ".var"))
            act.activation(small[:, 294:296], small[:, 291:294:2], ACT.Sqrt, bias=eps_ln[:, 0:1])\
               .then_inc(act_done, AC.step(tag + ".root"))

        def mix_vector(v, tag, layer, last):
            v.wait_ge(x_loaded, 16)
            v.wait_ge(con_loaded, 16)
            v.memset(cv[:, :, 0:PAD], 0.0).then_inc(vec_done, VE.step())
            v.memset(qkvr[:, :, 0:3], 0.0).then_inc(vec_done, VE.step(tag + "pad"))
            VE.names[tag + "n1.x"] = VE.n
            v_transposed(v, tag + "n1", None)
            VE.names[tag + "pj.go"] = VE.n
            for n in range(1, 12, 2):
                v.wait_ge(slots_used, n + 1)
                v.tensor_copy(evac2(n), PS[4 + n % 4][:, :].rearrange("p (a b) -> p a b", a=2))\
                 .then_inc(vec_done, VE.step(tag + f"pj.ev{n}"))
            v.wait_ge(par_loaded, 16 * ((DEPTH if RUN_FIRST else 0) + layer + 1))
            v.wait_ge(act_done, AC.at(tag + "pj.ev10"))
            v_wait(v)
            sc = p2("sconv")
            for w in range(4):
                for b in range(12):
                    src = qkvr[:, b, w:w + T]
                    if w == 0:
                        v.tensor_scalar(qc[:, b, :], src, sc[:, 4 * b:4 * b + 1], None, ALU.mult)\
                         .then_inc(vec_done, VE.step())
                    else:
                        v.wait_ge(vec_done, VE.n - 11)
                        v.scalar_tensor_tensor(out=qc[:, b, :], in0=src, scalar=sc[:, 4 * b + w:4 * b + w + 1],
                                               in1=qc[:, b, :], op0=ALU.mult, op1=ALU.add)\
                         .then_inc(vec_done, VE.step(tag + "qkv" if (w, b) == (3, 11) else None))
            v.wait_ge(pe_done, PE.at(tag + "ba"))
            gp = p2("gpar", 4)
            v.tensor_copy(rows[1], PS[0][0:4, 0:T]).then_inc(vec_done, VE.step())
            v.tensor_copy(small[0:4, 0:1], gp[:, 0:1]).then_inc(vec_done, VE.step())
            v.tensor_scalar(rows[2], PS[0][0:4, T:2 * T], gp[:, 1:2], None, ALU.add)\
             .then_inc(vec_done, VE.step(tag + "z"))
            v_gated(v, tag)
            v_taps(v, tag, 0, 2)
            v.wait_ge(act_done, AC.at(tag + "qkv"))
            qkf = big[:, 6300:6300 + 2048]
            scf = scr[:, :, :].rearrange("p t n -> p (t n)")
            v.tensor_tensor(scf, qkf, qkf, ALU.mult).then_inc(vec_done, VE.step(tag + "sq"))
            v_taps(v, tag, 2, 3)
            v.wait_ge(act_done, AC.at(tag + "ea"))
            v.scalar_tensor_tensor(out=rows[3], in0=rows[2], scalar=0.0, in1=rows[3], op0=ALU.max, op1=ALU.add)\
             .then_inc(vec_done, VE.step())
            v_wait(v)
            v.tensor_scalar(rows[2], rows[3], small[0:4, 0:1], -1.0, ALU.mult, ALU.mult)\
             .then_inc(vec_done, VE.step())
            v_wait(v)
            v.tensor_tensor_scan(rows[0], reset[0:4, 0:T], rows[2], 0.0, ALU.mult, ALU.add)\
             .then_inc(vec_done, VE.step())
            v_wait(v)
            ch = [r.rearrange("p (c l) -> p c l", l=CHUNK) for r in rows]
            v.tensor_tensor(ch[3], ch[0][:, :, CHUNK - 1:CHUNK].to_broadcast([4, 4, CHUNK]), ch[0], ALU.subtract)\
             .then_inc(vec_done, VE.step())
            v.tensor_copy(rows[5][:, 0:4], ch[0][:, :, CHUNK - 1]).then_inc(vec_done, VE.step(tag + "gc"))
            v_taps(v, tag, 3, 4)
            v.wait_ge(act_done, AC.at(tag + "rows"))
            v.tensor_tensor(rows[2], rows[1], rows[4], ALU.mult).then_inc(vec_done, VE.step(tag + "rows"))
            v_taps(v, tag, 4, 5)
            v.wait_ge(act_done, AC.at(tag + "l2r"))
            v.reciprocal(scf, scf).then_inc(vec_done, VE.step())
            v_wait(v)
            v.scalar_tensor_tensor(out=qkf[:, 0:1024], in0=qkf[:, 0:1024], scalar=float(P) ** -0.5,
                                   in1=scf[:, 0:1024], op0=ALU.mult, op1=ALU.mult).then_inc(vec_done, VE.step())
            v.tensor_tensor(qkf[:, 1024:2048], qkf[:, 1024:2048], scf[:, 1024:2048], ALU.mult)\
             .then_inc(vec_done, VE.step(tag + "l2"))
            col = small[:, 80:112].rearrange("p (n t h) -> p n t h", n=4, t=NT)
            v.wait_ge(pe_done, PE.at(tag + "cols"))
            v.tensor_copy(small[:, 80:112], PS[0][:, 0:32]).then_inc(vec_done, VE.step())
            v_wait(v)
            v.wait_ge(pe_done, PE.at(tag + "bc0"))
            for t in range(NT):
                for h in range(4):
                    v.scalar_tensor_tensor(out=scr[:, 0, (t * 4 + h) * P:(t * 4 + h + 1) * P],
                                           in0=PS[1 + h // 2][:, (h % 2) * T + t * P:(h % 2) * T + (t + 1) * P],
                                           scalar=col[:, 0, t, h:h + 1], in1=c("neg"), op0=ALU.subtract,
                                           op1=ALU.min).then_inc(vec_done, VE.step())
            VE.names[tag + "ex"] = VE.n
            v.wait_ge(pe_done, PE.at(tag + "bc1"))
            for i in range(2):
                v.tensor_tensor(kbTf[:, i * 512:(i + 1) * 512], qkf[:, 1024 + i * 512:1536 + i * 512],
                                PS[3 + i][:, :], ALU.mult).then_inc(vec_done, VE.step())
            v.wait_ge(pe_done, PE.at(tag + "bc2"))
            for i in range(2):
                v.tensor_tensor(qgf[:, i * 512:(i + 1) * 512], qkf[:, i * 512:(i + 1) * 512],
                                PS[5 + i][:, :], ALU.mult).then_inc(vec_done, VE.step())
            v.wait_ge(pe_done, PE.at(tag + "egl"))
            egl = small[:, 112:128].rearrange("p (h c) -> p h c", h=4)
            v.tensor_copy(small[:, 112:128], PS[7][:, 0:16]).then_inc(vec_done, VE.step(tag + "bcs"))
            for t in range(NT):
                v.wait_ge(pe_done, PE.at(tag + f"trv{t}"))
                v.tensor_tensor(hh(vb[:, t, :]), hh(PS[t][:, :]), col[:, 1, t, :].unsqueeze(2)
                                .to_broadcast([P, 4, P]), ALU.mult).then_inc(vec_done, VE.step())
            for t in range(NT):
                v.wait_ge(pe_done, PE.at(tag + f"trk{t}"))
                for n, dst in ((2, kbg), (3, kdec)):
                    v.tensor_tensor(hh(dst[:, t, :]), hh(PS[2 + t][:, :]), col[:, n, t, :].unsqueeze(2)
                                    .to_broadcast([P, 4, P]), ALU.mult).then_inc(vec_done, VE.step())
            VE.names[tag + "kdec"] = VE.n
            v_wait(v)
            v.wait_ge(act_done, AC.at(tag + "ET"))
            for t in range(NT):
                v.wait_ge(pe_done, PE.at(tag + f"kk{t}"))
                v.tensor_tensor(mA_T[:, t, :], PS[4 + 2 * t][:, :], scr[:, 0, t * 512:(t + 1) * 512], ALU.mult)\
                 .then_inc(vec_done, VE.step())
                v.tensor_tensor(attn[:, t, :], PS[5 + 2 * t][:, :], scr[:, 0, t * 512:(t + 1) * 512], ALU.mult)\
                 .then_inc(vec_done, VE.step())
            v_wait(v)
            for t in range(NT):
                v.tensor_tensor(hh(mNT[:, t, :]), hh(mA_T[:, t, :]), over_heads(c("m8")), ALU.mult)\
                 .then_inc(vec_done, VE.step())
                v_wait(v)
                v.tensor_tensor(hh(mQ[:, t, :]), hh(mNT[:, t, :]), over_heads(ident), ALU.add)\
                 .then_inc(vec_done, VE.step(tag + f"Q{t}"))
            EARLY, PER_TILE = 5, 9
            off = c("off").rearrange("p (l n) -> p l n", l=3)
            for t in range(NT):
                if t:
                    v.wait_ge(pe_done, PE.at(tag + f"UX2{t - 1}"))
                tap = EARLY + PER_TILE * t
                v_taps(v, tag, tap, tap + 1)
                v.wait_ge(pe_done, PE.at(tag + f"N2{t}"))
                v.tensor_copy(mN2, PS[2][:, :]).then_inc(vec_done, VE.step())
                v.tensor_tensor(hh(mIN2), hh(PS[2][:, :]), over_heads(ident), ALU.add)\
                 .then_inc(vec_done, VE.step(tag + f"IN2{t}"))
                v_taps(v, tag, tap + 1, tap + 2)
                v.wait_ge(pe_done, PE.at(tag + f"N4{t}"))
                v.tensor_tensor(hh(mIN4[:, t, :]), hh(PS[0][:, :]), over_heads(ident), ALU.add)\
                 .then_inc(vec_done, VE.step(tag + f"IN4{t}"))
                v_taps(v, tag, tap + 2, tap + 3)
                v.wait_ge(pe_done, PE.at(tag + f"U{t}"))
                v.tensor_copy(mU[:, t, :], PS[2][:, :]).then_inc(vec_done, VE.step())
                v.wait_ge(act_done, AC.at(tag + f"A{t}"))
                for lev in range(3):
                    v.tensor_tensor(hh(mN2T[:, t, :]), hh(mA[:, t, :]), over_heads(off[:, lev, :]), ALU.mult)\
                     .then_inc(vec_done, VE.step(tag + f"U{lev}{t}"))
                    v_taps(v, tag, tap + 3 + 2 * lev, tap + 4 + 2 * lev)
                    v.wait_ge(pe_done, PE.at(tag + f"T{lev}{t}"))
                    v.tensor_copy(mN2, PS[0][:, :]).then_inc(vec_done, VE.step(tag + f"T{lev}{t}"))
                    v_taps(v, tag, tap + 4 + 2 * lev, tap + 5 + 2 * lev)
                    v.wait_ge(pe_done, PE.at(tag + f"UX{lev}{t}"))
                    v.tensor_tensor(mU[:, t, :], mU[:, t, :], PS[2][:, :], ALU.subtract)\
                     .then_inc(vec_done, VE.step(tag + f"U3{t}" if lev == 2 else None))
            LATE = EARLY + NT * PER_TILE + 2
            v_taps(v, tag, LATE - 2, LATE)
            for t in range(NT):
                v.wait_ge(pe_done, PE.at(tag + f"w{t}"))
                v.tensor_scalar(nw[:, :, t * P:(t + 1) * P], hh(PS[t][:, :]), -1.0, None, ALU.mult)\
                 .then_inc(vec_done, VE.step(tag + "w" if t else None))
            for cc in range(NCH):
                t, r = cc // 2, slice(CHUNK * (cc % 2), CHUNK * (cc % 2) + CHUNK)
                if LATE + 2 * cc < CONV_WIN:
                    v_taps(v, tag, LATE + 2 * cc, min(LATE + 2 * cc + 2, CONV_WIN))
                v.wait_ge(pe_done, PE.at(tag + f"vn{cc}"))
                v.tensor_copy(vn[r, t, :], PS[2 + 3 * (cc % 2)][r, :]).then_inc(vec_done, VE.step(tag + f"vn{cc}"))
                if cc < NCH - 1:
                    v.wait_ge(pe_done, PE.at(tag + f"dS{cc}"))
                    bank = PS[4] if cc % 2 == 0 else PS[7]
                    if cc == 0:
                        v.tensor_copy(S, bank[:, :]).then_inc(vec_done, VE.step(tag + "S0"))
                    else:
                        v_wait(v)
                        for h in range(4):
                            hc = slice(h * P, (h + 1) * P)
                            v.scalar_tensor_tensor(out=S[:, hc], in0=S[:, hc], scalar=egl[:, h, cc:cc + 1],
                                                   in1=bank[:, hc], op0=ALU.mult, op1=ALU.add)\
                             .then_inc(vec_done, VE.step(tag + f"S{cc}" if h == 3 else None))
            v.wait_ge(act_done, AC.at(tag + "o3"))
            v_headnorm(v, tag + "d", o_tm[:, :, :], p2("ong"), zt, dq, 0)
            v.wait_ge(pe_done, PE.at(tag + "cmu"))
            for b in range(4):
                v.scalar_tensor_tensor(out=ca[:, b, :], in0=PS[2][:, 0:T], scalar=-1.0 / 512, in1=ca[:, b, :],
                                       op0=ALU.mult, op1=ALU.add).then_inc(vec_done, VE.step())
            v_wait(v)
            v.tensor_tensor(scr[:, 0, :], caf, caf, ALU.mult).then_inc(vec_done, VE.step(tag + "csq"))
            v.wait_ge(act_done, AC.at(tag + "crs"))
            v.reciprocal(scr[:, 1, T:2 * T], scr[:, 1, 0:T]).then_inc(vec_done, VE.step())
            v_wait(v)
            v.tensor_tensor(ca[:, :, :], ca[:, :, :], scr[:, 1, T:2 * T].unsqueeze(1).to_broadcast([P, 4, T]),
                            ALU.mult).then_inc(vec_done, VE.step(tag + "cn"))
            v_residual(v, SLOTS_MIX2, ALPHA, tag + "x1")
            v_wait(v)
            v_ln(v, tag + "m", p2("lnmg"), p2("lnmb"), tag + "n2.x")
            v_transposed(v, tag + "n2", None)
            if last:
                v.memset(Y[:, :, :], 0.0).then_inc(vec_done, VE.step())
                v.wait_ge(pe_done, PE.at(tag + "route"))
                lg = small[:, 0:16]
                v.tensor_copy(lg, PS[0][:, 0:16]).then_inc(vec_done, VE.step())
                v_wait(v)
                for t in range(NT):
                    v.max(top[:, t, :], lg[:, t * 8:(t + 1) * 8]).then_inc(vec_done, VE.step())
                v_wait(v)
                for t in range(NT):
                    v.max_index(topi[:, t, :], top[:, t, :], lg[:, t * 8:(t + 1) * 8]).then_inc(vec_done, VE.step())
                v.tensor_tensor(small[:, 40:42], top[:, :, 1], top[:, :, 0], ALU.subtract)\
                 .then_inc(vec_done, VE.step(tag + "d21"))
                v_wait(v)
                v.tensor_copy(topf[:, :, :], topi[:, :, :]).then_inc(vec_done, VE.step())
                v.wait_ge(act_done, AC.at(tag + "e21"))
                v.tensor_scalar(small[:, 42:44], small[:, 40:42], 1.0, None, ALU.add).then_inc(vec_done, VE.step())
                v_wait(v)
                v.reciprocal(small[:, 44:46], small[:, 42:44]).then_inc(vec_done, VE.step())
                v_wait(v)
                v.tensor_tensor(small[:, 46:48], small[:, 40:42], small[:, 44:46], ALU.mult)\
                 .then_inc(vec_done, VE.step())
                v_wait(v)
                for t in range(NT):
                    v.tensor_scalar(comb[:, t, :], c("iota")[:, 0:NEXP], topf[:, t, 0:1], small[:, 44 + t:45 + t],
                                    ALU.is_equal, ALU.mult).then_inc(vec_done, VE.step())
                    v.tensor_scalar(comb2[:, t, :], c("iota")[:, 0:NEXP], topf[:, t, 1:2], small[:, 46 + t:47 + t],
                                    ALU.is_equal, ALU.mult).then_inc(vec_done, VE.step())
                v_wait(v)
                for t in range(NT):
                    v.tensor_tensor(comb[:, t, :], comb[:, t, :], comb2[:, t, :], ALU.add)\
                     .then_inc(vec_done, VE.step())
                    v_wait(v)
                    v.tensor_scalar(member[:, t, :], c("iota")[:, 0:NEXP], topf[:, t, 0:1], None, ALU.is_equal)\
                     .then_inc(vec_done, VE.step())
                    v.tensor_scalar(comb2[:, t, :], c("iota")[:, 0:NEXP], topf[:, t, 1:2], None, ALU.is_equal)\
                     .then_inc(vec_done, VE.step())
                    v_wait(v)
                v.tensor_tensor(member[:, :, :], member[:, :, :], comb2[:, :, :], ALU.add)\
                 .then_inc(vec_done, VE.step(tag + "member"))
                v.wait_ge(pe_done, PE.at(tag + "places"))
                v_wait(v)
                v.tensor_tensor(place[:, :, 0:NEXP], PS[0][:, 0:16].rearrange("p (t e) -> p t e", t=NT),
                                member[:, :, :], ALU.mult).then_inc(vec_done, VE.step())
                v_wait(v)
                v.tensor_tensor(place[:, :, 0:NEXP], place[:, :, 0:NEXP], member[:, :, :], ALU.add)\
                 .then_inc(vec_done, VE.step())
                v_wait(v)
                v.tensor_scalar(place[:, :, 0:NEXP], place[:, :, 0:NEXP], -1.0, None, ALU.add)\
                 .then_inc(vec_done, VE.step())
                v.tensor_copy(wgt[:, :, 0:NEXP], comb[:, :, :]).then_inc(vec_done, VE.step())
                over, rank, hot, numf = small[:, 0:8], small[:, 8:16], small[:, 16:24], small[:, 60:60 + NPASS + 2]
                v.tensor_scalar(over, PS[0][:, 16:24], float(CAP), None, ALU.is_gt).then_inc(vec_done, VE.step())
                v.memset(small[:, 24:32], 1.0).then_inc(vec_done, VE.step())
                v.tensor_copy(numf[:, 0:NEXP], c("iota")[:, 0:NEXP]).then_inc(vec_done, VE.step())
                v.memset(numf[:, NPASS:NPASS + 1], 0.0).then_inc(vec_done, VE.step())
                v_wait(v)
                v.tensor_tensor_scan(rank, small[:, 24:32], over, 0.0, ALU.mult, ALU.add)\
                 .then_inc(vec_done, VE.step())
                v_wait(v)
                v.tensor_scalar(numf[:, NPASS + 1:NPASS + 2], rank[:, 7:8], float(NEXP), None, ALU.add)\
                 .then_inc(vec_done, VE.step())
                v.memset(place[:, :, NPASS:NPASS + 1], -1.0).then_inc(vec_done, VE.step())
                v.memset(wgt[:, :, NPASS:NPASS + 1], 0.0).then_inc(vec_done, VE.step())
                for q in range(NPASS - NEXP):
                    v.tensor_scalar(hot, rank, float(q + 1), None, ALU.is_equal).then_inc(vec_done, VE.step())
                    v_wait(v)
                    v.tensor_tensor(hot, hot, over, ALU.mult).then_inc(vec_done, VE.step())
                    v_wait(v)
                    v.tensor_tensor(small[:, 32:40], hot, numf[:, 0:NEXP], ALU.mult).then_inc(vec_done, VE.step())
                    v_wait(v)
                    v.tensor_reduce(numf[:, NEXP + q:NEXP + q + 1], small[:, 32:40], AX.X, ALU.add)\
                     .then_inc(vec_done, VE.step())
                    for src, dst in ((place, place), (wgt, wgt)):
                        v_wait(v)
                        v.tensor_tensor(comb2[:, :, :], src[:, :, 0:NEXP], hot.unsqueeze(1)
                                        .to_broadcast([P, NT, NEXP]), ALU.mult).then_inc(vec_done, VE.step())
                        v_wait(v)
                        v.tensor_reduce(dst[:, :, NEXP + q], comb2[:, :, :], AX.X, ALU.add)\
                         .then_inc(vec_done, VE.step())
                v_wait(v)
                v.tensor_scalar(place[:, :, NEXP:NPASS], place[:, :, NEXP:NPASS], -float(CAP), None, ALU.add)\
                 .then_inc(vec_done, VE.step())
                v.tensor_copy(table[0:1, :], numf[0:1, :]).then_inc(vec_done, VE.step())
                v.memset(og, 0.0).then_inc(vec_done, VE.step())
                v.memset(put[:, :, :], 0.0).then_inc(vec_done, VE.step())
                for t in range(NT):
                    v.tensor_scalar(pick[:, t, :], c("iota"), place[:, t, 0:1], None, ALU.is_equal)\
                     .then_inc(vec_done, VE.step())
                VE.names[tag + "pick"] = VE.n
                v_gather(v, tag)

        member = sb("member", [P, NT, NEXP])

        def t_gather(pe, tag):
            for k in range(KD):
                for t in range(NT):
                    mm = pe.matmul(PS[6 + k // 4][:, (k % 4) * CAP:(k % 4 + 1) * CAP], X[:, t, k * P:(k + 1) * P],
                                   pick[:, t, :], start=(t == 0), stop=(t == NT - 1))
                if k % 4 == 3:
                    mm.then_inc(pe_done, PE.step(tag + f".xg{k // 4}"))

        def v_gather(v, tag):
            v.wait_ge(pe_done, PE.at(tag + ".xg0"))
            v.tensor_copy(xg[:, 0:4, :], hh(PS[6][:, :])).then_inc(vec_done, VE.step(tag + ".xg"))

        def a_gather(act, tag):
            act.wait_ge(pe_done, PE.at(tag + ".xg1"))
            act.activation(xg[:, 4:8, :], hh(PS[7][:, :]), ACT.Copy).then_inc(act_done, AC.step(tag + ".xg"))

        def t_scatter(pe, tag, t):
            for f in range(2):
                mm = pe.matmul(PS[6 + f][:, :], put[:, t, :], og[:, f * 512:(f + 1) * 512], start=True, stop=True)
            mm.then_inc(pe_done, PE.step(tag + f".sc{t}"))

        def v_scatter(v, tag, t):
            v.wait_ge(pe_done, PE.at(tag + f".sc{t}"))
            for f in range(2):
                cols = slice(f * 512, (f + 1) * 512)
                v.tensor_tensor(Y[:, t, cols], Y[:, t, cols], PS[6 + f][:, :], ALU.add)\
                 .then_inc(vec_done, VE.step(tag + f".y{t}" if f else None))

        hidc = [big[:, 4864 + 256 * i:5120 + 256 * i] for i in range(2)]
        silc = [big[:, 5376 + 256 * i:5632 + 256 * i] for i in range(2)]

        def t_expert(pe, tag, units):
            def up(u):
                b = 2 * (u % 2)
                if u >= 2:
                    pe.wait_ge(vec_done, VE.at(tag + f".h{u - 2}"))
                for g in range(2):
                    w = rg.take(pe).rearrange("p (k n) -> p k n", n=UNIT)
                    for h in range(2):
                        for k in range(KD):
                            mm = pe.matmul(PS[b + g][:, h * CAP:(h + 1) * CAP], w[:, k, h * P:(h + 1) * P],
                                           xg[:, k, :], start=(k == 0), stop=(k == KD - 1))
                    mm.then_inc(slots_used, 1)

            def down(u):
                w = rg.take(pe).rearrange("p (k n) -> p k n", n=D)
                pe.wait_ge(vec_done, VE.at(tag + f".h{u}"))
                for k in range(2):
                    for f in range(2):
                        mm = pe.matmul(PS[4 + f][:, :], hidc[u % 2][:, k * CAP:(k + 1) * CAP],
                                       w[:, k, f * 512:(f + 1) * 512], start=(u == 0 and k == 0),
                                       stop=(u == units - 1 and k == 1))
                mm.then_inc(slots_used, 1)

            for u in range(units + 1):
                if u < units:
                    up(u)
                if u == units:
                    pe.wait_ge(vec_done, VE.at(tag + ".pick"))
                    pe.wait_ge(act_done, AC.at(tag + ".put"))
                    t_gather(pe, tag)
                if u > 0:
                    down(u - 1)
                if u == 2:
                    t_scatter(pe, tag, 0)
                if u == 4:
                    pe.wait_ge(vec_done, VE.at(tag + ".y0"))
                    t_scatter(pe, tag, 1)
                if u == 6:
                    pe.wait_ge(vec_done, VE.at(tag + ".y1"))
                    for t in range(NT):
                        mm = pe.transpose(PS[6][:, t * P:(t + 1) * P], pickw[:, t, :], ident)
                    mm.then_inc(pe_done, PE.step(tag + ".put"))

        def a_expert(act, tag, units):
            for u in range(units):
                up, _ = slot_index(u, units, True)
                act.wait_ge(slots_used, up)
                if u >= 2:
                    act.wait_ge(vec_done, VE.at(tag + f".h{u - 2}"))
                act.activation(silc[u % 2], PS[2 * (u % 2)][:, 0:2 * CAP], ACT.Silu)\
                   .then_inc(act_done, AC.step(tag + f".s{u}"))
                if u == 7:
                    act.wait_ge(pe_done, PE.at(tag + ".put"))
                    act.activation(put[:, :, :], PS[6][:, 0:NT * P].rearrange("p (t c) -> p t c", t=NT), ACT.Copy)\
                       .then_inc(act_done, AC.step(tag + ".put"))
            a_gather(act, tag)
            act.wait_ge(slots_used, SLOTS_EXP)
            act.activation(og[:, 512:1024], PS[5][:, :], ACT.Copy).then_inc(act_done, AC.step())

        def v_expert(v, tag, units, it):
            v.tensor_copy(ccol[:, 0:NT].unsqueeze(2), wgt[:, :, bass.ds(it, 1)]).then_inc(vec_done, VE.step())
            v.tensor_copy(ccol[:, NT:2 * NT].unsqueeze(2), place[:, :, bass.ds(it + 1, 1)])\
             .then_inc(vec_done, VE.step())
            v_wait(v)
            for t in range(NT):
                v.tensor_scalar(pickw[:, t, :], pick[:, t, :], ccol[:, t:t + 1], None, ALU.mult)\
                 .then_inc(vec_done, VE.step())
            v_wait(v)
            for t in range(NT):
                v.tensor_scalar(pick[:, t, :], c("iota"), ccol[:, NT + t:NT + t + 1], None, ALU.is_equal)\
                 .then_inc(vec_done, VE.step(tag + ".pick" if t else None))
            for u in range(units):
                v.wait_ge(act_done, AC.at(tag + f".s{u}"))
                if u >= 2:
                    v.wait_ge(slots_used, slot_index(u - 2, units, True)[1])
                v.tensor_tensor(hidc[u % 2], silc[u % 2], PS[2 * (u % 2) + 1][:, 0:2 * CAP], ALU.mult)\
                 .then_inc(vec_done, VE.step(tag + f".h{u}"))
                if u == 3:
                    v_scatter(v, tag, 0)
                if u == 5:
                    v_scatter(v, tag, 1)
            v_gather(v, tag)
            v.wait_ge(slots_used, SLOTS_EXP)
            v.tensor_copy(og[:, 0:512], PS[4][:, :]).then_inc(vec_done, VE.step())

        comb2 = sb("comb2", [P, NT, NEXP])
        top = sb("top", [P, NT, 8])
        topf = sb("topf", [P, NT, 8])
        topi = sb("topi", [P, NT, 8], U32)

        def second_tensor(pe):
            eng = ("pe", pe, PE, pe_done)
            for_segment(eng, "mixA", 1, lambda it: mix_tensor(pe, "A", 0, False))

            def dense(it):
                rg.start("dense", it)
                t_ffn3(pe, "fd", UNITS_DENSE, True)
            for_segment(eng, "dense", 1, dense)
            for_segment(eng, "mixB", 1, lambda it: mix_tensor(pe, "B", 1, True))

            def expert(it):
                rg.start("moe", it)
                t_expert(pe, "fe", UNITS_EXP)
            for_segment(eng, "moe", NEXP, expert)
            for t in range(NT):
                if t:
                    pe.wait_ge(vec_done, VE.at("fin.y0"))
                t_scatter(pe, "fin", t)

        def second_scalar(act):
            eng = ("act", act, AC, act_done)
            for_segment(eng, "mixA", 1, lambda it: mix_scalar(act, "A", 0, False))

            def dense(it):
                rga.start("dense", it)
                a_split(act, "fd", 0, rga)
                a_splitx(act, "fd")
                a_ffn3(act, "fd", UNITS_DENSE, True, rga, 1)
                a_ln(act, "fdn")
            for_segment(eng, "dense", 1, dense)
            for_segment(eng, "mixB", 1, lambda it: mix_scalar(act, "B", 1, True))

            def expert(it):
                a_expert(act, "fe", UNITS_EXP)
            for_segment(eng, "moe", NEXP, expert)
            a_ln(act, "fin")

        def second_vector(v):
            eng = ("vec", v, VE, vec_done)
            for_segment(eng, "mixA", 1, lambda it: mix_vector(v, "A", 0, False))

            def dense(it):
                rgv.start("dense", it)
                v_split(v, "fd", 0, rgv)
                v_splitx(v, "fd")
                v_ffn3(v, "fd", UNITS_DENSE, True, rgv, 1)
                v_residual(v, "fd.end", ALPHA, "xd")
                v_wait(v)
                v_ln(v, "fdn", p2("lnfg"), p2("lnfb"), "fdx")
            for_segment(eng, "dense", 1, dense)
            for_segment(eng, "mixB", 1, lambda it: mix_vector(v, "B", 1, True))

            def expert(it):
                v_expert(v, "fe", UNITS_EXP, it)
            for_segment(eng, "moe", NEXP, expert)
            for t in range(NT):
                v_scatter(v, "fin", t)
            v_wait(v)
            for t in range(NT):
                v.scalar_tensor_tensor(out=X[:, t, :], in0=X[:, t, :], scalar=ALPHA, in1=Y[:, t, :],
                                       op0=ALU.mult, op1=ALU.add).then_inc(vec_done, VE.step())
            v_wait(v)
            v_ln(v, "fin", p2("lnfg"), p2("lnfb"), "final")

        def v_gated(v, tag):
            v.wait_ge(act_done, AC.at(tag + "cg"))
            v_wait(v)
            v.tensor_tensor(cv[:, :, PAD:PAD + T], cv[:, :, PAD:PAD + T], cg[:, :, :], ALU.mult)\
             .then_inc(vec_done, VE.step(tag + "gated"))

        def v_taps(v, tag, first, last):
            dw = p2("dww")
            for w in range(first, last):
                for b in range(4):
                    tap = dw[:, b * CONV_WIN + w:b * CONV_WIN + w + 1]
                    if w == 0:
                        v.wait_ge(vec_done, VE.at(tag + "gated"))
                        v.tensor_scalar(ca[:, b, :], cv[:, b, w:w + T], tap, p2("dwb")[:, b:b + 1], ALU.mult,
                                        ALU.add).then_inc(vec_done, VE.step(tag + f"tap{w}.{b}"))
                    else:
                        v.wait_ge(vec_done, VE.at(tag + f"tap{w - 1}.{b}"))
                        v.scalar_tensor_tensor(out=ca[:, b, :], in0=cv[:, b, w:w + T], scalar=tap,
                                               in1=ca[:, b, :], op0=ALU.mult, op1=ALU.add)\
                         .then_inc(vec_done, VE.step(tag + f"tap{w}.{b}"))
            if last == CONV_WIN:
                VE.names[tag + "cc"] = VE.n

        @block.gpsimd
        def _(pool):
            def body(tag):
                def f(it):
                    pool.wait_ge(arrived, it * 4 + 4 * (seg_no[tag] + 1))
                    pool.sem_inc(pool_turns, 1)
                    for s in (pe_done, act_done, vec_done, slots_used, slots_split):
                        pool.sem_clear(s)
                    pool.sem_inc(cleared, 1)
                return f
            for tag, _, loops in segs[:-1]:
                for_segment(("pool", pool, None, None), tag, loops, body(tag))

        @block.tensor
        def _(pe):
            pe.wait_ge(con_loaded, 16)
            if RUN_FIRST:
                for_segment(("pe", pe, PE, pe_done), "l1", DEPTH, lambda it: l1_tensor(pe, it))
            if RUN_SECOND:
                second_tensor(pe)

        @block.scalar
        def _(act):
            act.wait_ge(consts_ready, 4)
            if RUN_FIRST:
                for_segment(("act", act, AC, act_done), "l1", DEPTH, lambda it: l1_scalar(act, it))
            if RUN_SECOND:
                second_scalar(act)

        @block.vector
        def _(v):
            v.memset(eps_rms[:, :], EPS).then_inc(consts_ready, 1)
            v.memset(eps_ln[:, :], LN_EPS).then_inc(consts_ready, 1)
            v.memset(reset[:, :], 1.0).then_inc(consts_ready, 1)
            v.wait_ge(consts_ready, 3)
            v.memset(reset[:, 0:4 * T:CHUNK], 0.0).then_inc(consts_ready, 1)
            v.wait_ge(consts_ready, 4)
            if RUN_FIRST:
                for_segment(("vec", v, VE, vec_done), "l1", DEPTH, lambda it: l1_vector(v, it))
            if RUN_SECOND:
                second_vector(v)


def _pack(cols, total, parts):
    import numpy as np
    out = np.zeros((128, total), np.float32)
    for name, a in parts.items():
        lo, hi = cols[name]
        assert a.shape[1] == hi - lo, (name, a.shape)
        out[:a.shape[0], lo:hi] = a
    return out


def _constants():
    import numpy as np
    i, j = np.arange(128)[:, None], np.arange(128)[None, :]
    keep = (i // CHUNK == j // CHUNK) & (j >= i)
    causal = np.where(j <= i, 0.0, NEG)
    sel = np.zeros((4, 4, 128), np.float32)
    selp = np.zeros((4, 2, 128), np.float32)
    for h in range(4):
        sel[h, h] = 1.0
        selp[h, h // 2, 64 * (h % 2):64 * (h % 2) + 64] = 1.0
    off = [((i // (2 * b) == j // (2 * b)) & (i % (2 * b) >= b) & (j % (2 * b) < b)) for b in (8, 16, 32)]
    inv = (1.0 / (np.float32(10000.0) ** (np.arange(0, HD, 2, dtype=np.float32) / np.float32(HD)))).astype(np.float32)
    ang = np.arange(T, dtype=np.float32)[:, None] * inv[None, :]
    tab = lambda a: a.reshape(NT, 128, 32).transpose(1, 0, 2).reshape(128, 64)
    return _pack(CON, NC, {
        "ident": np.eye(128), "ones": np.ones((128, 128)), "keep": keep, "neg": np.where(keep, 0.0, NEG),
        "moba": np.concatenate([causal, np.zeros((128, 128)), causal], 1),
        "m8": -1.0 * ((i // 8 == j // 8) & (j > i)), "off": np.concatenate(off, 1),
        "sel": sel.reshape(4, 512), "selp": selp.reshape(4, 256), "cos": tab(np.cos(ang)), "sin": tab(np.sin(ang)),
        "iota": np.broadcast_to(np.arange(128), (128, 128)), "before": i < j})


def kernel(**inputs):
    import numpy as np
    import concourse.bacc as bacc
    from concourse.bass_utils import run_bass_kernel_spmd

    a = {k: np.asarray(v) for k, v in inputs.items()}

    def by_feature(v):
        return v.reshape(-1, 128).T

    def taps(w):
        return w.T.reshape(-1, 128, w.shape[0]).transpose(1, 0, 2).reshape(128, -1)

    def ktile(w):
        return w.reshape(-1, 128, w.shape[1]).transpose(1, 0, 2).reshape(128, -1)

    slots = []

    def by_columns(w, n):
        for c in range(0, w.shape[1], n):
            slots.append(ktile(w[:, c:c + n]))

    def by_rows(w):
        for r in range(0, w.shape[0], 256):
            slots.append(ktile(w[r:r + 256]))

    par1, par2 = [], []
    if RUN_FIRST:
        for l in range(DEPTH):
            w = a["w_in"][l]
            at = np.cumsum([0, 512, 512, 512, 512, 16, 512, 512, 512, 256, 256, 512, 512, 4, 4, 3072])
            g_q, g_k, g_v, g_g, g_a, m_q, m_k, m_v, l_q, l_k, l_v, l_o, l_i, l_f, br = (
                w[:, at[i]:at[i + 1]] for i in range(15))
            for y in (g_q, g_k, g_g, g_v, m_q, m_k, m_v, l_q, l_k, l_v, l_o, br):
                by_columns(y, 256)
            for name in ("w_br_gla", "w_br_moba", "w_br_mlstm"):
                by_columns(a[name][l], 512)
            by_rows(a["w_out"][l])
            ff2 = a["w_ff2"][l]
            for u in range(0, 4096 // 256 + 1):
                if u < 16:
                    by_columns(a["w_ff1"][l][:, u * 256:(u + 1) * 256], 256)
                if u > 0:
                    by_rows(ff2[(u - 1) * 256:u * 256])
            par1.append(_pack(PAR1, NP1, {
                "n1": by_feature(a["norm1_g"][l]), "n2": by_feature(a["norm2_g"][l]),
                "ab": by_feature(a["gla_a_b"][l]), "gn": by_feature(a["gla_norm_g"][l]),
                "mn": by_feature(a["mlstm_norm_g"][l]), "gateb": by_feature(a["gate_b"][l]),
                "convw": taps(a["mlstm_conv_w"][l]), "wga": ktile(g_a), "wli": ktile(l_i), "wlf": ktile(l_f),
                "qng": np.broadcast_to(a["moba_qn_g"][l], (128, HD)),
                "kng": np.broadcast_to(a["moba_kn_g"][l], (128, HD)),
                "aup": a["gla_a_up"][l], "ifb": np.stack([a["mlstm_i_b"][l], a["mlstm_f_b"][l]], 1)}))
    else:
        par1 = [np.zeros((128, NP1), np.float32)] * DEPTH
    if RUN_SECOND:
        for l in range(DEPTH):
            w = a["w_in_2"][l]
            by_columns(w[:, :3072], 256)
            by_rows(a["w_out_2"][l])
            if l % 2 == 0:
                ffns = [(a["ffn_w_gate_2"][0], a["ffn_w_up_2"][0], a["ffn_w_down_2"][0])]
            else:
                ffns = [(a["moe_w_gate_2"][0][e], a["moe_w_up_2"][0][e], a["moe_w_down_2"][0][e])
                        for e in range(NEXP)]
            for gate, up, down in ffns:
                units = gate.shape[1] // 256
                for u in range(units + 1):
                    if u < units:
                        by_columns(gate[:, u * 256:(u + 1) * 256], 256)
                        by_columns(up[:, u * 256:(u + 1) * 256], 256)
                    if u > 0:
                        by_rows(down[(u - 1) * 256:u * 256])
            wide = lambda v: np.broadcast_to(v, (128, D))
            parts = {
                "wb": ktile(w[:, 3072:3076]), "wa": ktile(w[:, 3076:3080]), "sconv": taps(a["short_conv_w_2"][l]),
                "dww": taps(a["conv_dw_w_2"][l]), "dwb": by_feature(a["conv_dw_b_2"][l]),
                "clng": by_feature(a["conv_ln_g_2"][l]), "clnb": by_feature(a["conv_ln_b_2"][l]),
                "ong": by_feature(a["out_norm_g_2"][l]),
                "gpar": np.stack([a["a_log_2"][l], a["dt_bias_2"][l]], 1),
                "lnmg": wide(a["ln_mix_g_2"][l]), "lnmb": wide(a["ln_mix_b_2"][l]),
                "lnfg": wide(a["ln_ffn_g_2"][l]), "lnfb": wide(a["ln_ffn_b_2"][l])}
            if l % 2:
                parts["router"] = ktile(a["router_w_2"][0])
            par2.append(_pack(PAR2, NP2, parts))
    else:
        par2 = [np.zeros((128, NP2), np.float32)] * DEPTH
    slots += [np.zeros((128, SLOT), np.float32)] * NSLOT
    arrays = {"x": a["x"][0], "stream": np.stack(slots), "par1": np.stack(par1), "par2": np.stack(par2),
              "con": _constants()}

    def program(known):
        nc = bacc.Bacc("TRN2", target_bir_lowering=False, num_devices=1)
        ins = [nc.dram_tensor("in_" + name, v.shape, F32, kind="ExternalInput").ap() for name, v in arrays.items()]
        y = nc.dram_tensor("out_y", (T, D), F32, kind="ExternalOutput").ap()
        build(nc, *ins, y, known)
        return nc, known

    _, known = program({})
    nc, _ = program({k: s.names for k, s in zip(("pe", "act", "vec"), known["now"])})
    r = run_bass_kernel_spmd(nc, [{"in_" + k: np.ascontiguousarray(v) for k, v in arrays.items()}], core_ids=[0])
    return r.results[0]["out_y"][None]
```
